# Optimizing a Trainium2 kernel written in Bass

```python
import math
import jax, jax.numpy as jnp
from jax import lax
import numpy as np

D_MODEL = 2048
BATCH = 1
SEQ = 512
DEPTH = 2

EPS = 1e-6
GLA_HEADS = 4
GLA_DK = D_MODEL // 16
GLA_DV = D_MODEL // 8
GLA_LOWRANK = 16
GLA_TAU = 16.0
GLA_CHUNK = 64
FOX_HEADS = 8
FOX_DH = D_MODEL // 16
FOX_W = FOX_HEADS * FOX_DH
FOX_BLOCK = 128
S5_WIDTH = D_MODEL
S5_GROUP_CH = 16
S5_GROUPS = S5_WIDTH // S5_GROUP_CH
S5_STATE = 64
N_EVEN = (DEPTH + 1) // 2
N_ODD = DEPTH // 2
AB_SIZES = (GLA_HEADS * GLA_DK, GLA_HEADS * GLA_DK, GLA_HEADS * GLA_DV, GLA_LOWRANK, GLA_HEADS * GLA_DV,
            FOX_W, FOX_W, FOX_W, FOX_HEADS, FOX_W)
AB_IN = sum(AB_SIZES)
MIX_W = GLA_HEADS * GLA_DV + FOX_W


def rms_norm(x, g):
    xf = x.astype(jnp.float32)
    y = xf * lax.rsqrt(jnp.mean(xf * xf, axis=-1, keepdims=True) + EPS)
    return (y * g.astype(jnp.float32)).astype(x.dtype)

def gla_chunked(q, k, v, log_a):
    Bsz, H, L, dk = q.shape
    dv = v.shape[-1]
    n = L // GLA_CHUNK

    def to_chunks(t):
        t = t.astype(jnp.float32).reshape(Bsz, H, n, GLA_CHUNK, t.shape[-1])
        return jnp.moveaxis(t, 2, 0)

    qc, kc, vc, gc = (to_chunks(q * (dk ** -0.5)), to_chunks(k), to_chunks(v), to_chunks(log_a))
    mask = jnp.tril(jnp.ones((GLA_CHUNK, GLA_CHUNK), dtype=bool))[:, :, None]

    def step(S, inp):
        qi, ki, vi, gi = inp
        b = jnp.cumsum(gi, axis=-2)
        o_inter = jnp.einsum('bhck,bhkv->bhcv', qi * jnp.exp(b), S)
        rel = b[..., :, None, :] - b[..., None, :, :]
        decay = jnp.exp(jnp.where(mask, rel, -jnp.inf))
        attn = jnp.einsum('bhik,bhjk,bhijk->bhij', qi, ki, decay)
        o_intra = jnp.einsum('bhij,bhjv->bhiv', attn, vi)
        b_last = b[..., -1:, :]
        S = jnp.exp(b_last[..., 0, :])[..., None] * S + jnp.einsum(
            'bhck,bhcv->bhkv', ki * jnp.exp(b_last - b), vi)
        return S, o_inter + o_intra

    S0 = jnp.zeros((Bsz, H, dk, dv), jnp.float32)
    _, out = lax.scan(step, S0, (qc, kc, vc, gc))
    return jnp.moveaxis(out, 0, 2).reshape(Bsz, H, L, dv)

def forgetting_attention(q, k, v, log_f):
    L, d = q.shape[2], q.shape[3]
    scale = d ** -0.5
    c = jnp.cumsum(log_f, axis=-1)
    outs = []
    for blk in range(L // FOX_BLOCK):
        s0, s1 = blk * FOX_BLOCK, (blk + 1) * FOX_BLOCK
        qb, kb, vb = q[:, :, s0:s1], k[:, :, :s1], v[:, :, :s1]
        logits = (jnp.einsum('bhqd,bhkd->bhqk', qb, kb).astype(jnp.float32) * scale
                  + c[:, :, s0:s1, None] - c[:, :, None, :s1])
        causal = jnp.arange(s0, s1)[:, None] >= jnp.arange(s1)[None, :]
        p = jax.nn.softmax(jnp.where(causal, logits, -jnp.inf), axis=-1)
        outs.append(jnp.einsum('bhqk,bhkd->bhqd', p.astype(v.dtype), vb))
    return jnp.concatenate(outs, axis=2)

def _complex_combine(e1, e2):
    a1r, a1i, b1r, b1i = e1
    a2r, a2i, b2r, b2i = e2
    ar = a2r * a1r - a2i * a1i
    ai = a2r * a1i + a2i * a1r
    br = a2r * b1r - a2i * b1i + b2r
    bi = a2r * b1i + a2i * b1r + b2i
    return ar, ai, br, bi

def s5_ssm(u, lam_re, lam_im, log_step, b_re, b_im, c_re, c_im, d):
    Bsz, L, E = u.shape
    f32 = jnp.float32
    uf = u.astype(f32).reshape(Bsz, L, S5_GROUPS, S5_GROUP_CH)
    lr = jnp.minimum(lam_re.astype(f32), -1e-4)
    li = lam_im.astype(f32)
    step = jnp.exp(log_step.astype(f32))[:, None]
    mag = jnp.exp(lr * step)
    lb_re, lb_im = mag * jnp.cos(li * step), mag * jnp.sin(li * step)
    den = lr * lr + li * li
    nr, ni = lb_re - 1.0, lb_im
    coef_re = (nr * lr + ni * li) / den
    coef_im = (ni * lr - nr * li) / den
    br_, bi_ = b_re.astype(f32), b_im.astype(f32)
    bb_re = coef_re[..., None] * br_ - coef_im[..., None] * bi_
    bb_im = coef_re[..., None] * bi_ + coef_im[..., None] * br_
    bu_re = jnp.einsum('gpc,blgc->blgp', bb_re, uf)
    bu_im = jnp.einsum('gpc,blgc->blgp', bb_im, uf)
    a_re = jnp.broadcast_to(lb_re, (1, L, S5_GROUPS, S5_STATE))
    a_im = jnp.broadcast_to(lb_im, (1, L, S5_GROUPS, S5_STATE))
    _, _, x_re, x_im = lax.associative_scan(_complex_combine, (a_re, a_im, bu_re, bu_im), axis=1)
    y = (jnp.einsum('gcp,blgp->blgc', c_re.astype(f32), x_re)
         - jnp.einsum('gcp,blgp->blgc', c_im.astype(f32), x_im))
    return y.reshape(Bsz, L, E) + d.astype(f32) * uf.reshape(Bsz, L, E)

def layer_ab(x, norm_g, w_in, alpha_up, alpha_b, head_g, f_b, w_out):
    Bsz, L, _ = x.shape
    h = rms_norm(x, norm_g)
    split_idx = np.cumsum(AB_SIZES)[:-1].tolist()
    g_q, g_k, g_v, g_lr, g_gate, f_q, f_k, f_v, f_f, f_gate = jnp.split(h @ w_in, split_idx, axis=-1)

    def heads(t, nh):
        return t.reshape(Bsz, L, nh, -1).transpose(0, 2, 1, 3)

    log_a = jax.nn.log_sigmoid((g_lr @ alpha_up + alpha_b).astype(jnp.float32)) / GLA_TAU
    o = gla_chunked(heads(g_q, GLA_HEADS), heads(g_k, GLA_HEADS), heads(g_v, GLA_HEADS),
                    heads(log_a, GLA_HEADS))
    o = o * lax.rsqrt(jnp.mean(o * o, axis=-1, keepdims=True) + EPS)
    o = o * head_g.astype(jnp.float32).reshape(GLA_HEADS, 1, GLA_DV)
    o_gla = o.transpose(0, 2, 1, 3).reshape(Bsz, L, -1).astype(x.dtype) * jax.nn.silu(g_gate)

    log_f = jax.nn.log_sigmoid((f_f + f_b).astype(jnp.float32)).transpose(0, 2, 1)
    o_fox = forgetting_attention(heads(f_q, FOX_HEADS), heads(f_k, FOX_HEADS), heads(f_v, FOX_HEADS), log_f)
    o_fox = o_fox.transpose(0, 2, 1, 3).reshape(Bsz, L, -1) * jax.nn.silu(f_gate)

    return x + jnp.concatenate([o_gla, o_fox], axis=-1) @ w_out

def layer_c(x, norm_g, w_in, lam_re, lam_im, log_step, b_re, b_im, c_re, c_im, d, glu_w, glu_b, w_out):
    h = rms_norm(x, norm_g)
    u, gate = jnp.split(h @ w_in, 2, axis=-1)
    y = s5_ssm(u, lam_re, lam_im, log_step, b_re, b_im, c_re, c_im, d).astype(x.dtype)
    z = jax.nn.gelu(y)
    z = z * jax.nn.sigmoid(z @ glu_w + glu_b)
    return x + (z * jax.nn.silu(gate)) @ w_out

def first_inputs(seed: int = 0) -> dict:
    key = jax.random.key(seed)
    ks = jax.random.split(key, 24)
    nrm = jax.random.normal
    f32 = jnp.float32
    D, E, G, P, Cg = D_MODEL, S5_WIDTH, S5_GROUPS, S5_STATE, S5_GROUP_CH
    x = nrm(ks[0], (BATCH, SEQ, D), f32)
    ab_norm_g = 1.0 + 0.01 * nrm(ks[1], (N_EVEN, D), f32)
    ab_w_in = nrm(ks[2], (N_EVEN, D, AB_IN), f32) * D ** -0.5
    gla_alpha_up = nrm(ks[3], (N_EVEN, GLA_LOWRANK, GLA_HEADS * GLA_DK), f32) * GLA_LOWRANK ** -0.5
    gla_alpha_b = 0.01 * nrm(ks[4], (N_EVEN, GLA_HEADS * GLA_DK), f32)
    gla_head_g = 1.0 + 0.01 * nrm(ks[5], (N_EVEN, GLA_HEADS * GLA_DV), f32)
    fox_f_b = 1.0 + 0.1 * nrm(ks[6], (N_EVEN, FOX_HEADS), f32)
    ab_w_out = nrm(ks[7], (N_EVEN, MIX_W, D), f32) * MIX_W ** -0.5
    c_norm_g = 1.0 + 0.01 * nrm(ks[8], (N_ODD, D), f32)
    c_w_in = nrm(ks[9], (N_ODD, D, 2 * E), f32) * D ** -0.5
    n_idx = jnp.arange(P, dtype=f32)
    s5_lambda_re = -0.5 + 0.01 * nrm(ks[10], (N_ODD, G, P), f32)
    s5_lambda_im = math.pi * n_idx + 0.01 * nrm(ks[11], (N_ODD, G, P), f32)
    s5_log_step = jax.random.uniform(ks[12], (N_ODD, G), f32, math.log(1e-3), math.log(1e-1))
    s5_b_re = nrm(ks[13], (N_ODD, G, P, Cg), f32) * (2.0 * Cg) ** -0.5
    s5_b_im = nrm(ks[14], (N_ODD, G, P, Cg), f32) * (2.0 * Cg) ** -0.5
    s5_c_re = nrm(ks[15], (N_ODD, G, Cg, P), f32) * (2.0 * P) ** -0.5
    s5_c_im = nrm(ks[16], (N_ODD, G, Cg, P), f32) * (2.0 * P) ** -0.5
    s5_d = nrm(ks[17], (N_ODD, E), f32)
    glu_w = nrm(ks[18], (N_ODD, E, E), f32) * E ** -0.5
    glu_b = 0.01 * nrm(ks[19], (N_ODD, E), f32)
    c_w_out = nrm(ks[20], (N_ODD, E, D), f32) * E ** -0.5
    final_norm_g = 1.0 + 0.01 * nrm(ks[21], (D,), f32)
    return {"x": x, "ab_norm_g": ab_norm_g, "ab_w_in": ab_w_in, "gla_alpha_up": gla_alpha_up,
            "gla_alpha_b": gla_alpha_b, "gla_head_g": gla_head_g, "fox_f_b": fox_f_b,
            "ab_w_out": ab_w_out, "c_norm_g": c_norm_g, "c_w_in": c_w_in,
            "s5_lambda_re": s5_lambda_re, "s5_lambda_im": s5_lambda_im, "s5_log_step": s5_log_step,
            "s5_b_re": s5_b_re, "s5_b_im": s5_b_im, "s5_c_re": s5_c_re, "s5_c_im": s5_c_im,
            "s5_d": s5_d, "glu_w": glu_w, "glu_b": glu_b, "c_w_out": c_w_out,
            "final_norm_g": final_norm_g}

def first_block(x, ab_norm_g, ab_w_in, gla_alpha_up, gla_alpha_b, gla_head_g, fox_f_b, ab_w_out,
              c_norm_g, c_w_in, s5_lambda_re, s5_lambda_im, s5_log_step, s5_b_re, s5_b_im,
              s5_c_re, s5_c_im, s5_d, glu_w, glu_b, c_w_out, final_norm_g):
    for layer in range(DEPTH):
        i = layer // 2
        if layer % 2 == 0:
            x = layer_ab(x, ab_norm_g[i], ab_w_in[i], gla_alpha_up[i], gla_alpha_b[i],
                         gla_head_g[i], fox_f_b[i], ab_w_out[i])
        else:
            x = layer_c(x, c_norm_g[i], c_w_in[i], s5_lambda_re[i], s5_lambda_im[i], s5_log_step[i],
                        s5_b_re[i], s5_b_im[i], s5_c_re[i], s5_c_im[i], s5_d[i], glu_w[i], glu_b[i],
                        c_w_out[i])
    return rms_norm(x, final_norm_g)


NORM_EPS = 1e-6
BLOCK = 128

LRU_WIDTH = 1024
LRU_BLOCKS = 8
LRU_BLOCK_DIM = LRU_WIDTH // LRU_BLOCKS
CONV_WIDTH = 4
LRU_C = 8.0
SWA_Q_HEADS = 16
SWA_KV_HEADS = 2
SWA_HEAD_DIM = 64
SWA_GROUP = SWA_Q_HEADS // SWA_KV_HEADS
SWA_WIDTH = SWA_Q_HEADS * SWA_HEAD_DIM
SWA_KV_WIDTH = SWA_KV_HEADS * SWA_HEAD_DIM
WINDOW = 128
EVEN_SPLITS = [LRU_WIDTH, LRU_WIDTH, SWA_WIDTH, SWA_KV_WIDTH, SWA_KV_WIDTH, SWA_WIDTH]
EVEN_IN = sum(EVEN_SPLITS)
EVEN_MIX = LRU_WIDTH + SWA_WIDTH

MLA_HEADS = 8
MLA_Q_RANK = 768
MLA_KV_RANK = 512
MLA_NOPE = 128
MLA_ROPE = 64
MLA_V = 128
MLA_WIDTH = MLA_HEADS * MLA_V
ROPE_THETA = 10000.0
DIFF_HEADS = 8
DIFF_QK = 64
DIFF_V = 2 * DIFF_QK
DIFF_QK_WIDTH = DIFF_HEADS * 2 * DIFF_QK
DIFF_WIDTH = DIFF_HEADS * DIFF_V
DIFF_LAYER_IDX = 1
DIFF_LAMBDA_INIT = 0.8 - 0.6 * math.exp(-0.3 * DIFF_LAYER_IDX)
ODD_SPLITS = [MLA_Q_RANK, MLA_KV_RANK, MLA_ROPE, MLA_WIDTH,
              DIFF_QK_WIDTH, DIFF_QK_WIDTH, DIFF_WIDTH, DIFF_WIDTH]
ODD_IN = sum(ODD_SPLITS)
ODD_MIX = MLA_WIDTH + DIFF_WIDTH


def rmsnorm(x, g):
    xf = x.astype(jnp.float32)
    y = xf * lax.rsqrt(jnp.mean(xf * xf, axis=-1, keepdims=True) + NORM_EPS)
    return (y * g.astype(jnp.float32)).astype(x.dtype)

def split_cols(z, sizes):
    idx = [int(i) for i in np.cumsum(sizes)[:-1]]
    return jnp.split(z, idx, axis=-1)

def rope(x, pos):
    half = x.shape[-1] // 2
    freq = ROPE_THETA ** (-jnp.arange(half, dtype=jnp.float32) / half)
    ang = pos.astype(jnp.float32)[:, None] * freq[None, :]
    cos = jnp.cos(ang)[:, None, :]
    sin = jnp.sin(ang)[:, None, :]
    xf = x.astype(jnp.float32)
    x1, x2 = xf[..., :half], xf[..., half:]
    return jnp.concatenate([x1 * cos - x2 * sin, x1 * sin + x2 * cos], axis=-1).astype(x.dtype)

def causal_depthwise_conv(x, w, b):
    y = lax.conv_general_dilated(
        x, w[:, None, :].astype(x.dtype), window_strides=(1,),
        padding=[(CONV_WIDTH - 1, 0)], dimension_numbers=("NWC", "WIO", "NWC"),
        feature_group_count=x.shape[-1])
    return y + b

def rg_lru(x, gx_w, gx_b, ga_w, ga_b, lru_lambda):
    B, S, _ = x.shape
    xb = x.reshape(B, S, LRU_BLOCKS, LRU_BLOCK_DIM)
    gate_i = jax.nn.sigmoid(jnp.einsum("bsnd,nde->bsne", xb, gx_w) + gx_b).reshape(B, S, LRU_WIDTH)
    gate_r = jax.nn.sigmoid(jnp.einsum("bsnd,nde->bsne", xb, ga_w) + ga_b).reshape(B, S, LRU_WIDTH)
    log_a = -LRU_C * jax.nn.softplus(-lru_lambda.astype(jnp.float32)) * gate_r.astype(jnp.float32)
    a = jnp.exp(log_a)
    mult = jnp.sqrt(-jnp.expm1(2.0 * log_a))
    u = mult * gate_i.astype(jnp.float32) * x.astype(jnp.float32)

    def combine(c1, c2):
        a1, b1 = c1
        a2, b2 = c2
        return a1 * a2, a2 * b1 + b2

    _, h = lax.associative_scan(combine, (a, u), axis=1)
    return h.astype(x.dtype)

def sliding_window_gqa_sinks(q, k, v, sinks):
    B, S = q.shape[:2]
    nb = S // BLOCK
    qb = q.reshape(B, nb, BLOCK, SWA_KV_HEADS, SWA_GROUP, SWA_HEAD_DIM)

    def band(t):
        tp = jnp.pad(t, ((0, 0), (BLOCK, 0), (0, 0), (0, 0)))
        cur = tp[:, BLOCK:].reshape(B, nb, BLOCK, SWA_KV_HEADS, SWA_HEAD_DIM)
        prev = tp[:, :S].reshape(B, nb, BLOCK, SWA_KV_HEADS, SWA_HEAD_DIM)
        return jnp.concatenate([prev, cur], axis=2)

    kb, vb = band(k), band(v)
    s = jnp.einsum("bnqhgd,bnkhd->bnhgqk", qb, kb).astype(jnp.float32) * (SWA_HEAD_DIM ** -0.5)
    n = jnp.arange(nb)[:, None, None]
    qi = jnp.arange(BLOCK)[None, :, None]
    ki = jnp.arange(2 * BLOCK)[None, None, :]
    rel = qi + BLOCK - ki
    kpos = n * BLOCK - BLOCK + ki
    mask = (rel >= 0) & (rel < WINDOW) & (kpos >= 0)
    s = jnp.where(mask[None, :, None, None], s, -jnp.inf)
    sink = sinks.astype(jnp.float32).reshape(1, 1, SWA_KV_HEADS, SWA_GROUP, 1, 1)
    m = jnp.maximum(jnp.max(s, axis=-1, keepdims=True), sink)
    p = jnp.exp(s - m)
    p = p / (jnp.sum(p, axis=-1, keepdims=True) + jnp.exp(sink - m))
    o = jnp.einsum("bnhgqk,bnkhd->bnqhgd", p.astype(vb.dtype), vb)
    return o.reshape(B, S, SWA_WIDTH)

def sweep_query_blocks(block_fn, q):
    B, S = q.shape[:2]
    nb = S // BLOCK
    qb = jnp.moveaxis(q.reshape((B, nb, BLOCK) + q.shape[2:]), 1, 0)

    def body(args):
        qblk, n = args
        return block_fn(qblk, n * BLOCK + jnp.arange(BLOCK))

    o = lax.map(body, (qb, jnp.arange(nb)))
    o = jnp.moveaxis(o, 0, 1)
    return o.reshape((B, S) + o.shape[3:])

def causal_mla_attention(q, k, v):
    S = k.shape[1]
    kpos = jnp.arange(S)
    scale = (MLA_NOPE + MLA_ROPE) ** -0.5

    def block_fn(qblk, qpos):
        s = jnp.einsum("bqhd,bkhd->bhqk", qblk, k).astype(jnp.float32) * scale
        s = jnp.where(kpos[None, :] <= qpos[:, None], s, -jnp.inf)
        p = jax.nn.softmax(s, axis=-1)
        return jnp.einsum("bhqk,bkhd->bqhd", p.astype(v.dtype), v)

    return sweep_query_blocks(block_fn, q)

def causal_diff_attention(q, k, v, lam):
    S = k.shape[1]
    kpos = jnp.arange(S)
    scale = DIFF_QK ** -0.5

    def block_fn(qblk, qpos):
        s = jnp.einsum("bqhcd,bkhcd->bchqk", qblk, k).astype(jnp.float32) * scale
        s = jnp.where(kpos[None, :] <= qpos[:, None], s, -jnp.inf)
        p = jax.nn.softmax(s, axis=-1)
        a = p[:, 0] - lam * p[:, 1]
        return jnp.einsum("bhqk,bkhd->bqhd", a.astype(v.dtype), v)

    return sweep_query_blocks(block_fn, q)

def even_layer(h, w_in, conv_w, conv_b, gx_w, gx_b, ga_w, ga_b, lru_lambda, sinks, w_out):
    B, S, _ = h.shape
    z = h @ w_in
    lru_x, lru_gate, q, k, v, swa_gate = split_cols(z, EVEN_SPLITS)
    lru_x = causal_depthwise_conv(lru_x, conv_w, conv_b)
    y_a = rg_lru(lru_x, gx_w, gx_b, ga_w, ga_b, lru_lambda) * jax.nn.silu(lru_gate)
    q = q.reshape(B, S, SWA_Q_HEADS, SWA_HEAD_DIM)
    k = k.reshape(B, S, SWA_KV_HEADS, SWA_HEAD_DIM)
    v = v.reshape(B, S, SWA_KV_HEADS, SWA_HEAD_DIM)
    y_b = sliding_window_gqa_sinks(q, k, v, sinks) * jax.nn.silu(swa_gate)
    return jnp.concatenate([y_a, y_b], axis=-1) @ w_out

def odd_layer(h, w_in, q_norm, w_uq, kv_norm, w_ukv, lambda_q1, lambda_k1, lambda_q2, lambda_k2,
              subln, w_out):
    B, S, _ = h.shape
    pos = jnp.arange(S)
    z = h @ w_in
    c_q, c_kv, k_rope, mla_gate, dq, dk, dv, diff_gate = split_cols(z, ODD_SPLITS)
    q = (rmsnorm(c_q, q_norm) @ w_uq).reshape(B, S, MLA_HEADS, MLA_NOPE + MLA_ROPE)
    q = jnp.concatenate([q[..., :MLA_NOPE], rope(q[..., MLA_NOPE:], pos)], axis=-1)
    kv = (rmsnorm(c_kv, kv_norm) @ w_ukv).reshape(B, S, MLA_HEADS, MLA_NOPE + MLA_V)
    k_nope, v_c = kv[..., :MLA_NOPE], kv[..., MLA_NOPE:]
    k_r = rope(k_rope.reshape(B, S, 1, MLA_ROPE), pos)
    k_c = jnp.concatenate([k_nope, jnp.broadcast_to(k_r, (B, S, MLA_HEADS, MLA_ROPE))], axis=-1)
    y_c = causal_mla_attention(q, k_c, v_c).reshape(B, S, MLA_WIDTH) * jax.nn.silu(mla_gate)
    qd = dq.reshape(B, S, DIFF_HEADS, 2, DIFF_QK)
    kd = dk.reshape(B, S, DIFF_HEADS, 2, DIFF_QK)
    vd = dv.reshape(B, S, DIFF_HEADS, DIFF_V)
    lam = (jnp.exp(jnp.sum(lambda_q1.astype(jnp.float32) * lambda_k1.astype(jnp.float32)))
           - jnp.exp(jnp.sum(lambda_q2.astype(jnp.float32) * lambda_k2.astype(jnp.float32)))
           + DIFF_LAMBDA_INIT)
    od = causal_diff_attention(qd, kd, vd, lam)
    od = rmsnorm(od, subln) * (1.0 - DIFF_LAMBDA_INIT)
    y_d = od.reshape(B, S, DIFF_WIDTH) * jax.nn.silu(diff_gate)
    return jnp.concatenate([y_c, y_d], axis=-1) @ w_out

def second_inputs(seed: int = 0) -> dict:
    key = jax.random.key(seed)
    ks = jax.random.split(key, 32)
    f32 = jnp.float32

    def dense(k, shape, fan_in):
        return jax.random.normal(k, shape, f32) * (fan_in ** -0.5)

    def gain(k, shape):
        return 1.0 + 0.05 * jax.random.normal(k, shape, f32)

    def small(k, shape, s=0.02):
        return s * jax.random.normal(k, shape, f32)

    u = jax.random.uniform(ks[10], (LRU_WIDTH,), f32, minval=0.9, maxval=0.999)
    a_base = u ** (1.0 / LRU_C)
    lru_lambda = jnp.log(a_base) - jnp.log1p(-a_base)

    return {
        "x": jax.random.normal(ks[0], (BATCH, SEQ, D_MODEL), f32),
        "norm_gains": gain(ks[1], (DEPTH, D_MODEL)),
        "final_norm_gain": gain(ks[2], (D_MODEL,)),
        "l0_w_in": dense(ks[3], (D_MODEL, EVEN_IN), D_MODEL),
        "l0_conv_w": dense(ks[4], (CONV_WIDTH, LRU_WIDTH), CONV_WIDTH),
        "l0_conv_b": small(ks[5], (LRU_WIDTH,)),
        "l0_gate_x_w": dense(ks[6], (LRU_BLOCKS, LRU_BLOCK_DIM, LRU_BLOCK_DIM), LRU_BLOCK_DIM),
        "l0_gate_x_b": small(ks[7], (LRU_BLOCKS, LRU_BLOCK_DIM)),
        "l0_gate_a_w": dense(ks[8], (LRU_BLOCKS, LRU_BLOCK_DIM, LRU_BLOCK_DIM), LRU_BLOCK_DIM),
        "l0_gate_a_b": small(ks[9], (LRU_BLOCKS, LRU_BLOCK_DIM)),
        "l0_lru_lambda": lru_lambda,
        "l0_sinks": 0.5 * jax.random.normal(ks[11], (SWA_Q_HEADS,), f32),
        "l0_w_out": dense(ks[12], (EVEN_MIX, D_MODEL), EVEN_MIX),
        "l1_w_in": dense(ks[13], (D_MODEL, ODD_IN), D_MODEL),
        "l1_q_norm": gain(ks[14], (MLA_Q_RANK,)),
        "l1_w_uq": dense(ks[15], (MLA_Q_RANK, MLA_HEADS * (MLA_NOPE + MLA_ROPE)), MLA_Q_RANK),
        "l1_kv_norm": gain(ks[16], (MLA_KV_RANK,)),
        "l1_w_ukv": dense(ks[17], (MLA_KV_RANK, MLA_HEADS * (MLA_NOPE + MLA_V)), MLA_KV_RANK),
        "l1_lambda_q1": small(ks[18], (DIFF_QK,), 0.1),
        "l1_lambda_k1": small(ks[19], (DIFF_QK,), 0.1),
        "l1_lambda_q2": small(ks[20], (DIFF_QK,), 0.1),
        "l1_lambda_k2": small(ks[21], (DIFF_QK,), 0.1),
        "l1_subln": gain(ks[22], (DIFF_V,)),
        "l1_w_out": dense(ks[23], (ODD_MIX, D_MODEL), ODD_MIX),
    }

def second_block(x, norm_gains, final_norm_gain,
              l0_w_in, l0_conv_w, l0_conv_b, l0_gate_x_w, l0_gate_x_b, l0_gate_a_w, l0_gate_a_b,
              l0_lru_lambda, l0_sinks, l0_w_out,
              l1_w_in, l1_q_norm, l1_w_uq, l1_kv_norm, l1_w_ukv,
              l1_lambda_q1, l1_lambda_k1, l1_lambda_q2, l1_lambda_k2, l1_subln, l1_w_out):
    even_params = (l0_w_in, l0_conv_w, l0_conv_b, l0_gate_x_w, l0_gate_x_b, l0_gate_a_w,
                   l0_gate_a_b, l0_lru_lambda, l0_sinks, l0_w_out)
    odd_params = (l1_w_in, l1_q_norm, l1_w_uq, l1_kv_norm, l1_w_ukv, l1_lambda_q1, l1_lambda_k1,
                  l1_lambda_q2, l1_lambda_k2, l1_subln, l1_w_out)
    for layer in range(DEPTH):
        h = rmsnorm(x, norm_gains[layer])
        if layer % 2 == 0:
            x = x + even_layer(h, *even_params)
        else:
            x = x + odd_layer(h, *odd_params)
    return rmsnorm(x, final_norm_gain)


def setup_inputs(seed=0):
    out = dict(first_inputs(seed))
    for name, value in second_inputs(seed + 1).items():
        if name != "x":
            out[name + "_2"] = value
    return out


def reference(
    x, ab_norm_g, ab_w_in, gla_alpha_up, gla_alpha_b, gla_head_g, fox_f_b, ab_w_out, c_norm_g,
    c_w_in, s5_lambda_re, s5_lambda_im, s5_log_step, s5_b_re, s5_b_im, s5_c_re, s5_c_im, s5_d,
    glu_w, glu_b, c_w_out, final_norm_g, norm_gains_2, final_norm_gain_2, l0_w_in_2,
    l0_conv_w_2, l0_conv_b_2, l0_gate_x_w_2, l0_gate_x_b_2, l0_gate_a_w_2, l0_gate_a_b_2,
    l0_lru_lambda_2, l0_sinks_2, l0_w_out_2, l1_w_in_2, l1_q_norm_2, l1_w_uq_2, l1_kv_norm_2,
    l1_w_ukv_2, l1_lambda_q1_2, l1_lambda_k1_2, l1_lambda_q2_2, l1_lambda_k2_2, l1_subln_2,
    l1_w_out_2,
):
    x = first_block(
        x, ab_norm_g, ab_w_in, gla_alpha_up, gla_alpha_b, gla_head_g, fox_f_b, ab_w_out,
        c_norm_g, c_w_in, s5_lambda_re, s5_lambda_im, s5_log_step, s5_b_re, s5_b_im, s5_c_re,
        s5_c_im, s5_d, glu_w, glu_b, c_w_out, final_norm_g,
    )
    return second_block(
        x, norm_gains_2, final_norm_gain_2, l0_w_in_2, l0_conv_w_2, l0_conv_b_2, l0_gate_x_w_2,
        l0_gate_x_b_2, l0_gate_a_w_2, l0_gate_a_b_2, l0_lru_lambda_2, l0_sinks_2, l0_w_out_2,
        l1_w_in_2, l1_q_norm_2, l1_w_uq_2, l1_kv_norm_2, l1_w_ukv_2, l1_lambda_q1_2,
        l1_lambda_k1_2, l1_lambda_q2_2, l1_lambda_k2_2, l1_subln_2, l1_w_out_2,
    )


_drawn_inputs = setup_inputs


def setup_inputs(seed=0):
    import zlib

    import numpy as np

    out = dict(_drawn_inputs(seed))
    spreads = {}
    factors = {'ab_norm_g': 5.398,
     'gla_alpha_b': 8.0,
     'gla_head_g': 8.0,
     'fox_f_b': 4.986,
     'c_norm_g': 8.0,
     's5_lambda_re': 64.0,
     's5_lambda_im': 35.216,
     's5_log_step': 36.8,
     's5_b_re': 49.52,
     's5_b_im': 49.832,
     's5_c_re': 49.848,
     's5_c_im': 49.424,
     'glu_b': 8.0,
     'final_norm_g': 4.814,
     'l0_gate_x_b_2': 24.819,
     'l0_gate_a_b_2': 38.659,
     'l0_sinks_2': 8.0,
     'l1_q_norm_2': 8.0,
     'l1_kv_norm_2': 8.0,
     'l1_lambda_q1_2': 8.0,
     'l1_lambda_q2_2': 3.821,
     'l1_subln_2': 29.61}
    for name, (base, spread) in spreads.items():
        noise = np.random.default_rng([zlib.crc32(name.encode()), seed]).standard_normal(out[name].shape)
        drawn = base * np.exp(spread * noise) if base else spread * noise
        out[name] = __import__('jax').numpy.asarray(drawn.astype(out[name].dtype))
    for name, factor in factors.items():
        out[name] = (out[name] * factor).astype(out[name].dtype)
    return out
```

```python
from contextlib import ExitStack

import concourse.bass as bass
from concourse import mybir

F32 = mybir.dt.float32
F32R = mybir.dt.float32r
I32 = mybir.dt.int32
ALU = mybir.AluOpType
ACT = mybir.ActivationFunctionType
AX = mybir.AxisListType

P = 128
L = 512
NTOK = L // P
D = 2048
KT = D // P
BLK = 512
MT = BLK // P
PK = 2
RING = 4
AHEAD = 3
EPS = 1e-6
NEG = -1e30
STOP, NPHASES = 99, 99
LOWEST = -3e38

GH, GDK, GDV, GRANK, GTAU = 4, 128, 256, 16, 16.0
FH, FD = 8, 128
SG, SC, SP_, ST = 128, 16, 64, 8
SK = L // ST
SPAIR = 8
SSL = SG // (2 * SPAIR)
RB, CW, LRU_C = 8, 4, 8.0
WH, WD, WKV = 16, 64, 2
MH, MNOPE, MROPE, MQR, MKVR = 8, 128, 64, 768, 512
DH, DQK = 8, 64
LAMBDA_INIT = 0.8 - 0.6 * 2.718281828459045 ** -0.3

AB = dict(q=0, k=512, v=1024, lr=2048, gate=2064, fq=3088, fk=4112, fv=5136, ff=6160, fgate=6168)
L0 = dict(x=0, gate=1024, q=2048, k=3072, v=3200, sgate=3328)
L1 = dict(cq=0, ckv=768, kr=1280, gate=1344, dq=2368, dk=3392, dv=4416, dgate=5440)

ZT = dict(lr=0, ff=128, q=256, k=768, gate=1280, fq=2304, fk=3328, fgate=4352,
          sgate=5376, z=7424,
          rx=9472, rgate=10496, wq=11520, wkv=12544, wgate=12800,
          kr=13824, mgate=13952, dq=14976, dk=16000, dgate=17024, qn=18048, qr=19072, kn=19584)
ZT_ROWS = 20608
ZN = dict(v=0, fv=1024, u=2048, wv=4096, dv=4224, mv=5248)
ZN_COLS = 6272


class Region:

    def __init__(self, w, kts, c0, blocks, width, form, evac, dst=None, d0=0, arg=None):
        self.w, self.kts, self.c0, self.blocks, self.width = w, kts, c0, blocks, width
        self.form, self.evac, self.dst, self.d0, self.arg = form, evac, dst, d0, arg
        self.pieces = kts // PK
        self.dmas = 1
        self.banks = -(-width // P) if form == "T" else MT

    def rows(self, m):
        return min(P, self.width - m * P) if self.form == "T" else P

    def cols(self):
        return L if self.form == "T" else self.width


class Attention:

    def __init__(self, *, buf, tiles, heads, comps, dv, scale, key_tiles, products, bias, bias_ready, pool_work, value,
                 gate, gate_of, kt0, loads, hi, lo, units0, jobs0, tiles0, in0, sink=None, lam=None, gain=None):
        self.buf, self.tiles, self.heads, self.comps, self.dv, self.scale = buf, tiles, heads, comps, dv, scale
        self.key_tiles, self.products, self.bias, self.bias_ready = key_tiles, products, bias, bias_ready
        self.pool_work, self.value, self.gate, self.gate_of, self.kt0 = pool_work, value, gate, gate_of, kt0
        self.loads, self.hi, self.lo, self.sink, self.lam, self.gain = loads, hi, lo, sink, lam, gain
        self.units0, self.jobs0, self.tiles0, self.in0 = units0, jobs0, tiles0, in0
        self.per = heads * NTOK
        self.jobs = tiles * self.per
        self.units = self.jobs * comps


def count_regions(regions):
    piece, bank, stage = 0, [0] * MT, [0] * MT
    for r in regions:
        r.piece0, r.bank0, r.stage0 = piece, list(bank), list(stage)
        piece += r.blocks * r.pieces
        for m in range(r.banks):
            bank[m] += r.blocks
            if r.dst is not None:
                stage[m] += r.blocks
    return piece

VECTORS = dict(
    ab_norm_g=("ab_norm_g", 0, D), c_norm_g=("c_norm_g", 0, D), final_norm_g=("final_norm_g", None, D),
    norm_a=("norm_gains_2", 0, D), norm_b=("norm_gains_2", 1, D), last_g=("final_norm_gain_2", None, D),
    alpha_b=("gla_alpha_b", 0, GH * GDK), head_g=("gla_head_g", 0, GH * GDV), glu_b=("glu_b", 0, D),
    kv_norm=("l1_kv_norm_2", None, MKVR),
    conv_b=("l0_conv_b_2", None, RB * P), lam=("l0_lru_lambda_2", None, RB * P),
    q_norm=("l1_q_norm_2", None, MQR), subln=("l1_subln_2", None, P),
    gx_b=("l0_gate_x_b_2", None, RB * P), ga_b=("l0_gate_a_b_2", None, RB * P),
    conv_w=("l0_conv_w_2", None, CW * RB * P), f_b=("fox_f_b", None, FH))
COL, NROWS = {}, 0
for _name, (_, _, _n) in VECTORS.items():
    COL[_name] = NROWS
    assert NROWS // P == (NROWS + -(-_n // P) - 1) // P
    NROWS += -(-_n // P)
COL["sinks"] = NROWS
NCOLS = NROWS + WH


def build(nc, inp, out):
    ctx = ExitStack()

    def sem(name):
        return ctx.enter_context(nc.semaphore(name))

    def dram(name, shape):
        return nc.dram_tensor(name, shape, F32, kind="Internal").ap()

    def sb(name, shape, dtype=F32):
        return ctx.enter_context(nc.sbuf_tensor(name, [P] + shape, dtype))

    def overlay(base, tensors):
        made = {}
        with ExitStack() as scope:
            if base:
                scope.enter_context(nc.sbuf_tensor(f"gap_{base}_{tensors[0][0]}", [P, base // 4], F32))
            for name, shape, dtype in tensors:
                made[name] = scope.enter_context(nc.sbuf_tensor(name, [P] + shape, dtype))
        return made

    zt = dram("zt", (ZT_ROWS, L))
    zn = dram("zn", (L, ZN_COLS))
    xds = [dram(f"xd{n}", (D, L)) for n in range(4)]
    negc_dram = dram("negc_dram", (FH, L))

    raw = sb("raw", [RING, PK * BLK])
    whi = sb("whi", [RING, PK * BLK], F32R)
    wlo = sb("wlo", [RING, PK * BLK], F32R)
    stage = sb("stage", [MT, L])
    ident = sb("ident", [P])
    ones = sb("ones", [P])
    cols = sb("cols", [NCOLS])
    acc = sb("acc", [L])
    rstd = sb("rstd", [L])
    wide = sb("wide", [L])
    band = sb("band", [2 * P])

    eps, onecol, halfpi = sb("eps", [1]), sb("onecol", [1]), sb("halfpi", [1])
    rows = sb("rows", [2, P])
    made, cols_turned, cols_ready = sem("constants_made"), sem("vectors_turned"), sem("vectors_ready")

    HALF = 2 * KT * L * 4
    EXTRA = 2 * HALF
    G = overlay(EXTRA, [("glu_z", [2, L], F32), ("glu_g", [2, L], F32)])
    A = overlay(0, [("a_hi", [KT, L], F32R), ("a_lo", [KT, L], F32R)])
    B = overlay(HALF, [("b_hi", [KT, L], F32R), ("b_lo", [KT, L], F32R)])
    XA = overlay(0, [("xa", [KT, L], F32), ("xa_in", [MT, L], F32), ("xa_sq", [2, L], F32), ("xa_n", [2, L], F32)])
    XB = overlay(HALF, [("xb", [KT, L], F32), ("xb_in", [MT, L], F32), ("xb_sq", [2, L], F32), ("xb_n", [2, L], F32),
                        ("xb_tok", [2, D], F32)])
    AB_HI_LO = {"A": (A["a_hi"], A["a_lo"]), "B": (B["b_hi"], B["b_lo"])}
    X_OF = {"A": (XA["xa"], XA["xa_in"], XA["xa_sq"], XA["xa_n"]),
            "B": (XB["xb"], XB["xb_in"], XB["xb_sq"], XB["xb_n"])}

    pg = [ctx.enter_context(nc.psum_tensor(f"pg{m}", [P, L], F32)) for m in range(MT)]
    pm = [ctx.enter_context(nc.psum_tensor(f"pm{m}", [P, L], F32)) for m in range(4)]

    bar = sem("phase_ended")
    consts_in = sem("consts_in")
    raw_in = [sem(f"raw_in{s}") for s in range(RING)]
    hi_ready, lo_ready, w_used = sem("w_hi_ready"), sem("w_lo_ready"), sem("w_used")
    bank_ready = [sem(f"bank_ready{m}") for m in range(MT)]
    evacd = [sem(f"bank_evacuated{m}") for m in range(MT)]
    stored = [sem(f"stored{m}") for m in range(MT)]
    xin_in = [sem(f"old_x_in{m}") for m in range(MT)]
    sq_ready, acc_done = sem("squares_ready"), sem("squares_added")
    x_stored = sem("x_stored")
    rs_ready, sd_ready, rstd_ready = sem("square_sum_ready"), sem("deviation_ready"), sem("rstd_ready")
    xn_ready, nh_ready, h_ready = sem("normed_ready"), sem("normed_hi_ready"), sem("normed_lo_ready")
    act_seq, dve_seq = sem("act_seq"), sem("dve_seq")
    glu_in = [sem(f"glu_operands_in{n}") for n in range(2)]
    glu_mid, glu_done, glu_hi, glu_lo = sem("glu_gates"), sem("glu_products"), sem("glu_hi"), sem("glu_lo")
    counts = {}

    def col(name, n=0):
        return cols[:, COL[name] + n:COL[name] + n + 1]

    def serial(eng, s):
        def run(ins):
            counts[s.name] = counts.get(s.name, 0) + 1
            ins.then_inc(s, 1)
            eng.wait_ge(s, counts[s.name])
        return run

    barriers = {}

    def barrier(eng, who):
        barriers[who] = barriers.get(who, 0) + 1
        eng.drain().then_inc(bar, 1)
        eng.wait_ge(bar, 4 * barriers[who])

    def window(w):
        return lambda i, q, c0: w[q * PK * P:(q + 1) * PK * P, bass.ds(c0 + i * BLK, BLK)].rearrange(
            "(k p) n -> p k n", p=P)

    def to_zt(name, row=0):
        return lambda i, m, r: zt[bass.ds(ZT[name] + row + i * BLK + m * P, r.rows(m)), :]

    def to_zn(name):
        return lambda i, m, r: zn[m * P:(m + 1) * P, bass.ds(ZN[name] + i * BLK, r.width)]

    def T(w, c0, n, evac, dst):
        made = []
        if n // BLK:
            made.append(Region(window(w), KT, c0, n // BLK, BLK, "T", evac, to_zt(dst)))
        if n % BLK:
            lo = n // BLK * BLK
            made.append(Region(window(w), KT, c0 + lo, 1, n % BLK, "T", evac, to_zt(dst, lo)))
        return made

    def N(w, c0, n, dst):
        return [Region(window(w), KT, c0, max(n // BLK, 1), min(n, BLK), "N", "copy", to_zn(dst))]

    def resid(w):
        return [Region(window(w), KT, 0, D // BLK, BLK, "T", "resid")]

    def as3(name):
        return inp[name][0]

    wab, wc = as3("ab_w_in"), as3("c_w_in")
    w0, w1 = inp["l0_w_in_2"], inp["l1_w_in_2"]
    uq = inp["l1_w_uq_2"].rearrange("(k p) (h c) -> p k h c", p=P, h=MH)
    ukv = inp["l1_w_ukv_2"].rearrange("(k p) (h c) -> p k h c", p=P, h=MH)

    def heads_of(w, n, c0, width):
        return lambda i, q, _: w[:, q * PK:(q + 1) * PK, i * n:(i + 1) * n, c0:c0 + width]

    PHASES = [
        ("A", T(wab, AB["lr"], GRANK, "copy", "lr") + T(wab, AB["ff"], FH, "copy", "ff")
         + T(wab, AB["q"], 1024, "copy", "q") + T(wab, AB["gate"], 1024, "silu", "gate")
         + T(wab, AB["fq"], 2048, "copy", "fq") + T(wab, AB["fgate"], 1024, "silu", "fgate")
         + N(wab, AB["v"], 1024, "v") + N(wab, AB["fv"], 1024, "fv")),
        ("A", resid(as3("ab_w_out"))),
        ("A", N(wc, 0, D, "u") + T(wc, D, D, "silu", "sgate")),
        ("A", [Region(window(as3("glu_w")), KT, 0, D // BLK, BLK, "T", "glu")]),
        ("B", resid(as3("c_w_out"))),
        ("B", T(w0, L0["x"], 1024, "copy", "rx") + T(w0, L0["gate"], 1024, "silu", "rgate")
         + T(w0, L0["q"], 1024, "copy", "wq") + T(w0, L0["k"], 128, "copy", "wkv")
         + N(w0, L0["v"], 128, "wv") + T(w0, L0["sgate"], 1024, "silu", "wgate")),
        ("B", resid(inp["l0_w_out_2"])),
        ("B", [Region(window(w1), KT, L1["cq"], 1, BLK, "T", "keep", None, 0, 0),
               Region(window(w1), KT, L1["cq"] + BLK, 1, MQR - BLK, "T", "keep", None, 0, 4),
               Region(window(w1), KT, L1["ckv"], 1, BLK, "T", "keep", None, 0, 6)]
         + T(w1, L1["kr"], MROPE, "copy", "kr") + T(w1, L1["gate"], 1024, "silu", "mgate")
         + T(w1, L1["dq"], 2048, "copy", "dq") + T(w1, L1["dgate"], 1024, "silu", "dgate")
         + N(w1, L1["dv"], 1024, "dv")),
        ("LQ", [Region(heads_of(uq, 4, 0, MNOPE), MQR // P, 0, 2, BLK, "T", "copy", to_zt("qn")),
                Region(heads_of(uq, 8, MNOPE, MROPE), MQR // P, 0, 1, BLK, "T", "copy", to_zt("qr"))]),
        ("LK", [Region(heads_of(ukv, 4, 0, MNOPE), MKVR // P, 0, 2, BLK, "T", "copy", to_zt("kn")),
                Region(heads_of(ukv, 4, MNOPE, P), MKVR // P, 0, 2, BLK, "N", "copy", to_zn("mv"))]),
        ("B", resid(inp["l1_w_out_2"])),
    ]
    PHASES = PHASES[:NPHASES]
    pieces_in_all = count_regions([r for _, rs in PHASES for r in rs])
    for n, (_, regions) in enumerate(PHASES):
        for r in regions:
            r.peel = n in (0, 2, 3, 5, 7) and r is regions[0]

    landed, at_slot = [], [0] * RING
    for _, rs in PHASES:
        for r in rs:
            if r.kts != KT:
                r.dmas = PK
            for n in range(r.piece0, r.piece0 + r.blocks * r.pieces):
                at_slot[n % RING] += 16 * r.dmas
                landed.append(at_slot[n % RING])
    in_order = [r for _, rs in PHASES for r in rs]
    for r, after in zip(in_order, in_order[1:] + [None]):
        r.peel_last = after is None or after.dmas != r.dmas

    def each_block(eng, r, body, unroll=False):
        first = 1 if (0 in r.bank0[:r.banks] or r.piece0 < 2 * RING or r.dst is not None and 0 in r.stage0[:r.banks]
                      or r.evac == "resid" or r.peel) else 0
        last = 1 if r.peel_last else 0
        looped = r.blocks - first - last if r.pieces % RING == 0 and r.evac != "keep" and not unroll else 0
        if looped < 2:
            for i in range(r.blocks):
                body(i)
            return
        if first:
            body(0)
        with eng.Fori(first, first + looped) as i:
            body(i)
        if last:
            body(r.blocks - 1)

    def fixed(v):
        return isinstance(v, int)

    def sp_loads(sp, r):
        def body(i):
            for q in range(r.pieces):
                n = r.piece0 + q + i * r.pieces
                slot = (r.piece0 + q + (i * r.pieces if fixed(i) else 0)) % RING
                if r.evac == "glu" and fixed(i) and i == 0 and q == AHEAD + RING:
                    s5_sp(sp)
                if not fixed(i) or n >= RING:
                    sp.wait_ge(lo_ready, n - RING + 1)
                src = r.w(i, q, r.c0)
                if r.dmas == PK:
                    for k in range(PK):
                        sp.dma_start(raw[:, slot, k * BLK:(k + 1) * BLK].rearrange("p (h c) -> p h c", h=src.shape[2]),
                                     src[:, k]).then_inc(raw_in[slot], 16)
                else:
                    sp.dma_start(raw[:, slot, :].rearrange("p (k n) -> p k n", k=PK), src).then_inc(raw_in[slot], 16)
        each_block(sp, r, body)

    def split_hi(act, n, slot, target):
        if not fixed(n) or n < pieces_in_all:
            act.wait_ge(raw_in[slot], target)
            if not fixed(n) or n >= RING:
                act.wait_ge(w_used, n - RING + 1)
            nc.scalar.activation(whi[:, slot, :], raw[:, slot, :], ACT.Copy).then_inc(hi_ready, 1)

    def split_lo(dve, n, slot, target):
        if not fixed(n) or n < pieces_in_all:
            dve.wait_ge(hi_ready, n + 1)
            nc.vector.tensor_tensor(wlo[:, slot, :], raw[:, slot, :], whi[:, slot, :].bitcast(F32),
                                    ALU.subtract).then_inc(lo_ready, 1)

    def splits(eng, r, i, split):
        for q in range(r.pieces):
            n = r.piece0 + q + AHEAD + i * r.pieces
            if fixed(i):
                split(eng, n, n % RING, landed[n] if n < pieces_in_all else None)
            else:
                first = r.piece0 + q + AHEAD
                split(eng, n, first % RING, landed[first] + i * (16 * r.pieces // RING))

    def bank_full(eng, r, i, m):
        if m == r.banks - 1:
            eng.wait_ge(w_used, r.piece0 + r.pieces + i * r.pieces)
        else:
            eng.wait_ge(bank_ready[m], r.ready0[m] + 1 + i)

    ready = [0] * MT
    for _, rs in PHASES:
        for r in rs:
            r.ready0 = list(ready)
            for m in range(r.banks - 1):
                ready[m] += r.blocks

    def act_block(act, r, i, extra):
        splits(act, r, i, split_hi)
        if r.evac in ("copy", "silu"):
            for m in range(r.banks):
                bank_full(act, r, i, m)
                if not fixed(i) or r.stage0[m] + i > 0:
                    act.wait_ge(stored[m], 16 * r.stage0[m] + 16 * i)
                nc.scalar.activation(stage[:r.rows(m), m, :r.cols()], pg[m][:r.rows(m), :r.cols()],
                                     ACT.Copy if r.evac == "copy" else ACT.Silu).then_inc(evacd[m], 1)
        elif r.evac == "resid":
            x, _, sq, _ = X_OF["B" if extra["src"] == "A" else "A"]
            for m in range(r.banks):
                act.wait_ge(evacd[m], r.bank0[m] + 1 + i)
                if m >= 2 or not fixed(i) or i:
                    act.wait_ge(acc_done, extra["acc0"] + m - 1 + i * MT)
                nc.scalar.activation(sq[:, m % 2, :], x[:, bass.ds(i * MT + m, 1), :], ACT.Square).then_inc(sq_ready, 1)
        elif r.evac == "glu":
            for m in range(r.banks):
                bank_full(act, r, i, m)
                if i:
                    act.wait_ge(glu_mid, MT * (i - 1) + m + 1)
                nc.scalar.activation(stage[:, m, :], pg[m][:, :], ACT.Sigmoid,
                                     bias=col("glu_b", MT * i + m)).then_inc(evacd[m], 1)
            for m in range(r.banks):
                n = MT * i + m
                act.wait_ge(glu_done, n + 1)
                nc.scalar.activation(B["b_hi"][:, n, :], G["glu_z"][:, n % 2, :], ACT.Copy).then_inc(glu_hi, 1)

    def dve_block(dve, r, i, extra):
        splits(dve, r, i, split_lo)
        if r.evac == "resid":
            x, xin, _, _ = X_OF["B" if extra["src"] == "A" else "A"]
            for m in range(r.banks):
                bank_full(dve, r, i, m)
                dve.wait_ge(xin_in[m], 16 * (extra["xin0"] + 1) + 16 * i)
                nc.vector.tensor_tensor(x[:, bass.ds(i * MT + m, 1), :], xin[:, m:m + 1, :], pg[m][:, :],
                                        ALU.add).then_inc(evacd[m], 1)
        elif r.evac == "keep":
            for m in range(r.banks):
                bank_full(dve, r, i, m)
                dve.wait_ge(x_stored, 16 * 4)
                nc.vector.tensor_copy(M["latent"][:, r.arg + m, :], pg[m][:, :]).then_inc(evacd[m], 1)
        elif r.evac == "glu":
            for m in range(r.banks):
                n = MT * i + m
                z, g = G["glu_z"][:, n % 2, :], G["glu_g"][:, n % 2, :]
                dve.wait_ge(evacd[m], r.bank0[m] + i + 1)
                dve.wait_ge(glu_in[n % 2], 8 * KT + 32 * (n // 2 + 1))
                nc.vector.tensor_tensor(g, stage[:, m, :], g, ALU.mult).then_inc(glu_mid, 1)
                dve.wait_ge(glu_mid, n + 1)
                nc.vector.tensor_tensor(z, z, g, ALU.mult).then_inc(glu_done, 1)
                dve.wait_ge(glu_hi, n + 1)
                nc.vector.tensor_tensor(B["b_lo"][:, n, :], z, B["b_hi"][:, n, :].bitcast(F32),
                                        ALU.subtract).then_inc(glu_lo, 1)

    def pe_block(pe, r, i, extra):
        hi, lo = extra["hilo"]
        for q in range(r.pieces):
            n = r.piece0 + q + i * r.pieces
            slot = (r.piece0 + q + (i * r.pieces if fixed(i) else 0)) % RING
            pe.wait_ge(lo_ready, n + 1)
            for m in range(r.banks):
                if q == 0 and (not fixed(i) or r.bank0[m] + i > 0):
                    pe.wait_ge(evacd[m], r.bank0[m] + i)
                for k in range(PK):
                    kt = q * PK + k
                    if m == 0 and extra["h0"] is not None and fixed(i) and i == 0 and r is extra["first"]:
                        pe.wait_ge(h_ready, extra["h0"] + kt + 1)
                    for n_pass, (ws, hs) in enumerate(((whi, hi), (whi, lo), (wlo, hi))):
                        c = k * BLK
                        if r.form == "T":
                            lhsT = ws[:, slot, c + m * P:c + (m + 1) * P]
                            rhs = hs[:, kt, :]
                        else:
                            lhsT = hs[:, kt, m * P:(m + 1) * P]
                            rhs = ws[:, slot, c:c + r.width]
                        ins = nc.tensor.matmul(pg[m][:, :r.cols()], lhsT, rhs,
                                               start=(kt == 0 and n_pass == 0),
                                               stop=(kt == r.kts - 1 and n_pass == 2))
                if m == r.banks - 1:
                    ins.then_inc(w_used, 1)
                elif q == r.pieces - 1:
                    ins.then_inc(bank_ready[m], 1)

    def pool_block(pool, r, i, extra):
        if r.dst is not None:
            for m in range(r.banks):
                pool.wait_ge(evacd[m], r.bank0[m] + 1 + i)
                pool.dma_start(r.dst(i, m, r), stage[:r.rows(m), m, :r.cols()]).then_inc(stored[m], 16)
        elif r.evac == "resid":
            _, xin, sq, _ = X_OF["B" if extra["src"] == "A" else "A"]
            for m in range(r.banks):
                pool.wait_ge(evacd[m], r.bank0[m] + i)
                pool.dma_start(xin[:, m, :], extra["old"][bass.ds((i * MT + m) * P, P), :]).then_inc(xin_in[m], 16)
            for m in range(r.banks):
                pool.wait_ge(sq_ready, extra["acc0"] + m + 1 + i * MT)
                if m or not fixed(i) or i or extra["acc0"]:
                    pool.wait_ge(acc_done, extra["acc0"] + m + i * MT)
                if fixed(i) and i == 0 and m == 0:
                    nc.gpsimd.tensor_copy(acc[:, :], sq[:, 0, :]).then_inc(acc_done, 1)
                else:
                    nc.gpsimd.tensor_tensor(acc[:, :], acc[:, :], sq[:, m % 2, :], ALU.add).then_inc(acc_done, 1)
        elif r.evac == "glu":
            for m in range(r.banks):
                n = MT * i + m
                if n >= 2:
                    pool.wait_ge(glu_lo, n - 1)
                for name, src in (("glu_z", "z"), ("glu_g", "sgate")):
                    pool.dma_start(G[name][:, n % 2, :], zt[ZT[src] + n * P:ZT[src] + (n + 1) * P, :]).then_inc(glu_in[n % 2], 16)

    norms = {"n": 0}

    def squares_act(act, x, sq, base):
        for kt in range(KT):
            if kt >= 2:
                act.wait_ge(acc_done, base + kt - 1)
            nc.scalar.activation(sq[:, kt % 2, :], x[:, kt, :], ACT.Square).then_inc(sq_ready, 1)

    def squares_pool(pool, sq, base):
        for kt in range(KT):
            pool.wait_ge(sq_ready, base + kt + 1)
            if kt == 0:
                nc.gpsimd.tensor_copy(acc[:, :], sq[:, 0, :]).then_inc(acc_done, 1)
            else:
                pool.wait_ge(acc_done, base + kt)
                nc.gpsimd.tensor_tensor(acc[:, :], acc[:, :], sq[:, kt % 2, :], ALU.add).then_inc(acc_done, 1)

    def rstd_pe(pe, j):
        pe.wait_ge(acc_done, KT * (j + 1))
        if j:
            pe.wait_ge(sd_ready, j)
        nc.tensor.matmul(pm[0][:, :], ones[:, :], acc[:, :], start=True, stop=True).then_inc(rs_ready, 1)

    def rstd_act(act, j):
        act.wait_ge(rs_ready, j + 1)
        if j:
            act.wait_ge(xn_ready, xn_after[j])
        nc.scalar.activation(rstd[:, :], pm[0][:, :], ACT.Sqrt, scale=1.0 / D, bias=eps[:, 0:1]).then_inc(sd_ready, 1)

    def rstd_dve(dve, j):
        dve.wait_ge(sd_ready, j + 1)
        nc.vector.reciprocal(rstd[:, :], rstd[:, :]).then_inc(rstd_ready, 1)
        dve.wait_ge(rstd_ready, j + 1)

    xn_after = [0, 16, 32, 48, 64, 80, 96]

    def split_norm_dve(dve, x, xn, gain, hi, lo, j, done):
        def sub(kt):
            dve.wait_ge(nh_ready, done + kt + 1)
            nc.vector.tensor_tensor(lo[:, kt, :], xn[:, kt % 2, :], hi[:, kt, :].bitcast(F32),
                                    ALU.subtract).then_inc(h_ready, 1)
        for kt in range(KT):
            if kt >= 2:
                dve.wait_ge(h_ready, done + kt - 1)
            nc.vector.scalar_tensor_tensor(out=xn[:, kt % 2, :], in0=x[:, kt, :], scalar=col(gain, kt),
                                           in1=rstd[:, :], op0=ALU.mult, op1=ALU.mult).then_inc(xn_ready, 1)
            if kt:
                sub(kt - 1)
        sub(KT - 1)

    def split_norm_act(act, xn, hi, j, done):
        for kt in range(KT):
            act.wait_ge(xn_ready, xn_after[j] + kt + 1)
            nc.scalar.activation(hi[:, kt, :], xn[:, kt % 2, :], ACT.Copy).then_inc(nh_ready, 1)

    def scale_x_dve(dve, x, gain, j):
        for kt in range(KT):
            nc.vector.scalar_tensor_tensor(out=x[:, kt, :], in0=x[:, kt, :], scalar=col(gain, kt),
                                           in1=rstd[:, :], op0=ALU.mult, op1=ALU.mult).then_inc(xn_ready, 1)

    xt_in = [sem(f"x_tokens_in{n}") for n in range(2)]
    xt_ready, xt_ev = sem("x_transposed"), sem("x_tile_copied")

    def turn_in_pool(pool):
        for t in range(NTOK):
            if t >= 2:
                pool.wait_ge(xt_ready, 4 * (t - 1))
            pool.dma_start(XB["xb_tok"][:, t % 2, :], inp["x"][0, t * P:(t + 1) * P, :]).then_inc(xt_in[t % 2], 16)

    def turn_in_pe(pe):
        for n in range(4 * NTOK):
            t, c = n // 4, n % 4
            pe.wait_ge(xt_in[t % 2], 16 * (t // 2 + 1))
            if n == 3:
                pe.wait_ge(cols_ready, 1)
            if n >= 4:
                pe.wait_ge(xt_ev, n - 3)
            for k in range(4):
                ins = nc.tensor.transpose(pm[n % 4][:, k * P:(k + 1) * P],
                                          XB["xb_tok"][:, t % 2, (4 * c + k) * P:(4 * c + k + 1) * P], ident[:, :])
            ins.then_inc(xt_ready, 1)

    def turn_in_dve(dve):
        for n in range(4 * NTOK):
            t, c = n // 4, n % 4
            dve.wait_ge(xt_ready, n + 1)
            nc.vector.tensor_copy(XB["xb"][:, 4 * c:4 * c + 4, t * P:(t + 1) * P],
                                  pm[n % 4][:, :].rearrange("p (k t) -> p k t", k=4)).then_inc(xt_ev, 1)

    yt_out = [sem(f"y_tokens_out{n}") for n in range(2)]
    yt_ready, yt_ev = sem("y_transposed"), sem("y_tile_copied")

    def turn_out_pe(pe, x):
        pe.wait_ge(xn_ready, xn_after[6])
        for n in range(4 * NTOK):
            t, c = n // 4, n % 4
            if n >= 3:
                pe.wait_ge(yt_ev, n - 2)
            for k in range(4):
                ins = nc.tensor.transpose(pm[1 + n % 3][:, k * P:(k + 1) * P], x[:, 4 * c + k, t * P:(t + 1) * P],
                                          ident[:, :])
            ins.then_inc(yt_ready, 1)

    def turn_out_act(act, tok):
        for n in range(4 * NTOK):
            t, c = n // 4, n % 4
            act.wait_ge(yt_ready, n + 1)
            if t >= 2:
                act.wait_ge(yt_out[t % 2], 16 * (t // 2))
            nc.scalar.activation(tok[:, t % 2, 4 * c * P:4 * (c + 1) * P], pm[1 + n % 3][:, :], ACT.Copy).then_inc(yt_ev, 1)

    def turn_out_pool(pool, tok):
        for t in range(NTOK):
            pool.wait_ge(yt_ev, 4 * (t + 1))
            pool.dma_start(out[0, t * P:(t + 1) * P, :], tok[:, t % 2, :]).then_inc(yt_out[t % 2], 16)
        for n in range(2):
            pool.wait_ge(yt_out[n], 16 * (NTOK // 2))

    def store_x(pool, x, n):
        pool.wait_ge(acc_done, {0: 16, 1: 32, 2: 64, 3: 80}[n])
        pool.dma_start(xds[n].rearrange("(k p) t -> p k t", p=P), x[:, :, :]).then_inc(x_stored, 16)

    def pool_end(pool, n):
        for m in range(MT):
            pool.wait_ge(stored[m], 16 * sum(r.blocks for _, rs in PHASES[:n + 1] for r in rs if m < r.banks and r.dst is not None))
        pool.wait_ge(x_stored, 16 * {0: 1, 2: 2, 5: 3, 7: 4, 9: 4}[n])

    LEVELS = 8
    V0 = overlay(HALF, [
        ("g_q", [2, L], F32), ("g_k", [2, L], F32), ("g_v", [2, NTOK, GDV], F32), ("g_gate", [2, 2, L], F32),
        ("g_z", [L], F32), ("g_m", [L], F32), ("g_b", [L], F32), ("g_e", [2, L], F32),
        ("g_qe", [2, L], F32), ("g_ke", [2, L], F32), ("g_s", [NTOK, P], F32), ("g_qb", [L], F32),
        ("g_kd", [L], F32), ("g_kt", [NTOK, P], F32), ("g_state", [2, GDV], F32), ("g_sq", [2, L], F32),
        ("g_o", [2, L], F32), ("g_one", [P], F32), ("g_last4", [NTOK], F32)])
    EX0 = overlay(EXTRA, [("g_lr", [L], F32), ("g_up", [L], F32), ("g_masks", [LEVELS, P], F32)])
    gla_in = [sem(f"gla_head_in{n}") for n in range(2)]
    shared_in = sem("shared_operands_in")
    gz_ready, gz_read, gln_ready, gdl_ready = sem("gla_gate_ready"), sem("gla_gate_read"), sem("gla_ln_ready"), sem("gla_b_ready")
    ged_ready, gkd_ready, gkt_ready, gktok_ready = sem("gla_decays"), sem("gla_kd"), sem("gla_kd_turned"), sem("gla_kd_copied")
    gd_ready, gE_ready, gq_ready, gk_ready = sem("gla_level_diff"), sem("gla_level_exp"), sem("gla_level_q"), sem("gla_level_k")
    gs_ready, gsel_done = sem("gla_level_scores"), sem("gla_level_picked")
    gkv_ready, gst_ready, go_ready = sem("gla_kv"), sem("gla_state"), sem("gla_out")
    gsq_ready, gss_ready, gsd_ready, gf_ready, gf_hi, gf_lo = (sem("gla_out_sq"), sem("gla_out_sum"), sem("gla_out_dev"),
                                                               sem("gla_fin"), sem("gla_fin_hi"), sem("gla_fin_lo"))

    def gla_pool(pool):
        pool.dma_start(EX0["g_lr"][:GRANK, :], zt[ZT["lr"]:ZT["lr"] + GRANK, :]).then_inc(shared_in, 16)
        pool.dma_start(EX0["g_up"][:GRANK, :], inp["gla_alpha_up"][0]).then_inc(shared_in, 16)
        pool.dma_start(EX0["g_masks"][:, :, :], inp["masks"].rearrange("p (l j) -> p l j", l=LEVELS)).then_inc(shared_in, 16)
        for h in range(GH):
            s = h % 2
            if h >= 2:
                pool.wait_ge(gf_lo, 2 * (h - 1))
            pool.dma_start(V0["g_q"][:, s, :], zt[ZT["q"] + h * P:ZT["q"] + (h + 1) * P, :]).then_inc(gla_in[s], 16)
            pool.dma_start(V0["g_k"][:, s, :], zt[ZT["k"] + h * P:ZT["k"] + (h + 1) * P, :]).then_inc(gla_in[s], 16)
            pool.dma_start(V0["g_v"][:, s, :, :], zn[:, ZN["v"] + h * GDV:ZN["v"] + (h + 1) * GDV].rearrange(
                "(t p) c -> p t c", p=P)).then_inc(gla_in[s], 16)
            pool.dma_start(V0["g_gate"][:, s, :, :], zt[ZT["gate"] + h * GDV:ZT["gate"] + (h + 1) * GDV, :].rearrange(
                "(e p) t -> p e t", p=P)).then_inc(gla_in[s], 16)
            pool.wait_ge(gla_in[s], 64 * (h // 2 + 1))
            for lv in range(1, LEVELS):
                n = 7 * h + lv - 1
                pool.wait_ge(gE_ready, n + 1)
                if n >= 2:
                    pool.wait_ge(gs_ready, LEVELS * h + lv - 1 if lv > 2 else LEVELS * h)
                nc.gpsimd.tensor_tensor(V0["g_ke"][:, n % 2, :], V0["g_k"][:, s, :], V0["g_e"][:, n % 2, :],
                                        ALU.mult).then_inc(gk_ready, 1)

    def gla_pe(pe):
        pe.wait_ge(shared_in, 48)
        for h in range(GH):
            s = h % 2
            if h:
                pe.wait_ge(gz_read, h)
            nc.tensor.matmul(pm[0][:, :], EX0["g_up"][:GRANK, h * P:(h + 1) * P], EX0["g_lr"][:GRANK, :],
                             start=True, stop=True).then_inc(gz_ready, 1)
            pe.wait_ge(gkd_ready, h + 1)
            if h:
                pe.wait_ge(gktok_ready, h)
            for c in range(NTOK):
                ins = nc.tensor.transpose(pm[1][:, c * P:(c + 1) * P], V0["g_kd"][:, c * P:(c + 1) * P], ident[:, :])
            ins.then_inc(gkt_ready, 1)
            for lv in range(LEVELS):
                n = LEVELS * h + lv
                e = 7 * h + lv - 1
                if lv:
                    pe.wait_ge(gq_ready, 8 * h + lv + 1)
                    pe.wait_ge(gk_ready, e + 1)
                    q, k = V0["g_qe"][:, e % 2, :], V0["g_ke"][:, e % 2, :]
                else:
                    pe.wait_ge(gla_in[s], 64 * (h // 2 + 1))
                    pe.wait_ge(gq_ready, 8 * h + 1)
                    q, k = V0["g_q"][:, s, :], V0["g_k"][:, s, :]
                if n >= 2:
                    pe.wait_ge(gsel_done, n - 1)
                for c in range(NTOK):
                    ins = nc.tensor.matmul(pm[2 + n % 2][:, c * P:(c + 1) * P], k[:, c * P:(c + 1) * P],
                                           q[:, c * P:(c + 1) * P], start=True, stop=True)
                ins.then_inc(gs_ready, 1)
            pe.wait_ge(gsel_done, LEVELS * (h + 1))
            pe.wait_ge(gktok_ready, h + 1)
            if h:
                pe.wait_ge(gf_ready, 2 * h)
            for c in range(NTOK):
                if c or h:
                    pe.wait_ge(gst_ready, 3 * h + c)
                if c < NTOK - 1:
                    nc.tensor.matmul(pg[2][:, :GDV], V0["g_kt"][:, c, :], V0["g_v"][:, s, c, :],
                                     start=True, stop=True).then_inc(gkv_ready, 1)
                for e in range(2):
                    ins = nc.tensor.matmul(pg[e][:, c * P:(c + 1) * P], V0["g_v"][:, s, c, e * P:(e + 1) * P],
                                           V0["g_s"][:, c, :], start=True, stop=(c == 0))
                    if c:
                        ins = nc.tensor.matmul(pg[e][:, c * P:(c + 1) * P],
                                               V0["g_state"][:, (c - 1) % 2, e * P:(e + 1) * P],
                                               V0["g_qb"][:, c * P:(c + 1) * P], start=False, stop=True)
                if c == NTOK - 1:
                    ins.then_inc(go_ready, 1)
            pe.wait_ge(gsq_ready, 2 * (h + 1))
            if h:
                pe.wait_ge(gsd_ready, h)
            for e in range(2):
                ins = nc.tensor.matmul(pg[3][:, :], ones[:, :], V0["g_sq"][:, e, :], start=(e == 0), stop=(e == 1))
            ins.then_inc(gss_ready, 1)

    def gla_act(act):
        run = serial(act, act_seq)
        for h in range(GH):
            act.wait_ge(gz_read, h + 1)
            run(nc.scalar.activation(V0["g_m"][:, :], V0["g_z"][:, :], ACT.Abs))
            run(nc.scalar.activation(V0["g_m"][:, :], V0["g_m"][:, :], ACT.Exp, scale=-1.0))
            nc.scalar.activation(V0["g_m"][:, :], V0["g_m"][:, :], ACT.Ln, bias=V0["g_one"][:, 0:1]).then_inc(gln_ready, 1)
            act.wait_ge(gdl_ready, h + 1)
            if h:
                act.wait_ge(go_ready, h)
            run(nc.scalar.activation(V0["g_qb"][:, :], V0["g_b"][:, :], ACT.Exp))
            nc.scalar.activation(V0["g_kd"][:, :], V0["g_kd"][:, :], ACT.Exp, scale=-1.0).then_inc(ged_ready, 1)
            act.wait_ge(gkt_ready, h + 1)
            nc.scalar.activation(V0["g_kt"][:, :, :], pm[1][:, :], ACT.Copy).then_inc(gktok_ready, 1)
            for lv in range(1, LEVELS):
                n = 7 * h + lv - 1
                act.wait_ge(gd_ready, n + 1)
                run(nc.scalar.activation(V0["g_e"][:, n % 2, :], V0["g_e"][:, n % 2, :], ACT.Abs))
                nc.scalar.activation(V0["g_e"][:, n % 2, :], V0["g_e"][:, n % 2, :], ACT.Exp, scale=-1.0).then_inc(gE_ready, 1)
            act.wait_ge(go_ready, h + 1)
            if h:
                act.wait_ge(gss_ready, h)
            for e in range(2):
                nc.scalar.activation(V0["g_sq"][:, e, :], pg[e][:, :], ACT.Square).then_inc(gsq_ready, 1)
            act.wait_ge(gss_ready, h + 1)
            if h:
                act.wait_ge(gf_ready, 2 * h)
            nc.scalar.activation(rstd[:, :], pg[3][:, :], ACT.Sqrt, scale=1.0 / GDV, bias=eps[:, 0:1]).then_inc(gsd_ready, 1)
            for e in range(2):
                act.wait_ge(gf_ready, 2 * h + e + 1)
                nc.scalar.activation(A["a_hi"][:, 2 * h + e, :], V0["g_o"][:, e, :], ACT.Copy).then_inc(gf_hi, 1)

    def gla_dve(dve):
        run = serial(dve, dve_seq)
        vec = nc.vector
        tt = vec.tensor_tensor
        run(vec.memset(V0["g_one"][:, :], 1.0))
        dve.wait_ge(shared_in, 48)
        for h in range(GH):
            s = h % 2
            dve.wait_ge(gz_ready, h + 1)
            vec.tensor_scalar(V0["g_z"][:, :], pm[0][:, :], col("alpha_b", h), None, ALU.add).then_inc(gz_read, 1)
            dve.wait_ge(gz_read, h + 1)
            dve.wait_ge(gla_in[s], 64 * (h // 2 + 1))
            if h:
                dve.wait_ge(gE_ready, 7 * h)
            vec.tensor_scalar(V0["g_q"][:, s, :], V0["g_q"][:, s, :], GDK ** -0.5, None, ALU.mult).then_inc(gq_ready, 1)
            dve.wait_ge(gln_ready, h + 1)
            run(vec.tensor_scalar(V0["g_z"][:, :], V0["g_z"][:, :], 0.0, 1.0 / GTAU, ALU.min, ALU.mult))
            run(vec.scalar_tensor_tensor(out=V0["g_z"][:, :], in0=V0["g_m"][:, :], scalar=-1.0 / GTAU,
                                         in1=V0["g_z"][:, :], op0=ALU.mult, op1=ALU.add))
            for c in range(NTOK):
                cs = slice(c * P, (c + 1) * P)
                run(vec.tensor_tensor_scan(V0["g_b"][:, cs], V0["g_one"][:, :], V0["g_z"][:, cs], 0.0, ALU.mult, ALU.add))
            b3 = V0["g_b"][:, :].rearrange("p (c t) -> p c t", t=P)
            tt(V0["g_kd"][:, :].rearrange("p (c t) -> p c t", t=P), b3, b3[:, :, P - 1:P].broadcast_to([P, NTOK, P]),
               ALU.subtract).then_inc(gdl_ready, 1)

            def diff(lv):
                n = 7 * h + lv - 1
                step = 2 ** (lv - 1)
                if n >= 2:
                    dve.wait_ge(gq_ready, 8 * h + lv - 1 if lv > 2 else 8 * h)
                    dve.wait_ge(gk_ready, n - 1)
                v = V0["g_b"][:, :].rearrange("p (c t) -> p c t", t=2 * step)
                tt(V0["g_e"][:, n % 2, :].rearrange("p (c t) -> p c t", t=2 * step), v,
                   v[:, :, step - 1:step].broadcast_to([P, L // (2 * step), 2 * step]), ALU.subtract).then_inc(gd_ready, 1)

            def pick(lv):
                n = LEVELS * h + lv
                dve.wait_ge(gs_ready, n + 1)
                scores = pm[2 + n % 2][:, :].rearrange("p (c t) -> p c t", t=P)
                mask = EX0["g_masks"][:, lv:lv + 1, :].broadcast_to([P, NTOK, P])
                if lv == 0:
                    if h:
                        dve.wait_ge(go_ready, h)
                    tt(V0["g_s"][:, :, :], scores, mask, ALU.mult).then_inc(gsel_done, 1)
                else:
                    dve.wait_ge(gsel_done, n)
                    vec.copy_predicated(V0["g_s"][:, :, :], mask.bitcast(I32), scores).then_inc(gsel_done, 1)

            dve.wait_ge(ged_ready, h + 1)
            dve.wait_ge(gq_ready, 8 * h + 1)
            run(vec.tensor_copy(V0["g_last4"][:, :], V0["g_qb"][:, :].rearrange("p (c t) -> p c t", t=P)[:, :, P - 1]))
            run(tt(V0["g_qb"][:, :], V0["g_qb"][:, :], V0["g_q"][:, s, :], ALU.mult))
            tt(V0["g_kd"][:, :], V0["g_kd"][:, :], V0["g_k"][:, s, :], ALU.mult).then_inc(gkd_ready, 1)
            diff(1)
            for lv in range(1, LEVELS + 1):
                if lv + 1 < LEVELS:
                    diff(lv + 1)
                if lv < LEVELS:
                    n = 7 * h + lv - 1
                    dve.wait_ge(gE_ready, n + 1)
                    if n >= 2:
                        dve.wait_ge(gs_ready, LEVELS * h + lv - 1 if lv > 2 else LEVELS * h)
                    tt(V0["g_qe"][:, n % 2, :], V0["g_q"][:, s, :], V0["g_e"][:, n % 2, :], ALU.mult).then_inc(gq_ready, 1)
                pick(lv - 1)
            for c in range(NTOK - 1):
                dve.wait_ge(gkv_ready, 3 * h + c + 1)
                if c == 0:
                    vec.tensor_copy(V0["g_state"][:, 0, :], pg[2][:, :GDV]).then_inc(gst_ready, 1)
                else:
                    dve.wait_ge(gst_ready, 3 * h + c)
                    vec.scalar_tensor_tensor(out=V0["g_state"][:, c % 2, :], in0=V0["g_state"][:, (c - 1) % 2, :],
                                             scalar=V0["g_last4"][:, c:c + 1], in1=pg[2][:, :GDV],
                                             op0=ALU.mult, op1=ALU.add).then_inc(gst_ready, 1)
            dve.wait_ge(gsd_ready, h + 1)
            run(vec.reciprocal(rstd[:, :], rstd[:, :]))
            for e in range(2):
                if h:
                    dve.wait_ge(gf_lo, 2 * (h - 1) + e + 1)
                run(vec.scalar_tensor_tensor(out=V0["g_o"][:, e, :], in0=pg[e][:, :], scalar=col("head_g", 2 * h + e),
                                             in1=rstd[:, :], op0=ALU.mult, op1=ALU.mult))
                tt(V0["g_o"][:, e, :], V0["g_o"][:, e, :], V0["g_gate"][:, s, e, :], ALU.mult).then_inc(gf_ready, 1)
            for e in range(2):
                dve.wait_ge(gf_hi, 2 * h + e + 1)
                tt(A["a_lo"][:, 2 * h + e, :], V0["g_o"][:, e, :], A["a_hi"][:, 2 * h + e, :].bitcast(F32),
                   ALU.subtract).then_inc(gf_lo, 1)

    att = dict(
        scores=sem("scores_ready"), nmax=sem("negated_max_ready"), probs=sem("exp_ready"), normed=sem("probs_normed"),
        turned=sem("probs_turned"), copied=sem("turned_copied"), pv=sem("pv_ready"), tile=sem("tile_gated"),
        hi=sem("tile_hi"), lo=sem("tile_lo"), sq=sem("tile_squares"), ss=sem("tile_square_sum"), sd=sem("tile_deviation"))
    att_in = [sem(f"attention_tile_in{n}") for n in range(2)]
    gate_in = [sem(f"attention_gate_in{n}") for n in range(2)]

    def head_rows(name):
        return lambda t: zt[ZT[name] + t * P:ZT[name] + (t + 1) * P, :]

    def place(a, j):
        return j // a.per, j // NTOK % a.heads, j % NTOK

    def att_pe(pe, a):
        def scores(u):
            t, h, qb = place(a, u // a.comps)
            n = a.units0 + u
            pe.wait_ge(att_in[t % 2], a.in0 + a.loads[1] * (t // 2 + 1))
            if n >= 2:
                pe.wait_ge(att["nmax"], n - 1)
            first, count = a.key_tiles(qb)
            ops = a.products(t, h, u % a.comps, qb, first, count)
            for i, (lhsT, rhs) in enumerate(ops):
                ins = nc.tensor.matmul(pm[n % 2][:, :count * P], lhsT, rhs, start=(i == 0), stop=(i == len(ops) - 1))
            ins.then_inc(att["scores"], 1)

        def turn(j):
            _, count = a.key_tiles(place(a, j)[2])
            n = a.jobs0 + j
            u = a.units0 + (j + 1) * a.comps
            pe.wait_ge(att["normed"], u)
            if n >= 2:
                pe.wait_ge(att["copied"], n - 1)
            for b in range(count):
                ins = nc.tensor.transpose(pm[2 + n % 2][:, b * P:(b + 1) * P],
                                          a.buf["p"][:, (u - 1) % 4, b * P:(b + 1) * P], ident[:, :])
            ins.then_inc(att["turned"], 1)

        def pv(j):
            t, h, qb = place(a, j)
            first, count = a.key_tiles(qb)
            n = a.jobs0 + j
            pe.wait_ge(att["copied"], n + 1)
            if a.tiles0 + t >= 2:
                pe.wait_ge(att["tile"], a.tiles0 + t - 1)
            rows = slice(h * a.dv, (h + 1) * a.dv)
            for b in range(count):
                ins = nc.tensor.matmul(pg[(a.tiles0 + t) % 2][rows, qb * P:(qb + 1) * P], a.value(t, h, first + b),
                                       a.buf["pt"][:, n % 2, b * P:(b + 1) * P], start=(b == 0), stop=(b == count - 1))
            ins.then_inc(att["pv"], 1)

        def square_sum(t):
            pe.wait_ge(att["sq"], t + 1)
            if t:
                pe.wait_ge(att["sd"], t)
            nc.tensor.matmul(pg[2][:, :], ones[:, :], a.buf["sq"][:, :], start=True, stop=True).then_inc(att["ss"], 1)

        for j in range(a.jobs + 3):
            for c in range(a.comps):
                if j < a.jobs:
                    scores(j * a.comps + c)
            if 1 <= j <= a.jobs:
                turn(j - 1)
            if 2 <= j < a.jobs + 2:
                pv(j - 2)
            if a.gain is not None and j >= a.per + 2 and (j - 2) % a.per == 0:
                square_sum((j - 2) // a.per - 1)

    def att_act(act, a):
        run = serial(act, act_seq)

        def exp(u):
            n = a.units0 + u
            t, h, _ = place(a, u // a.comps)
            first, count = a.key_tiles(place(a, u // a.comps)[2])
            act.wait_ge(att["nmax"], n + 1)
            s = n % 4
            if a.sink is not None:
                run(nc.scalar.activation(a.buf["small"][:, 12 + s:13 + s], a.sink(t, h), ACT.Exp,
                                         bias=a.buf["small"][:, s:s + 1]))
            p = a.buf["p"][:, s, :count * P]
            nc.scalar.activation(p, p, ACT.Exp, bias=a.buf["small"][:, s:s + 1],
                                 accum_out=a.buf["small"][:, 4 + s:5 + s]).then_inc(att["probs"], 1)

        def copy(j):
            n = a.jobs0 + j
            _, count = a.key_tiles(place(a, j)[2])
            act.wait_ge(att["turned"], n + 1)
            if n >= 2:
                act.wait_ge(att["pv"], n - 1)
            nc.scalar.activation(a.buf["pt"][:, n % 2, :count * P], pm[2 + n % 2][:, :count * P],
                                 ACT.Copy).then_inc(att["copied"], 1)

        def squares(t):
            n = a.tiles0 + t
            if a.gain is not None:
                act.wait_ge(att["pv"], a.jobs0 + (t + 1) * a.per)
                if t:
                    act.wait_ge(att["ss"], t)
                nc.scalar.activation(a.buf["sq"][:, :], pg[n % 2][:, :], ACT.Square).then_inc(att["sq"], 1)

        def round_tile(t):
            n = a.tiles0 + t
            if a.gain is not None:
                act.wait_ge(att["ss"], t + 1)
                if t:
                    act.wait_ge(att["tile"], n)
                nc.scalar.activation(rstd[:, :], pg[2][:, :], ACT.Sqrt, scale=1.0 / P, bias=eps[:, 0:1]).then_inc(att["sd"], 1)
            act.wait_ge(att["tile"], n + 1)
            nc.scalar.activation(a.hi[:, a.kt0 + t, :], a.buf["o"][:, t % 2, :], ACT.Copy).then_inc(att["hi"], 1)

        for j in range(a.jobs + 5):
            if j < a.jobs:
                for c in range(a.comps):
                    exp(j * a.comps + c)
            if 1 <= j <= a.jobs:
                copy(j - 1)
            if j >= a.per + 2 and (j - 2) % a.per == 0:
                squares((j - 2) // a.per - 1)
            if j >= a.per + 4 and (j - 4) % a.per == 0:
                round_tile((j - 4) // a.per - 1)

    def att_dve(dve, a):
        run = serial(dve, dve_seq)
        vec = nc.vector
        small = a.buf["small"]

        def maxes(u):
            n = a.units0 + u
            t, h, qb = place(a, u // a.comps)
            s = n % 4
            _, count = a.key_tiles(qb)
            dve.wait_ge(att["scores"], n + 1)
            if n >= 4:
                dve.wait_ge(att["turned"], a.jobs0 + (u - 4) // a.comps + 1 if u >= 4 else a.jobs0)
            if a.bias_ready is not None and u % (a.per * a.comps) == 0:
                a.bias_ready(dve, t)
            run(vec.tensor_tensor_reduce(out=a.buf["p"][:, s, :count * P], in0=pm[n % 2][:, :count * P],
                                         in1=a.bias(t, qb, count), scale=a.scale, scalar=LOWEST, op0=ALU.add,
                                         op1=ALU.max, accum_out=small[:, 8 + s:9 + s]))
            vec.tensor_scalar(small[:, s:s + 1], small[:, 8 + s:9 + s], a.sink(t, h) if a.sink is not None else LOWEST, -1.0,
                              ALU.max, ALU.mult).then_inc(att["nmax"], 1)

        def norm(u):
            n = a.units0 + u
            _, count = a.key_tiles(place(a, u // a.comps)[2])
            s = n % 4
            p = a.buf["p"][:, s, :count * P]
            dve.wait_ge(att["probs"], n + 1)
            if a.sink is not None:
                run(vec.tensor_tensor(small[:, 4 + s:5 + s], small[:, 4 + s:5 + s], small[:, 12 + s:13 + s], ALU.add))
            run(vec.reciprocal(small[:, 8 + s:9 + s], small[:, 4 + s:5 + s]))
            if u % a.comps == 0:
                vec.tensor_scalar(p, p, small[:, 8 + s:9 + s], None, ALU.mult).then_inc(att["normed"], 1)
            else:
                run(vec.tensor_tensor(small[:, 8 + s:9 + s], small[:, 8 + s:9 + s], a.lam, ALU.mult))
                dve.wait_ge(att["normed"], n)
                vec.scalar_tensor_tensor(out=p, in0=p, scalar=small[:, 8 + s:9 + s],
                                         in1=a.buf["p"][:, (n - 1) % 4, :count * P], op0=ALU.mult,
                                         op1=ALU.add).then_inc(att["normed"], 1)

        def gate(t):
            n = a.tiles0 + t
            if n >= 2:
                dve.wait_ge(att["lo"], n - 1)
            o = a.buf["o"][:, t % 2, :]
            dve.wait_ge(gate_in[t % 2], 16 * (n // 2 + 1))
            if a.gain is not None:
                dve.wait_ge(att["sd"], t + 1)
                run(vec.reciprocal(rstd[:, :], rstd[:, :]))
                run(vec.scalar_tensor_tensor(out=o, in0=pg[n % 2][:, :], scalar=a.gain, in1=rstd[:, :],
                                             op0=ALU.mult, op1=ALU.mult))
                vec.tensor_tensor(o, o, a.gate(t), ALU.mult).then_inc(att["tile"], 1)
            else:
                dve.wait_ge(att["pv"], a.jobs0 + (t + 1) * a.per)
                vec.tensor_tensor(o, pg[n % 2][:, :], a.gate(t), ALU.mult).then_inc(att["tile"], 1)

        def low(t):
            n = a.tiles0 + t
            dve.wait_ge(att["hi"], n + 1)
            vec.tensor_tensor(a.lo[:, a.kt0 + t, :], a.buf["o"][:, t % 2, :], a.hi[:, a.kt0 + t, :].bitcast(F32),
                              ALU.subtract).then_inc(att["lo"], 1)

        for j in range(a.jobs + 6):
            if j < a.jobs:
                for c in range(a.comps):
                    maxes(j * a.comps + c)
            if 1 <= j <= a.jobs:
                for c in range(a.comps):
                    norm((j - 1) * a.comps + c)
            if j >= a.per + 4 and (j - 4) % a.per == 0:
                gate((j - 4) // a.per - 1)
            if j >= a.per + 5 and (j - 5) % a.per == 0:
                low((j - 5) // a.per - 1)

    def att_pool(pool, a):
        for t in range(a.tiles):
            n = a.tiles0 + t
            if n >= 2:
                pool.wait_ge(att["pv"], a.jobs0 + max(t - 1, 0) * a.per)
            for dst, src in a.loads[0](t):
                pool.dma_start(dst, src).then_inc(att_in[t % 2], 16)
            if a.pool_work is not None:
                a.pool_work(pool, t)
            if n >= 2:
                pool.wait_ge(att["tile"], n - 1)
            pool.dma_start(a.gate(t), a.gate_of(t)).then_inc(gate_in[t % 2], 16)

    V1 = overlay(HALF, [
        ("f_p", [4, L], F32), ("f_pt", [2, L], F32), ("f_o", [2, L], F32), ("f_q", [2, L], F32),
        ("f_k", [2, L], F32), ("f_v", [2, NTOK, FD], F32), ("f_gate", [2, L], F32), ("f_nc", [2, L], F32),
        ("f_small", [16], F32), ("f_bias", [2, 10 * P], F32)])
    EX1 = overlay(EXTRA, [("f_ff", [L], F32), ("f_t", [L], F32), ("f_c", [L], F32), ("f_one", [L], F32)])
    ff_in, ff_read, ff_ln, ff_neg, negc_stored, fb_ready = (sem("forget_in"), sem("forget_read"), sem("forget_ln"),
                                                            sem("forget_sums"), sem("forget_stored"), sem("forget_bias"))

    def fox_pre_pool(pool):
        pool.dma_start(EX1["f_ff"][:FH, :], zt[ZT["ff"]:ZT["ff"] + FH, :]).then_inc(ff_in, 16)
        pool.wait_ge(ff_neg, 1)
        pool.dma_start(negc_dram[:, :], EX1["f_c"][:FH, :]).then_inc(negc_stored, 16)
        pool.wait_ge(negc_stored, 16)

    def fox_pre_dve(dve):
        run = serial(dve, dve_seq)
        run(nc.vector.memset(EX1["f_one"][:, :], 1.0))
        dve.wait_ge(ff_in, 16)
        z, t, c = EX1["f_ff"][:FH, :], EX1["f_t"][:FH, :], EX1["f_c"][:FH, :]
        nc.vector.tensor_scalar(z, z, cols[:FH, COL["f_b"]:COL["f_b"] + 1], None, ALU.add).then_inc(ff_read, 1)
        dve.wait_ge(ff_ln, 1)
        run(nc.vector.tensor_scalar(z, z, 0.0, None, ALU.min))
        run(nc.vector.tensor_tensor(z, z, t, ALU.subtract))
        run(nc.vector.tensor_tensor_scan(c, EX1["f_one"][:FH, :], z, 0.0, ALU.mult, ALU.add))
        nc.vector.tensor_scalar(c, c, -FD ** 0.5, None, ALU.mult).then_inc(ff_neg, 1)

    def fox_pre_act(act):
        run = serial(act, act_seq)
        z, t = EX1["f_ff"][:FH, :], EX1["f_t"][:FH, :]
        act.wait_ge(ff_read, 1)
        run(nc.scalar.activation(t, z, ACT.Abs))
        run(nc.scalar.activation(t, t, ACT.Exp, scale=-1.0))
        nc.scalar.activation(t, t, ACT.Ln, bias=onecol[:FH, 0:1]).then_inc(ff_ln, 1)

    def fox_loads(t):
        s = t % 2
        rows = lambda name: zt[ZT[name] + t * P:ZT[name] + (t + 1) * P, :]
        return [(V1["f_q"][:, s, :], rows("fq")), (V1["f_k"][:, s, :], rows("fk")),
                (V1["f_v"][:, s, :, :], zn[:, ZN["fv"] + t * FD:ZN["fv"] + (t + 1) * FD].rearrange("(b p) c -> p b c", p=P)),
                (V1["f_nc"][:, s, :], negc_dram[t:t + 1, :].broadcast_to([P, L]))]

    def fox_bias_pool(pool, t):
        pool.wait_ge(att_in[t % 2], 64 * (t // 2 + 1))
        for qb in range(NTOK):
            at = qb * (qb + 1) // 2 * P
            ins = nc.gpsimd.tensor_tensor(V1["f_bias"][:, t % 2, at:at + (qb + 1) * P], V1["f_nc"][:, t % 2, :(qb + 1) * P],
                                          wide[:, (NTOK - 1 - qb) * P:], ALU.add)
            ins.then_inc(fb_ready, 1)

    FOX = Attention(
        buf=dict(p=V1["f_p"], pt=V1["f_pt"], o=V1["f_o"], small=V1["f_small"]), tiles=FH, heads=1, comps=1, dv=FD,
        scale=FD ** -0.5, key_tiles=lambda qb: (0, qb + 1),
        products=lambda t, h, c, qb, first, count: [(V1["f_q"][:, t % 2, qb * P:(qb + 1) * P],
                                                     V1["f_k"][:, t % 2, :count * P])],
        bias=lambda t, qb, count: V1["f_bias"][:, t % 2, qb * (qb + 1) // 2 * P:(qb * (qb + 1) // 2 + count) * P],
        bias_ready=lambda dve, t: dve.wait_ge(fb_ready, NTOK * (t + 1)), pool_work=fox_bias_pool,
        value=lambda t, h, b: V1["f_v"][:, t % 2, b, :], gate=lambda t: V1["f_gate"][:, t % 2, :], kt0=KT // 2,
        loads=(fox_loads, 64), gate_of=head_rows("fgate"), hi=A["a_hi"], lo=A["a_lo"], units0=0, jobs0=0, tiles0=0, in0=0,
        sink=None, lam=None, gain=None)

    V2 = overlay(0, [
        ("r_x", [2, L + CW - 1], F32), ("r_gate", [2, L], F32), ("r_y", [2, L], F32), ("r_i", [2, L], F32),
        ("r_r", [2, L], F32), ("r_a", [2, L], F32), ("r_t", [2, L], F32), ("r_m", [L], F32), ("r_h", [L], F32),
        ("r_o", [2, L], F32), ("r_gx", [RB, P], F32), ("r_ga", [RB, P], F32), ("r_sp", [6, RB], F32)])
    ru_in = [sem(f"lru_tile_in{n}") for n in range(2)]
    ru_e, ru_sp, ru_y, ru_g, ru_s, ru_a, ru_m, ru_q, ru_o, ru_hi, ru_lo = (sem(f"lru_{n}") for n in (
        "exp_lambda", "softplus", "conv", "gate_sums", "gates", "decay", "gain", "gain_root", "out", "out_hi", "out_lo"))

    def lru_pool(pool):
        pool.dma_start(V2["r_gx"][:, :, :], inp["l0_gate_x_w_2"].rearrange("n d e -> d n e")).then_inc(shared_in, 16)
        pool.dma_start(V2["r_ga"][:, :, :], inp["l0_gate_a_w_2"].rearrange("n d e -> d n e")).then_inc(shared_in, 16)
        pool.wait_ge(ru_e, 2)
        for n in range(RB):
            s = n % 2
            if n >= 2:
                pool.wait_ge(ru_lo, n - 1)
            pool.dma_start(V2["r_x"][:, s, CW - 1:], zt[ZT["rx"] + n * P:ZT["rx"] + (n + 1) * P, :]).then_inc(ru_in[s], 16)
            pool.dma_start(V2["r_gate"][:, s, :], zt[ZT["rgate"] + n * P:ZT["rgate"] + (n + 1) * P, :]).then_inc(ru_in[s], 16)

    def lru_pe(pe):
        pe.wait_ge(shared_in, 80)
        for n in range(RB):
            pe.wait_ge(ru_y, n + 1)
            if n >= 2:
                pe.wait_ge(ru_s, 2 * (n - 1))
            nc.tensor.matmul(pm[2 * (n % 2)][:, :], V2["r_gx"][:, n, :], V2["r_y"][:, n % 2, :], start=True, stop=True)
            nc.tensor.matmul(pm[2 * (n % 2) + 1][:, :], V2["r_ga"][:, n, :], V2["r_y"][:, n % 2, :],
                             start=True, stop=True).then_inc(ru_g, 1)

    def lru_act(act):
        sp = V2["r_sp"]
        run = serial(act, act_seq)
        act.wait_ge(ru_e, 3)
        run(nc.scalar.activation(sp[:, 0, :], cols[:, COL["lam"]:COL["lam"] + RB], ACT.Abs))
        nc.scalar.activation(sp[:, 0, :], sp[:, 0, :], ACT.Exp, scale=-1.0).then_inc(ru_e, 1)
        for n in range(RB + 1):
            if n < RB:
                s = n % 2
                act.wait_ge(ru_g, n + 1)
                if n >= 2:
                    act.wait_ge(ru_o, n - 1)
                nc.scalar.activation(V2["r_i"][:, s, :], pm[2 * s][:, :], ACT.Sigmoid, bias=col("gx_b", n)).then_inc(ru_s, 1)
                nc.scalar.activation(V2["r_r"][:, s, :], pm[2 * s + 1][:, :], ACT.Sigmoid, bias=col("ga_b", n)).then_inc(ru_s, 1)
                act.wait_ge(ru_s, 2 * (n + 1))
                act.wait_ge(ru_sp, 1)
                nc.scalar.activation(V2["r_a"][:, s, :], V2["r_r"][:, s, :], ACT.Exp, scale=sp[:, 4, n:n + 1]).then_inc(ru_a, 1)
                nc.scalar.activation(V2["r_t"][:, s, :], V2["r_r"][:, s, :], ACT.Tanh, scale=sp[:, 5, n:n + 1]).then_inc(ru_a, 1)
            if n:
                act.wait_ge(ru_o, n)
                nc.scalar.activation(B["b_hi"][:, n - 1, :], V2["r_o"][:, (n - 1) % 2, :], ACT.Copy).then_inc(ru_hi, 1)
            if n < RB:
                act.wait_ge(ru_m, n + 1)
                nc.scalar.activation(V2["r_t"][:, s, :], V2["r_t"][:, s, :], ACT.Sqrt).then_inc(ru_q, 1)

    def lru_dve(dve):
        run = serial(dve, dve_seq)
        vec, sp = nc.vector, V2["r_sp"]
        for n in range(2):
            vec.memset(V2["r_x"][:, n, :CW - 1], 0.0).then_inc(ru_e, 1)
        vec.tensor_scalar(sp[:, 1, :], cols[:, COL["lam"]:COL["lam"] + RB], -1.0, 0.0, ALU.mult, ALU.max).then_inc(ru_e, 1)
        dve.wait_ge(ru_e, 4)
        run(vec.tensor_scalar(sp[:, 2, :], sp[:, 0, :], 2.0, None, ALU.add))
        run(vec.reciprocal(sp[:, 2, :], sp[:, 2, :]))
        run(vec.tensor_tensor(sp[:, 0, :], sp[:, 0, :], sp[:, 2, :], ALU.mult))
        run(vec.tensor_tensor(sp[:, 2, :], sp[:, 0, :], sp[:, 0, :], ALU.mult))
        run(vec.tensor_scalar(sp[:, 3, :], sp[:, 2, :], 1.0 / 17, 1.0 / 15, ALU.mult, ALU.add))
        for k in (13, 11, 9, 7, 5, 3, 1):
            run(vec.tensor_tensor(sp[:, 3, :], sp[:, 3, :], sp[:, 2, :], ALU.mult))
            run(vec.tensor_scalar(sp[:, 3, :], sp[:, 3, :], 1.0 / k, None, ALU.add))
        run(vec.tensor_tensor(sp[:, 3, :], sp[:, 3, :], sp[:, 0, :], ALU.mult))
        run(vec.scalar_tensor_tensor(out=sp[:, 3, :], in0=sp[:, 3, :], scalar=2.0, in1=sp[:, 1, :], op0=ALU.mult, op1=ALU.add))
        run(vec.tensor_scalar(sp[:, 5, :], sp[:, 3, :], LRU_C, None, ALU.mult))
        vec.tensor_scalar(sp[:, 4, :], sp[:, 3, :], -LRU_C, None, ALU.mult).then_inc(ru_sp, 1)
        for n in range(RB + 1):
            s = n % 2
            if n < RB:
                dve.wait_ge(ru_in[s], 32 * (n // 2 + 1))
                if n >= 2:
                    dve.wait_ge(ru_g, n - 1)
                    dve.wait_ge(ru_o, n - 1)
                x, y = V2["r_x"][:, s, :], V2["r_y"][:, s, :]
                tap = lambda i: col("conv_w", i * RB + n)
                run(vec.tensor_scalar(y, x[:, 0:L], tap(0), col("conv_b", n), ALU.mult, ALU.add))
                for i in range(1, CW):
                    ins = vec.scalar_tensor_tensor(out=y, in0=x[:, i:i + L], scalar=tap(i), in1=y, op0=ALU.mult, op1=ALU.add)
                    run(ins) if i < CW - 1 else ins.then_inc(ru_y, 1)
                dve.wait_ge(ru_y, n + 1)
            if n:
                m, o = n - 1, 1 - s
                a, t, g = V2["r_a"][:, o, :], V2["r_t"][:, o, :], V2["r_i"][:, o, :]
                dve.wait_ge(ru_a, 2 * n)
                run(vec.tensor_tensor(V2["r_m"][:, :], a, a, ALU.mult))
                vec.scalar_tensor_tensor(out=t, in0=V2["r_m"][:, :], scalar=1.0, in1=t, op0=ALU.add,
                                         op1=ALU.mult).then_inc(ru_m, 1)
                dve.wait_ge(ru_s, 2 * n)
                run(vec.tensor_tensor(g, g, V2["r_y"][:, o, :], ALU.mult))
                dve.wait_ge(ru_q, n)
                run(vec.tensor_tensor(g, g, t, ALU.mult))
                run(vec.tensor_tensor_scan(V2["r_h"][:, :], a, g, 0.0, ALU.mult, ALU.add))
                vec.tensor_tensor(V2["r_o"][:, m % 2, :], V2["r_h"][:, :], V2["r_gate"][:, o, :], ALU.mult).then_inc(ru_o, 1)
                dve.wait_ge(ru_hi, n)
                vec.tensor_tensor(B["b_lo"][:, m, :], V2["r_o"][:, m % 2, :], B["b_hi"][:, m, :].bitcast(F32),
                                  ALU.subtract).then_inc(ru_lo, 1)

    V3 = overlay(0, [
        ("w_p", [4, 2 * P], F32), ("w_pt", [2, 2 * P], F32), ("w_o", [2, L], F32), ("w_q", [2, 2, L], F32),
        ("w_gate", [2, L], F32), ("w_k", [WKV, L], F32), ("w_v", [NTOK, WKV * WD], F32), ("w_small", [16], F32)])

    def swa_pre_pool(pool):
        pool.dma_start(V3["w_k"][:WD, :, :], zt[ZT["wkv"]:ZT["wkv"] + WKV * WD, :].rearrange("(n d) t -> d n t", d=WD)).then_inc(shared_in, 16)
        pool.dma_start(V3["w_v"][:, :, :], zn[:, ZN["wv"]:ZN["wv"] + WKV * WD].rearrange("(b p) c -> p b c", p=P)).then_inc(shared_in, 16)

    def swa_loads(t):
        s = t % 2
        return [(V3["w_q"][:WD, s, :, :], zt[ZT["wq"] + t * P:ZT["wq"] + (t + 1) * P, :].rearrange("(h d) t -> d h t", d=WD))]

    def swa_kv(t, h):
        return (2 * t + h) // (WH // WKV)

    SWA = Attention(
        buf=dict(p=V3["w_p"], pt=V3["w_pt"], o=V3["w_o"], small=V3["w_small"]), tiles=WH // 2, heads=2, comps=1, dv=WD,
        scale=WD ** -0.5, key_tiles=lambda qb: (max(qb - 1, 0), min(qb, 1) + 1),
        products=lambda t, h, c, qb, first, count: [(V3["w_q"][:WD, t % 2, h, qb * P:(qb + 1) * P],
                                                     V3["w_k"][:WD, swa_kv(t, h), first * P:(first + count) * P])],
        bias=lambda t, qb, count: band[:, (2 - count) * P:], bias_ready=None, pool_work=None,
        value=lambda t, h, b: V3["w_v"][:, b, swa_kv(t, h) * WD:(swa_kv(t, h) + 1) * WD],
        gate=lambda t: V3["w_gate"][:, t % 2, :], kt0=KT // 2, loads=(swa_loads, 16), gate_of=head_rows("wgate"), hi=B["b_hi"], lo=B["b_lo"],
        units0=32, jobs0=32, tiles0=8, in0=256,
        sink=lambda t, h: col("sinks", 2 * t + h), lam=None, gain=None)

    M = overlay(0, [("latent", [10, L], F32), ("l_sq", [2, L], F32), ("l_n", [2, L], F32), ("l_rs", [2, L], F32),
                    ("lq_hi", [6, L], F32R), ("lq_lo", [6, L], F32R)])
    MK = overlay(HALF, [("lk_hi", [4, L], F32R), ("lk_lo", [4, L], F32R)])
    lt_sq, lt_ss, lt_sd, lt_n, lt_hi, lt_lo = (sem(f"latent_{n}") for n in ("squares", "sum", "deviation", "normed", "hi", "lo"))
    LATENTS = [(0, 6, MQR, "q_norm"), (6, 4, MKVR, "kv_norm")]

    def latent_part(part, g):
        return M["lq_" + part][:, g, :] if g < 6 else MK["lk_" + part][:, g - 6, :]

    def latent_pe(pe):
        for j, (first, n, _, _) in enumerate(LATENTS):
            for g in range(first, first + n):
                pe.wait_ge(lt_sq, g + 1)
                nc.tensor.matmul(pm[j][:, :], ones[:, :], M["l_sq"][:, g % 2, :], start=(g == first),
                                 stop=(g == first + n - 1)).then_inc(lt_ss, 1)

    def latent_act(act):
        for j, (first, n, width, _) in enumerate(LATENTS):
            for g in range(first, first + n):
                if g >= 2:
                    act.wait_ge(lt_ss, g - 1)
                nc.scalar.activation(M["l_sq"][:, g % 2, :], M["latent"][:, g, :], ACT.Square).then_inc(lt_sq, 1)
            act.wait_ge(lt_ss, first + n)
            nc.scalar.activation(M["l_rs"][:, j, :], pm[j][:, :], ACT.Sqrt, scale=1.0 / width,
                                 bias=eps[:, 0:1]).then_inc(lt_sd, 1)
        for g in range(10):
            act.wait_ge(lt_n, g + 1)
            nc.scalar.activation(latent_part("hi", g), M["l_n"][:, g % 2, :], ACT.Copy).then_inc(lt_hi, 1)

    def latent_dve(dve):
        run = serial(dve, dve_seq)
        for j, (first, n, _, gain) in enumerate(LATENTS):
            dve.wait_ge(lt_sd, j + 1)
            run(nc.vector.reciprocal(M["l_rs"][:, j, :], M["l_rs"][:, j, :]))
            for g in range(first, first + n):
                if g >= 2:
                    dve.wait_ge(lt_lo, g - 1)
                nc.vector.scalar_tensor_tensor(out=M["l_n"][:, g % 2, :], in0=M["latent"][:, g, :],
                                               scalar=col(gain, g - first), in1=M["l_rs"][:, j, :], op0=ALU.mult,
                                               op1=ALU.mult).then_inc(lt_n, 1)
                dve.wait_ge(lt_hi, g + 1)
                nc.vector.tensor_tensor(latent_part("lo", g), M["l_n"][:, g % 2, :], latent_part("hi", g).bitcast(F32),
                                        ALU.subtract).then_inc(lt_lo, 1)

    V4 = overlay(0, [
        ("m_p", [4, L], F32), ("m_pt", [2, L], F32), ("m_o", [2, L], F32), ("m_q", [2, L], F32), ("m_k", [2, L], F32),
        ("m_v", [2, NTOK, P], F32), ("m_gate", [2, L], F32), ("m_sq", [L], F32), ("m_small", [16], F32),
        ("m_qr", [4, L], F32), ("m_qs", [4, L], F32), ("m_kr", [L], F32), ("m_ks", [L], F32), ("m_cs", [2, L], F32),
        ("m_lam", [4, DQK], F32), ("m_l", [8], F32)])
    rope_done, lam_sums, lam_exp = sem("rope_done"), sem("lambda_sums"), sem("lambda_exp")

    def rope_pool(pool):
        qr = zt[ZT["qr"]:ZT["qr"] + MH * MROPE, :].rearrange("(j r) t -> r j t", r=P)
        kr = zt[ZT["kr"]:ZT["kr"] + MROPE, :]
        H2 = MROPE // 2
        pool.dma_start(V4["m_cs"][:, :, :], inp["rope"].rearrange("p (a t) -> p a t", a=2)).then_inc(shared_in, 16)
        pool.dma_start(V4["m_qr"][:, :, :], qr).then_inc(shared_in, 16)
        for h in range(2):
            pool.dma_start(V4["m_kr"][h * MROPE:(h + 1) * MROPE, :], kr).then_inc(shared_in, 16)
            for half in range(2):
                to, of = h * MROPE + half * H2, h * MROPE + (1 - half) * H2
                pool.dma_start(V4["m_qs"][to:to + H2, :, :], qr[of:of + H2]).then_inc(shared_in, 16)
                pool.dma_start(V4["m_ks"][to:to + H2, :], kr[(1 - half) * H2:(2 - half) * H2, :]).then_inc(shared_in, 16)
        for n, name in enumerate(("l1_lambda_q1_2", "l1_lambda_k1_2", "l1_lambda_q2_2", "l1_lambda_k2_2")):
            pool.dma_start(V4["m_lam"][:, n, :], inp[name].rearrange("(a d) -> a d", a=1).broadcast_to([P, DQK])).then_inc(shared_in, 16)

    def rope_dve(dve):
        run = serial(dve, dve_seq)
        vec = nc.vector
        dve.wait_ge(shared_in, 112 + 16 * 16)
        cos, sin = V4["m_cs"][:, 0:1, :], V4["m_cs"][:, 1:2, :]
        lam, l = V4["m_lam"], V4["m_l"]
        for n in range(2):
            run(vec.tensor_tensor_reduce(out=lam[:, 2 * n, :], in0=lam[:, 2 * n, :], in1=lam[:, 2 * n + 1, :], scale=1.0,
                                         scalar=0.0, op0=ALU.mult, op1=ALU.add, accum_out=l[:, n:n + 1]))
        vec.tensor_scalar(l[:, 4:5], col("subln"), 1.0 - LAMBDA_INIT, None, ALU.mult).then_inc(lam_sums, 1)
        for x, y, n in ((V4["m_qr"][:, :, :], V4["m_qs"][:, :, :], 4), (V4["m_kr"][:, :], V4["m_ks"][:, :], 0)):
            c, s = (cos.broadcast_to([P, n, L]), sin.broadcast_to([P, n, L])) if n else (cos[:, 0, :], sin[:, 0, :])
            run(vec.tensor_tensor(x, x, c, ALU.mult))
            run(vec.tensor_tensor(y, y, s, ALU.mult))
            run(vec.tensor_tensor(x, x, y, ALU.add))
        dve.wait_ge(lam_exp, 1)
        run(vec.tensor_tensor(l[:, 5:6], l[:, 3:4], l[:, 2:3], ALU.subtract))
        vec.tensor_scalar(l[:, 6:7], l[:, 5:6], -LAMBDA_INIT, None, ALU.add).then_inc(rope_done, 1)
        dve.wait_ge(rope_done, 1)

    def rope_act(act):
        act.wait_ge(lam_sums, 1)
        nc.scalar.activation(V4["m_l"][:, 2:4], V4["m_l"][:, 0:2], ACT.Exp).then_inc(lam_exp, 1)

    def mla_loads(t):
        s = t % 2
        rows = lambda name: zt[ZT[name] + t * P:ZT[name] + (t + 1) * P, :]
        return [(V4["m_q"][:, s, :], rows("qn")), (V4["m_k"][:, s, :], rows("kn")),
                (V4["m_v"][:, s, :, :], zn[:, ZN["mv"] + t * P:ZN["mv"] + (t + 1) * P].rearrange("(b p) c -> p b c", p=P))]

    def diff_loads(t):
        s = t % 2
        rows = lambda name: zt[ZT[name] + t * P:ZT[name] + (t + 1) * P, :]
        return [(V4["m_q"][:, s, :], rows("dq")), (V4["m_k"][:, s, :], rows("dk")),
                (V4["m_v"][:, s, :, :], zn[:, ZN["dv"] + t * P:ZN["dv"] + (t + 1) * P].rearrange("(b p) c -> p b c", p=P))]

    def half(t):
        return slice(64 * (t % 2), 64 * (t % 2) + 64)

    buf4 = dict(p=V4["m_p"], pt=V4["m_pt"], o=V4["m_o"], small=V4["m_small"], sq=V4["m_sq"])
    causal_bias = lambda t, qb, count: wide[:, (NTOK - count) * P:]
    MLA = Attention(
        buf=buf4, tiles=MH, heads=1, comps=1, dv=P, scale=(MNOPE + MROPE) ** -0.5, key_tiles=lambda qb: (0, qb + 1),
        products=lambda t, h, c, qb, first, count: [
            (V4["m_q"][:, t % 2, qb * P:(qb + 1) * P], V4["m_k"][:, t % 2, :count * P]),
            (V4["m_qr"][half(t), t // 2, qb * P:(qb + 1) * P], V4["m_kr"][half(t), :count * P])],
        bias=causal_bias, bias_ready=None, pool_work=None, value=lambda t, h, b: V4["m_v"][:, t % 2, b, :],
        gate=lambda t: V4["m_gate"][:, t % 2, :], kt0=0, loads=(mla_loads, 48), gate_of=head_rows("mgate"), hi=B["b_hi"], lo=B["b_lo"],
        units0=96, jobs0=96, tiles0=16, in0=320, sink=None, lam=None, gain=None)
    DIFF = Attention(
        buf=buf4, tiles=DH, heads=1, comps=2, dv=P, scale=DQK ** -0.5, key_tiles=lambda qb: (0, qb + 1),
        products=lambda t, h, c, qb, first, count: [(V4["m_q"][half(c), t % 2, qb * P:(qb + 1) * P],
                                                     V4["m_k"][half(c), t % 2, :count * P])],
        bias=causal_bias, bias_ready=None, pool_work=None, value=lambda t, h, b: V4["m_v"][:, t % 2, b, :],
        gate=lambda t: V4["m_gate"][:, t % 2, :], kt0=KT // 2, loads=(diff_loads, 48), gate_of=head_rows("dgate"), hi=B["b_hi"], lo=B["b_lo"],
        units0=128, jobs0=128, tiles0=24, in0=512, sink=None, lam=V4["m_l"][:, 6:7], gain=V4["m_l"][:, 4:5])

    s5_ug = sem("s5_u_by_group")
    s5_tmp2, s5_cc = sem("s5_scans"), sem("s5_c_copied")
    BARRIERS_BEFORE_S5 = 4
    NPAIR = SG // 2
    NG = 2 * SPAIR
    CH = NG * SC
    E9 = ST + 1
    V5 = overlay(HALF, [
        ("s_b", [2, SPAIR, SC], F32), ("s_B", [2, SPAIR, SC], F32), ("s_BP", [2, SPAIR, 2, SC], F32), ("s_cn", [4, P], F32), ("s_c", [2, SPAIR, SC], F32),
        ("s_C", [2, SPAIR, E9, SC], F32), ("s_t", [2, SPAIR, E9, SC], F32), ("s_L", [2, SPAIR, ST, SC], F32),
        ("s_u", [ST, CH], F32)])
    V6 = overlay(0, [
        ("s_pw", [2, E9, NPAIR], F32), ("s_small", [12, NPAIR], F32), ("s_ang", [2, E9, NPAIR], F32), ("s_nat", [3, P], F32),
        ("s_ls", [2], F32), ("s_kv", [SK], F32), ("s_BT", [2, SPAIR, P], F32), ("s_UT", [NG, SK], F32), ("s_K", [SPAIR, P], F32),
        ("s_MG", [NG, P], F32)])
    V7 = overlay(0 + 40 * 1024, [
        ("s_cs", [2, SPAIR, SK], F32), ("s_w", [2, SPAIR, SK], F32), ("s_x", [2, SPAIR, 2, SK], F32), ("s_z", [2, L], F32)])
    V8 = overlay(HALF + 41 * 1024, [("s_y", [ST, SPAIR * SC], F32), ("s_w2", [2, SPAIR, SK], F32), ("s_r", [SPAIR, SK], F32), ("s_ug", [NG, ST * SC], F32)])
    s5_nat, s5_ex, s5_tp, s5_th, s5_sc, s5_pre = (sem(f"s5_{n}") for n in (
        "parameters_in", "step_spread", "parameters_turned", "angles", "sines", "powers"))
    (s5_in, s5_ct, s5_ut, s5_bt, s5_kk, s5_v, s5_y, s5_yt, s5_bl, s5_c, s5_k, s5_xp, s5_ute, s5_bte, s5_ke, s5_ye, s5_ang,
     s5_cs, s5_mg, s5_ze, s5_zs) = (sem(f"s5_{n}") for n in (
        "slice_in", "c_turned", "u_turned", "b_turned", "kernels", "inputs_to_states", "y", "y_turned", "b_powers", "c_powers",
        "kernels_with_d", "states", "u_turned_copied", "b_turned_copied", "kernels_copied", "y_copied", "phase", "phase_sines",
        "kernels_spread", "z", "z_stored"))
    S_LR, S_LI, S_ST, S_TH, S_RR, S_DEN, S_NR, S_CR, S_CI, S_T1, S_T2, S_R8 = range(12)
    TWO_PI = 6.283185307179586
    C1 = 6.28125
    C2 = 0.0019350051879882812
    C3 = TWO_PI - C1 - C2
    MAGIC = 12582912.0
    PI_F = 3.1415925

    def reduce_angle(run, ang, n):
        vec = nc.vector
        run(vec.tensor_scalar(n, ang, 1.0 / TWO_PI, MAGIC, ALU.mult, ALU.add))
        run(vec.tensor_scalar(n, n, -MAGIC, None, ALU.add))
        for c in (C1, C2, C3):
            run(vec.scalar_tensor_tensor(out=ang, in0=n, scalar=-c, in1=ang, op0=ALU.mult, op1=ALU.add))
        run(vec.tensor_scalar(ang, ang, PI_F, -PI_F, ALU.min, ALU.max))

    spare = stage[:2 * SC, :, :].rearrange("p m c -> p (m c)")
    d_diag = spare[:, :NPAIR * SC].rearrange("p (j c) -> p j c", c=SC)
    same_c = spare[:, NPAIR * SC:NPAIR * SC + SC]

    def s5_pre_pool(pool):
        for n, name in enumerate(("s5_lambda_re", "s5_lambda_im")):
            pool.dma_start(V6["s_nat"][:NPAIR, n, :], inp[name][0].rearrange("(j g) p -> j (g p)", g=2)).then_inc(s5_nat, 16)
        pool.dma_start(V6["s_ls"][:NPAIR, :], inp["s5_log_step"][0].rearrange("(j g) -> j g", g=2)).then_inc(s5_nat, 16)
        pool.dma_start(V6["s_kv"][:, :], inp["steps"][:, :]).then_inc(s5_nat, 16)
        for g in range(2):
            d = inp["s5_d"].rearrange("a (j g c) -> a g j c", g=2, c=SC)[:, g]
            pool.dma_start(d_diag[g * SC:(g + 1) * SC], d.broadcast_to([SC, NPAIR, SC])).then_inc(s5_nat, 16)

    def s5_pre_pe(pe):
        pe.wait_ge(s5_ex, 1)
        for n in range(3):
            ins = nc.tensor.transpose(pm[0][:, n * NPAIR:(n + 1) * NPAIR], V6["s_nat"][:NPAIR, n, :], ident[:NPAIR, :NPAIR])
        ins.then_inc(s5_tp, 1)

    def s5_pre_dve(dve):
        run = serial(dve, dve_seq)
        vec = nc.vector
        s = lambda n: V6["s_small"][:, n, :]
        dve.wait_ge(s5_nat, 96)
        vec.tensor_copy(V6["s_nat"][:NPAIR, 2, :].rearrange("j (g p) -> j g p", g=2),
                        V6["s_ls"][:NPAIR, :].unsqueeze(2).broadcast_to([NPAIR, 2, P // 2])).then_inc(s5_ex, 1)
        run(vec.memset(V6["s_MG"][:, :, :], 0.0))
        run(vec.memset(V7["s_x"][:, :, :, :, :], 0.0))
        run(vec.memset(V5["s_BP"][:, :, :, :, :], 0.0))
        run(vec.memset(V8["s_r"][:, :, 0:1], 0.0))
        run(vec.tensor_tensor(same_c, ident[:2 * SC, :SC], ident[:2 * SC, SC:2 * SC], ALU.add))
        run(vec.tensor_tensor(d_diag, d_diag, same_c.unsqueeze(1).broadcast_to([2 * SC, NPAIR, SC]), ALU.mult))
        dve.wait_ge(s5_tp, 1)
        run(vec.tensor_copy(V6["s_small"][:, S_LR:S_ST + 1, :], pm[0][:, :3 * NPAIR].rearrange("p (n j) -> p n j", n=3)))
        vec.tensor_scalar(s(S_LR), s(S_LR), -1e-4, None, ALU.min).then_inc(s5_th, 1)
        dve.wait_ge(s5_sc, 1)
        run(vec.tensor_tensor(s(S_TH), s(S_LI), s(S_ST), ALU.mult))
        run(vec.tensor_tensor(s(S_RR), s(S_LR), s(S_ST), ALU.mult))
        reduce_angle(run, s(S_TH), s(S_T1))
        for e in range(E9):
            run(vec.tensor_scalar(V6["s_ang"][:, 0, e, :], s(S_TH), float(e), None, ALU.mult))
        reduce_angle(run, V6["s_ang"][:, 0, :, :], V6["s_ang"][:, 1, :, :])
        run(vec.tensor_copy(s(S_TH), V6["s_ang"][:, 0, ST, :]))
        vec.tensor_tensor(s(S_DEN), s(S_LR), s(S_LR), ALU.mult).then_inc(s5_th, 1)
        dve.wait_ge(s5_sc, 2)
        for c in range(2):
            run(vec.tensor_tensor(V6["s_pw"][:, c, :, :], V6["s_pw"][:, c, :, :], V6["s_ang"][:, 1, :, :], ALU.mult))
        run(vec.tensor_copy(s(S_R8), V6["s_ang"][:, 1, ST, :]))
        for i in range(ST):
            run(vec.tensor_copy(V6["s_ang"][:, :, i, :], V6["s_pw"][:, :, ST - 1 - i, :]))
        run(vec.tensor_tensor(s(S_T1), s(S_LI), s(S_LI), ALU.mult))
        run(vec.tensor_tensor(s(S_DEN), s(S_DEN), s(S_T1), ALU.add))
        run(vec.reciprocal(s(S_DEN), s(S_DEN)))
        run(vec.tensor_scalar(s(S_NR), V6["s_pw"][:, 0, 1, :], -1.0, None, ALU.add))
        ni = V6["s_pw"][:, 1, 1, :]
        for out_, a, b, op in ((S_CR, (S_NR, S_LR), (None, S_LI), ALU.add), (S_CI, (None, S_LR), (S_NR, S_LI), ALU.subtract)):
            run(vec.tensor_tensor(s(S_T1), s(a[0]) if a[0] is not None else ni, s(a[1]), ALU.mult))
            run(vec.tensor_tensor(s(S_T2), s(b[0]) if b[0] is not None else ni, s(b[1]), ALU.mult))
            run(vec.tensor_tensor(s(S_T1), s(S_T1), s(S_T2), op))
            run(vec.tensor_tensor(s(out_), s(S_T1), s(S_DEN), ALU.mult))

    def s5_pre_act(act):
        run = serial(act, act_seq)
        s = lambda n: V6["s_small"][:, n, :]
        act.wait_ge(s5_th, 1)
        nc.scalar.activation(s(S_ST), s(S_ST), ACT.Exp).then_inc(s5_sc, 1)
        act.wait_ge(s5_th, 2)
        run(nc.scalar.activation(V6["s_pw"][:, 1, :, :], V6["s_ang"][:, 0, :, :], ACT.Sin))
        run(nc.scalar.activation(V6["s_ang"][:, 0, :, :], V6["s_ang"][:, 0, :, :], ACT.Abs))
        run(nc.scalar.activation(V6["s_pw"][:, 0, :, :], V6["s_ang"][:, 0, :, :], ACT.Sin, scale=-1.0, bias=halfpi[:, 0:1]))
        for e in range(E9):
            ins = nc.scalar.activation(V6["s_ang"][:, 1, e, :], s(S_RR), ACT.Exp, scale=float(e))
            run(ins) if e < ST else ins.then_inc(s5_sc, 1)

    def s5_sp(sp):
        sp.wait_ge(bar, 4 * BARRIERS_BEFORE_S5)
        for sl in range(SSL + 1):
            if sl < SSL:
                g0 = sl * NG
                if sl:
                    sp.wait_ge(s5_ug, sl)
                    sp.wait_ge(s5_bl, sl)
                    sp.wait_ge(s5_ct, sl)
                for n, name in enumerate(("s5_b_re", "s5_b_im")):
                    src = inp[name][0, g0:g0 + NG].rearrange("(j g) p c -> g p j c", g=2)
                    for g in range(2):
                        sp.dma_start(V5["s_b"][g * SP_:(g + 1) * SP_, n, :, :], src[g]).then_inc(s5_in, 16)
                sp.dma_start(V5["s_u"][:SK, :, :], zn[:, ZN["u"] + sl * CH:ZN["u"] + (sl + 1) * CH].rearrange(
                    "(k t) c -> k t c", t=ST)).then_inc(s5_in, 16)
                for n, name in enumerate(("s5_c_re", "s5_c_im")):
                    for r in range(2):
                        src = inp[name][0, g0 + 8 * r:g0 + 8 * r + 8].rearrange("g c p -> (g c) p")
                        for twice in range(2):
                            sp.dma_start(V5["s_cn"][:, 2 * n + r, twice * SP_:(twice + 1) * SP_], src).then_inc(s5_in, 16)
            if sl:
                sp.wait_ge(s5_k, sl)
                if sl > 1:
                    sp.wait_ge(s5_y, sl - 1)
                by_g = V6["s_MG"][:, :, :].rearrange("p (j g) x -> p g j x", g=2)
                for i in range(ST):
                    for g in range(2):
                        sp.dma_start(by_g[i * SC:(i + 1) * SC, g, :, i * SC:],
                                     V6["s_K"][g * SC:(g + 1) * SC, :, :P - i * SC]).then_inc(s5_mg, 16)
        sp.wait_ge(s5_mg, MG_ALL * SSL)

    def s5_pool(pool):
        for sl in range(SSL):
            pool.wait_ge(s5_ke, sl + 1)
            nc.gpsimd.tensor_tensor(V6["s_K"][:2 * SC, :, :SC], V6["s_K"][:2 * SC, :, :SC],
                                    d_diag[:, sl * SPAIR:(sl + 1) * SPAIR, :], ALU.add).then_inc(s5_k, 1)
            pool.wait_ge(s5_ze, 2 * sl + 2)
            rows_of = zt[ZT["z"] + sl * CH:ZT["z"] + (sl + 1) * CH, :].rearrange("(j g c) t -> g j c t", g=2, c=SC)
            for g in range(2):
                pool.dma_start(rows_of[g], V7["s_z"][:, g, :]).then_inc(s5_zs, 16)
        pool.wait_ge(s5_zs, 16 * 2 * SSL)

    LOADS = 13

    MG_ALL = 16 * 2 * ST

    def s5_pe(pe):
        def turn_c(sl):
            pe.wait_ge(s5_in, 16 * LOADS * (sl + 1))
            if sl > 1:
                pe.wait_ge(s5_ze, 2 * (sl - 1))
            for n in range(2):
                for r in range(2):
                    ins = nc.tensor.transpose(pg[2][:, (2 * n + r) * P:(2 * n + r + 1) * P], V5["s_cn"][:, 2 * n + r, :], ident[:, :])
            ins.then_inc(s5_ct, 1)

        def turn_u(sl):
            pe.wait_ge(s5_ug, sl + 1)
            if sl:
                pe.wait_ge(s5_xp, sl)
            for g in range(NG):
                ins = nc.tensor.transpose(pg[g // 8][:, g % 8 * SK:(g % 8 + 1) * SK], V8["s_ug"][:SK, g, :],
                                          ident[:SK, :SK])
            ins.then_inc(s5_ut, 1)

        turn_c(0)
        turn_u(0)
        pe.wait_ge(s5_th, 1)
        for sl in range(SSL):
            pe.wait_ge(s5_bl, sl + 1)
            for n in range(2):
                for j in range(SPAIR):
                    ins = nc.tensor.transpose(pm[2 * n + j // 4][:, j % 4 * P:(j % 4 + 1) * P],
                                              V5["s_L"][:, n, j, :, :], ident[:, :])
            ins.then_inc(s5_bt, 1)
            pe.wait_ge(s5_bte, sl + 1)
            pe.wait_ge(s5_ute, sl + 1)
            for n in range(2):
                for g in range(NG):
                    rows = slice(g % 2 * SP_, (g % 2 + 1) * SP_)
                    ins = nc.tensor.matmul(pg[n][rows, g // 2 * SK:(g // 2 + 1) * SK], V6["s_BT"][:, n, g // 2, rows],
                                           V6["s_UT"][:, g, :], start=True, stop=True)
            ins.then_inc(s5_v, 1)
            pe.wait_ge(s5_c, sl + 1)
            for j in range(SPAIR):
                for n in range(2):
                    ins = nc.tensor.matmul(pm[j // 4][:2 * SC, j % 4 * P:(j % 4 + 1) * P],
                                           V5["s_BP"][:, n, j, :, :].rearrange("p g c -> p (g c)"),
                                           V5["s_C"][:, n, j, :ST, :], start=(n == 0), stop=(n == 1))
            ins.then_inc(s5_kk, 1)
            if sl + 1 < SSL:
                turn_c(sl + 1)
            y_of = lambda j: pm[2 + j // 4][:, j % 4 * P:(j % 4 + 1) * P]
            pe.wait_ge(s5_mg, MG_ALL * (sl + 1))
            pe.wait_ge(s5_xp, sl + 1)
            for j in range(SPAIR):
                for n in range(2):
                    nc.tensor.matmul(y_of(j), V7["s_x"][:, n, j, :, :].rearrange("p g k -> p (g k)"),
                                     V5["s_C"][:, n, j, 1:, :], start=(n == 0), stop=False)
                for g in range(2):
                    ins = nc.tensor.matmul(y_of(j)[g * SK:(g + 1) * SK, :], V6["s_UT"][:, 2 * j + g, :], V6["s_MG"][:, 2 * j + g, :],
                                           start=False, stop=True)
            ins.then_inc(s5_y, 1)
            if sl + 1 < SSL:
                turn_u(sl + 1)
                pe.wait_ge(s5_cc, sl + 2)
            pe.wait_ge(s5_ye, sl + 1)
            for i in range(ST):
                ins = nc.tensor.transpose(pg[2 + i // 4][:, i % 4 * P:(i % 4 + 1) * P], V8["s_y"][:, i, :], ident[:, :])
                if i % 4 == 3:
                    ins.then_inc(s5_yt, 1)

    def s5_act(act):
        run = serial(act, act_seq)

        def u_by_group(sl):
            act.wait_ge(s5_in, 16 * LOADS * (sl + 1))
            if sl:
                act.wait_ge(s5_ut, sl)
            nc.scalar.activation(V8["s_ug"][:SK, :, :].rearrange("k g (t c) -> k g t c", c=SC),
                                 V5["s_u"][:SK, :, :].rearrange("k t (g c) -> k g t c", c=SC), ACT.Copy).then_inc(s5_ug, 1)

        u_by_group(0)
        for sl in range(SSL):
            act.wait_ge(s5_ut, sl + 1)
            for h in range(2):
                ins = nc.scalar.activation(V6["s_UT"][:, 8 * h:8 * h + 8, :], pg[h][:, :], ACT.Copy)
                run(ins) if h == 0 else ins.then_inc(s5_ute, 1)
            act.wait_ge(s5_bt, sl + 1)
            for n in range(4):
                ins = nc.scalar.activation(V6["s_BT"][:, n // 2, n % 2 * 4:n % 2 * 4 + 4, :], pm[n][:, :], ACT.Copy)
                run(ins)
            for g in range(2):
                rows = slice(g * SP_, (g + 1) * SP_)
                ins = nc.scalar.activation(V5["s_BP"][rows, :, :, g, :], V5["s_B"][rows, :, :, :], ACT.Copy)
                run(ins) if g == 0 else ins.then_inc(s5_bte, 1)
            act.wait_ge(s5_ang, sl + 1)
            run(nc.scalar.activation(V7["s_cs"][:, 1, :, :], V8["s_w2"][:, 0, :, :], ACT.Sin))
            run(nc.scalar.activation(V8["s_w2"][:, 0, :, :], V8["s_w2"][:, 0, :, :], ACT.Abs))
            nc.scalar.activation(V7["s_cs"][:, 0, :, :], V8["s_w2"][:, 0, :, :], ACT.Sin, scale=-1.0,
                                 bias=halfpi[:, 0:1]).then_inc(s5_cs, 1)
            act.wait_ge(s5_kk, sl + 1)
            if sl:
                act.wait_ge(s5_mg, MG_ALL * sl)
            for h in range(2):
                ins = nc.scalar.activation(V6["s_K"][:2 * SC, 4 * h:4 * h + 4, :], pm[h][:2 * SC, :], ACT.Copy)
                run(ins) if h == 0 else ins.then_inc(s5_ke, 1)
            if sl + 1 < SSL:
                u_by_group(sl + 1)
            act.wait_ge(s5_y, sl + 1)
            if sl:
                act.wait_ge(s5_yt, 2 * sl)
            for h in range(2):
                ins = nc.scalar.activation(
                    V8["s_y"][:, :, :].rearrange("p t (j c) -> p j t c", c=SC)[:, 4 * h:4 * h + 4],
                    pm[2 + h][:, :].rearrange("p (j t c) -> p j t c", j=4, t=ST), ACT.Copy)
                run(ins) if h == 0 else ins.then_inc(s5_ye, 1)
            if sl:
                act.wait_ge(s5_zs, 32 * sl)
            for h in range(2):
                act.wait_ge(s5_yt, 2 * sl + h + 1)
                nc.scalar.activation(V7["s_z"][:, :, :].rearrange("p g (k t) -> p t g k", t=ST)[:, 4 * h:4 * h + 4],
                                     pg[2 + h][:, :].rearrange("p (t g k) -> p t g k", t=4, g=2),
                                     ACT.Gelu_apprx_tanh).then_inc(s5_ze, 1)

    def s5_dve(dve):
        run = serial(dve, dve_seq)
        vec = nc.vector
        tt = vec.tensor_tensor
        for sl in range(SSL):
            js = slice(sl * SPAIR, (sl + 1) * SPAIR)
            over_c = lambda n: V6["s_small"][:, n, js].unsqueeze(2).broadcast_to([P, SPAIR, SC])
            t = V5["s_t"]
            dve.wait_ge(s5_ct, sl + 1)
            for n in range(2):
                for g in range(2):
                    rows = slice(g * SP_, (g + 1) * SP_)
                    ins = vec.tensor_copy(V5["s_c"][rows, n, :, :],
                                        pg[2][rows, 2 * n * P:2 * (n + 1) * P].rearrange("p (j g c) -> p j g c", g=2, c=SC)[:, :, g, :])
                    run(ins) if n + g < 2 else ins.then_inc(s5_cc, 1)
            dve.wait_ge(s5_in, 16 * LOADS * (sl + 1))
            if sl:
                dve.wait_ge(s5_kk, sl)
            for n in range(2):
                run(tt(t[:, 0, :, 0, :], V5["s_b"][:, n, :, :], over_c(S_CR), ALU.mult))
                run(tt(t[:, 1, :, 0, :], V5["s_b"][:, 1 - n, :, :], over_c(S_CI), ALU.mult))
                run(tt(V5["s_B"][:, n, :, :], t[:, 0, :, 0, :], t[:, 1, :, 0, :], ALU.subtract if n == 0 else ALU.add))
            power = lambda table, c, n: V6[table][:, c, :n, js].rearrange("p e j -> p j e").unsqueeze(3).broadcast_to([P, SPAIR, n, SC])
            for n in range(2):
                b3 = lambda x: V5["s_B"][:, x, :, :].unsqueeze(2).broadcast_to([P, SPAIR, ST, SC])
                run(tt(t[:, 0, :, :ST, :], b3(n), power("s_ang", 0, ST), ALU.mult))
                run(tt(t[:, 1, :, :ST, :], b3(1 - n), power("s_ang", 1, ST), ALU.mult))
                ins = tt(V5["s_L"][:, n, :, :, :], t[:, 0, :, :ST, :], t[:, 1, :, :ST, :], ALU.subtract if n == 0 else ALU.add)
                run(ins) if n == 0 else ins.then_inc(s5_bl, 1)
            ang, n_ = V8["s_w2"][:, 0, :, :], V8["s_w2"][:, 1, :, :]
            run(tt(ang, V6["s_small"][:, S_TH, js].unsqueeze(2).broadcast_to([P, SPAIR, SK]),
                   V6["s_kv"][:, :].unsqueeze(1).broadcast_to([P, SPAIR, SK]), ALU.mult))
            reduce_angle(run, ang, n_)
            vec.tensor_copy(V8["s_r"][:, :, 1:], V6["s_small"][:, S_R8, js].unsqueeze(2).broadcast_to([P, SPAIR, SK - 1])).then_inc(s5_ang, 1)
            dve.wait_ge(s5_bl, sl + 1)
            dve.wait_ge(s5_cc, sl + 1)
            if sl:
                dve.wait_ge(s5_y, sl)
            for n in range(2):
                c3 = lambda x: V5["s_c"][:, x, :, :].unsqueeze(2).broadcast_to([P, SPAIR, E9, SC])
                run(tt(t[:, 0, :, :, :], c3(n), power("s_pw", 0, E9), ALU.mult))
                run(tt(t[:, 1, :, :, :], c3(1 - n), power("s_pw", 1, E9), ALU.mult))
                if n == 0:
                    run(tt(V5["s_C"][:, 0, :, :, :], t[:, 0, :, :, :], t[:, 1, :, :, :], ALU.subtract))
                else:
                    vec.scalar_tensor_tensor(out=V5["s_C"][:, 1, :, :, :], in0=t[:, 0, :, :, :], scalar=-1.0,
                                             in1=t[:, 1, :, :, :], op0=ALU.mult, op1=ALU.subtract).then_inc(s5_c, 1)
            dve.wait_ge(s5_v, sl + 1)
            dve.wait_ge(s5_cs, sl + 1)
            cs, w, w2, x = V7["s_cs"], V7["s_w"], V8["s_w2"], V7["s_x"]
            v = lambda n: pg[n][:, :].rearrange("p (j k) -> p j k", j=SPAIR)
            for n in range(2):
                run(tt(w[:, n, :, :], v(n), cs[:, 0, :, :], ALU.mult))
                run(tt(w2[:, n, :, :], v(1 - n), cs[:, 1, :, :], ALU.mult))
                run(tt(w[:, n, :, :], w[:, n, :, :], w2[:, n, :, :], ALU.add if n == 0 else ALU.subtract))
            row = lambda x: x.rearrange("p j k -> p (j k)")
            for n in range(2):
                vec.tensor_tensor_scan(row(w2[:, n, :, :]), row(V8["s_r"][:, :, :]), row(w[:, n, :, :]), 0.0, ALU.mult,
                                       ALU.add).then_inc(s5_tmp2, 1)
            dve.wait_ge(s5_tmp2, (sl + 1) * 2)
            m = SK - 1
            for n in range(2):
                run(tt(w[:, 0, :, :m], w2[:, n, :, :m], cs[:, 0, :, :m], ALU.mult))
                run(tt(w[:, 1, :, :m], w2[:, 1 - n, :, :m], cs[:, 1, :, :m], ALU.mult))
                for g in range(2):
                    rows = slice(g * SP_, (g + 1) * SP_)
                    ins = tt(x[rows, n, :, g, 1:], w[rows, 0, :, :m], w[rows, 1, :, :m], ALU.subtract if n == 0 else ALU.add)
                    run(ins) if n + g < 2 else ins.then_inc(s5_xp, 1)
            dve.wait_ge(s5_xp, sl + 1)


    def z_pool(pool):
        for kt in range(KT):
            if kt >= 2:
                pool.wait_ge(h_ready, H0_Z + kt - 1)
            pool.dma_start(G["glu_z"][:, kt % 2, :], zt[ZT["z"] + kt * P:ZT["z"] + (kt + 1) * P, :]).then_inc(glu_in[kt % 2], 16)

    def z_act(act):
        for kt in range(KT):
            act.wait_ge(glu_in[kt % 2], 16 * (kt // 2 + 1))
            nc.scalar.activation(A["a_hi"][:, kt, :], G["glu_z"][:, kt % 2, :], ACT.Copy).then_inc(nh_ready, 1)

    def z_dve(dve):
        for kt in range(KT):
            dve.wait_ge(nh_ready, H0_Z + kt + 1)
            nc.vector.tensor_tensor(A["a_lo"][:, kt, :], G["glu_z"][:, kt % 2, :], A["a_hi"][:, kt, :].bitcast(F32),
                                    ALU.subtract).then_inc(h_ready, 1)

    H0 = {0: 0, 1: 16, "z": 32, 3: 48, 4: 64}
    H0_Z = H0["z"]
    DETAILS = [
        dict(h0=H0[0]), dict(old=xds[0], acc0=16, xin0=0), dict(h0=H0[1]), dict(h0=H0["z"]),
        dict(old=xds[1], acc0=32, xin0=4), dict(h0=H0[3]), dict(old=xds[2], acc0=64, xin0=8), dict(h0=H0[4]),
        dict(), dict(), dict(old=xds[3], acc0=80, xin0=12)]

    def details(n):
        d = dict(h0=None, old=None, acc0=0, xin0=0)
        d.update(DETAILS[n])
        side, regions = PHASES[n]
        d["src"], d["first"] = side, regions[0]
        d["hilo"] = {"A": AB_HI_LO["A"], "B": AB_HI_LO["B"], "LQ": (M["lq_hi"], M["lq_lo"]),
                     "LK": (MK["lk_hi"], MK["lk_lo"])}[side]
        return d

    def products(eng, n, block):
        if n >= len(PHASES):
            return
        d = details(n)
        for r in PHASES[n][1]:
            each_block(eng, r, lambda i: block(eng, r, i, d), unroll=r.evac == "glu" and block is not pe_block)

    out_fm = out.rearrange("a t c -> (a t c)").rearrange("(r c) -> r c", c=L)

    block = ctx.enter_context(nc.Block())

    def stop(eng, who, n, x):
        if STOP != n:
            return False
        if who == "pool":
            eng.wait_ge(acc_done, {0: 16, 1: 32, 4: 48, 6: 80, 10: 96}[n])
            eng.dma_start(out_fm.rearrange("(k p) t -> p k t", p=P), x[:, :, :]).then_inc(x_stored, 16)
            eng.wait_ge(x_stored, 16 * ({0: 0, 1: 1, 4: 2, 6: 3, 10: 4}[n] + 1))
        return True

    @block.sync
    def _(sp):
        sp.dma_start(ident[:, :], inp["ident"]).then_inc(consts_in, 16)
        sp.wait_ge(made, 5)
        for name, (src, index, n) in VECTORS.items():
            v = inp[src] if index is None else inp[src][index]
            if len(v.shape) == 2:
                v = v.rearrange("a b -> (a b)")
            row, width = COL[name], min(n, P)
            sp.dma_start(rows[row % P:row % P + n // width, row // P, :width],
                         v.rearrange("(k p) -> k p", p=width)).then_inc(consts_in, 16)
        sp.dma_start(cols[:, COL["sinks"]:COL["sinks"] + WH],
                     inp["l0_sinks_2"].rearrange("(a h) -> a h", a=1).broadcast_to([P, WH])).then_inc(consts_in, 16)
        sp.dma_start(wide[:, :], inp["wide"]).then_inc(consts_in, 16)
        sp.dma_start(band[:, :], inp["band"]).then_inc(consts_in, 16)
        for _, regions in PHASES:
            for r in regions:
                sp_loads(sp, r)

    NCONST = len(VECTORS) + 4

    @block.gpsimd
    def _(pool):
        turn_in_pool(pool)
        squares_pool(pool, XB["xb_sq"], 0)
        if stop(pool, "pool", 0, XB["xb"]):
            return
        store_x(pool, XB["xb"], 0)
        products(pool, 0, pool_block)
        pool_end(pool, 0)
        barrier(pool, "pool")
        gla_pool(pool)
        barrier(pool, "pool")
        fox_pre_pool(pool)
        att_pool(pool, FOX)
        barrier(pool, "pool")
        products(pool, 1, pool_block)
        if stop(pool, "pool", 1, XB["xb"]):
            return
        store_x(pool, XB["xb"], 1)
        products(pool, 2, pool_block)
        pool_end(pool, 2)
        barrier(pool, "pool")
        s5_pre_pool(pool)
        s5_pool(pool)
        barrier(pool, "pool")
        z_pool(pool)
        pool.wait_ge(h_ready, H0_Z + KT)
        products(pool, 3, pool_block)
        barrier(pool, "pool")
        products(pool, 4, pool_block)
        if stop(pool, "pool", 4, XA["xa"]):
            return
        squares_pool(pool, XA["xa_sq"], 48)
        pool.wait_ge(xn_ready, 48)
        store_x(pool, XA["xa"], 2)
        products(pool, 5, pool_block)
        pool_end(pool, 5)
        barrier(pool, "pool")
        lru_pool(pool)
        barrier(pool, "pool")
        swa_pre_pool(pool)
        att_pool(pool, SWA)
        barrier(pool, "pool")
        products(pool, 6, pool_block)
        if stop(pool, "pool", 6, XA["xa"]):
            return
        store_x(pool, XA["xa"], 3)
        products(pool, 7, pool_block)
        pool_end(pool, 7)
        barrier(pool, "pool")
        barrier(pool, "pool")
        products(pool, 8, pool_block)
        products(pool, 9, pool_block)
        pool_end(pool, 9)
        barrier(pool, "pool")
        rope_pool(pool)
        att_pool(pool, MLA)
        att_pool(pool, DIFF)
        barrier(pool, "pool")
        products(pool, 10, pool_block)
        if stop(pool, "pool", 10, XA["xa"]):
            return
        turn_out_pool(pool, XB["xb_tok"])

    @block.tensor
    def _(pe):
        pe.wait_ge(consts_in, 16 * NCONST)
        for n in range(2):
            c = min(NROWS - n * P, P)
            ins = nc.tensor.transpose(pm[3][:, n * P:n * P + c], rows[:c, n, :], ident[:c, :c])
        ins.then_inc(cols_turned, 1)
        turn_in_pe(pe)
        if STOP == 0:
            return
        rstd_pe(pe, 0)
        products(pe, 0, pe_block)
        barrier(pe, "pe")
        gla_pe(pe)
        barrier(pe, "pe")
        att_pe(pe, FOX)
        barrier(pe, "pe")
        products(pe, 1, pe_block)
        if STOP == 1:
            return
        rstd_pe(pe, 1)
        products(pe, 2, pe_block)
        barrier(pe, "pe")
        s5_pre_pe(pe)
        s5_pe(pe)
        barrier(pe, "pe")
        products(pe, 3, pe_block)
        barrier(pe, "pe")
        products(pe, 4, pe_block)
        if STOP == 4:
            return
        rstd_pe(pe, 2)
        rstd_pe(pe, 3)
        products(pe, 5, pe_block)
        barrier(pe, "pe")
        lru_pe(pe)
        barrier(pe, "pe")
        pe.wait_ge(shared_in, 112)
        att_pe(pe, SWA)
        barrier(pe, "pe")
        products(pe, 6, pe_block)
        if STOP == 6:
            return
        rstd_pe(pe, 4)
        products(pe, 7, pe_block)
        barrier(pe, "pe")
        latent_pe(pe)
        barrier(pe, "pe")
        products(pe, 8, pe_block)
        products(pe, 9, pe_block)
        barrier(pe, "pe")
        pe.wait_ge(rope_done, 1)
        att_pe(pe, MLA)
        att_pe(pe, DIFF)
        barrier(pe, "pe")
        products(pe, 10, pe_block)
        if STOP == 10:
            return
        rstd_pe(pe, 5)
        turn_out_pe(pe, XA["xa"])

    @block.scalar
    def _(act):
        act.wait_ge(consts_in, 16 * NCONST)
        act.wait_ge(cols_ready, 1)
        for n in range(AHEAD):
            split_hi(act, n, n % RING, 16)
        act.wait_ge(xt_ev, 16)
        squares_act(act, XB["xb"], XB["xb_sq"], 0)
        if STOP == 0:
            return
        rstd_act(act, 0)
        split_norm_act(act, XB["xb_n"], A["a_hi"], 0, 0)
        products(act, 0, act_block)
        barrier(act, "act")
        gla_act(act)
        barrier(act, "act")
        fox_pre_act(act)
        att_act(act, FOX)
        barrier(act, "act")
        products(act, 1, act_block)
        if STOP == 1:
            return
        rstd_act(act, 1)
        split_norm_act(act, XB["xb_n"], A["a_hi"], 1, 16)
        products(act, 2, act_block)
        barrier(act, "act")
        s5_pre_act(act)
        s5_act(act)
        barrier(act, "act")
        z_act(act)
        products(act, 3, act_block)
        barrier(act, "act")
        products(act, 4, act_block)
        if STOP == 4:
            return
        rstd_act(act, 2)
        act.wait_ge(xn_ready, 48)
        squares_act(act, XA["xa"], XA["xa_sq"], 48)
        rstd_act(act, 3)
        split_norm_act(act, XA["xa_n"], B["b_hi"], 3, 48)
        products(act, 5, act_block)
        barrier(act, "act")
        lru_act(act)
        barrier(act, "act")
        att_act(act, SWA)
        barrier(act, "act")
        products(act, 6, act_block)
        if STOP == 6:
            return
        rstd_act(act, 4)
        split_norm_act(act, XA["xa_n"], B["b_hi"], 4, 64)
        products(act, 7, act_block)
        barrier(act, "act")
        latent_act(act)
        barrier(act, "act")
        products(act, 8, act_block)
        products(act, 9, act_block)
        barrier(act, "act")
        rope_act(act)
        att_act(act, MLA)
        att_act(act, DIFF)
        barrier(act, "act")
        products(act, 10, act_block)
        if STOP == 10:
            return
        rstd_act(act, 5)
        turn_out_act(act, XB["xb_tok"])

    @block.vector
    def _(dve):
        nc.vector.memset(ones[:, :], 1.0).then_inc(made, 1)
        nc.vector.memset(eps[:, :], EPS).then_inc(made, 1)
        nc.vector.memset(onecol[:, :], 1.0).then_inc(made, 1)
        nc.vector.memset(halfpi[:, :], 1.5707963267948966).then_inc(made, 1)
        nc.vector.memset(rows[:, :, :], 0.0).then_inc(made, 1)
        dve.wait_ge(cols_turned, 1)
        nc.vector.tensor_copy(cols[:, :NROWS], pm[3][:, :NROWS]).then_inc(cols_ready, 1)
        dve.wait_ge(cols_ready, 1)
        for n in range(AHEAD):
            split_lo(dve, n, n % RING, 16)
        turn_in_dve(dve)
        if STOP == 0:
            return
        rstd_dve(dve, 0)
        split_norm_dve(dve, XB["xb"], XB["xb_n"], "ab_norm_g", A["a_hi"], A["a_lo"], 0, 0)
        products(dve, 0, dve_block)
        barrier(dve, "dve")
        gla_dve(dve)
        barrier(dve, "dve")
        fox_pre_dve(dve)
        att_dve(dve, FOX)
        barrier(dve, "dve")
        products(dve, 1, dve_block)
        if STOP == 1:
            return
        rstd_dve(dve, 1)
        split_norm_dve(dve, XB["xb"], XB["xb_n"], "c_norm_g", A["a_hi"], A["a_lo"], 1, 16)
        products(dve, 2, dve_block)
        barrier(dve, "dve")
        s5_pre_dve(dve)
        s5_dve(dve)
        barrier(dve, "dve")
        z_dve(dve)
        products(dve, 3, dve_block)
        barrier(dve, "dve")
        products(dve, 4, dve_block)
        if STOP == 4:
            return
        rstd_dve(dve, 2)
        scale_x_dve(dve, XA["xa"], "final_norm_g", 2)
        rstd_dve(dve, 3)
        split_norm_dve(dve, XA["xa"], XA["xa_n"], "norm_a", B["b_hi"], B["b_lo"], 3, 48)
        products(dve, 5, dve_block)
        barrier(dve, "dve")
        lru_dve(dve)
        barrier(dve, "dve")
        att_dve(dve, SWA)
        barrier(dve, "dve")
        products(dve, 6, dve_block)
        if STOP == 6:
            return
        rstd_dve(dve, 4)
        split_norm_dve(dve, XA["xa"], XA["xa_n"], "norm_b", B["b_hi"], B["b_lo"], 4, 64)
        products(dve, 7, dve_block)
        barrier(dve, "dve")
        latent_dve(dve)
        barrier(dve, "dve")
        products(dve, 8, dve_block)
        products(dve, 9, dve_block)
        barrier(dve, "dve")
        rope_dve(dve)
        att_dve(dve, MLA)
        att_dve(dve, DIFF)
        barrier(dve, "dve")
        products(dve, 10, dve_block)
        if STOP == 10:
            return
        rstd_dve(dve, 5)
        scale_x_dve(dve, XA["xa"], "last_g", 5)

    ctx.close()


INPUTS = [
    "x", "ab_norm_g", "ab_w_in", "gla_alpha_up", "gla_alpha_b", "gla_head_g", "fox_f_b", "ab_w_out", "c_norm_g", "c_w_in",
    "s5_lambda_re", "s5_lambda_im", "s5_log_step", "s5_b_re", "s5_b_im", "s5_c_re", "s5_c_im", "s5_d", "glu_w", "glu_b",
    "c_w_out", "final_norm_g", "norm_gains_2", "final_norm_gain_2", "l0_w_in_2", "l0_conv_w_2", "l0_conv_b_2",
    "l0_gate_x_w_2", "l0_gate_x_b_2", "l0_gate_a_w_2", "l0_gate_a_b_2", "l0_lru_lambda_2", "l0_sinks_2", "l0_w_out_2",
    "l1_w_in_2", "l1_q_norm_2", "l1_w_uq_2", "l1_kv_norm_2", "l1_w_ukv_2", "l1_lambda_q1_2", "l1_lambda_k1_2",
    "l1_lambda_q2_2", "l1_lambda_k2_2", "l1_subln_2", "l1_w_out_2"]


def shape_constants():
    import numpy as np

    q, k = np.arange(P)[:, None], np.arange(P)[None, :]
    causal = np.where(k <= q, 0.0, NEG).astype(np.float32)
    before = np.where(k > q, 0.0, NEG).astype(np.float32)
    wide = np.concatenate([np.zeros((P, L - P), np.float32), causal], 1)
    masks = np.zeros((P, 8, P), np.float32)
    masks[:, 0, :] = q == k
    for level in range(1, 8):
        s = 2 ** (level - 1)
        masks[:, level, :] = (q // (2 * s) == k // (2 * s)) & (q // s % 2 == 0) & (k // s % 2 == 1)
    half = MROPE // 2
    freq = np.float32(10000.0) ** (-np.arange(half, dtype=np.float32) / np.float32(half))
    angle = np.arange(L, dtype=np.float32)[None, :] * freq.astype(np.float32)[:, None]
    cos, sin = np.cos(angle), np.sin(angle)
    rope = np.stack([np.concatenate([cos] * 4), np.concatenate([-sin, sin] * 2)], 1).astype(np.float32)
    steps = np.broadcast_to(np.arange(SK, dtype=np.float32), (P, SK)).copy()
    return {"ident": np.eye(P, dtype=np.float32), "wide": wide, "band": np.concatenate([before, causal], 1),
            "masks": masks.reshape(P, -1), "rope": rope.reshape(P, -1), "steps": steps}


def kernel(**inputs):
    import numpy as np
    import concourse.bacc as bacc
    from concourse.bass_utils import run_bass_kernel_spmd

    nc = bacc.Bacc("TRN2", target_bir_lowering=False, num_devices=1)
    arrays, inp = {}, {}
    given = {name: np.ascontiguousarray(inputs[name]) for name in INPUTS}
    given.update(shape_constants())
    for name, a in given.items():
        arrays["in_" + name] = a
        inp[name] = nc.dram_tensor("in_" + name, a.shape, mybir.dt.from_np(a.dtype), kind="ExternalInput").ap()
    out = nc.dram_tensor("out_x", (1, L, D), F32, kind="ExternalOutput").ap()
    build(nc, inp, out)
    r = run_bass_kernel_spmd(nc, [arrays], core_ids=[0])
    return r.results[0]["out_x"]
```

```python
from contextlib import ExitStack

import concourse.bass as bass
from concourse import mybir

F32 = mybir.dt.float32
F32R = mybir.dt.float32r
I32 = mybir.dt.int32
ALU = mybir.AluOpType
ACT = mybir.ActivationFunctionType
AX = mybir.AxisListType

P = 128
L = 512
NTOK = L // P
D = 2048
KT = D // P
BLK = 512
MT = BLK // P
PK = 2
RING = 4
AHEAD = 3
EPS = 1e-6
NEG = -1e30
LOWEST = -3e38

GH, GDK, GDV, GRANK, GTAU = 4, 128, 256, 16, 16.0
FH, FD = 8, 128
SG, SC, SP_, ST = 128, 16, 64, 8
SK = L // ST
SPAIR = 8
SSL = SG // (2 * SPAIR)
RB, CW, LRU_C = 8, 4, 8.0
WH, WD, WKV = 16, 64, 2
MH, MNOPE, MROPE, MQR, MKVR = 8, 128, 64, 768, 512
DH, DQK = 8, 64
LAMBDA_INIT = 0.8 - 0.6 * 2.718281828459045 ** -0.3

AB = dict(q=0, k=512, v=1024, lr=2048, gate=2064, fq=3088, fk=4112, fv=5136, ff=6160, fgate=6168)
L0 = dict(x=0, gate=1024, q=2048, k=3072, v=3200, sgate=3328)
L1 = dict(cq=0, ckv=768, kr=1280, gate=1344, dq=2368, dk=3392, dv=4416, dgate=5440)

ZT = dict(lr=0, ff=128, q=256, k=768, gate=1280, fq=2304, fk=3328, fgate=4352,
          sgate=5376, z=7424,
          rx=9472, rgate=10496, wq=11520, wkv=12544, wgate=12800,
          kr=13824, mgate=13952, dq=14976, dk=16000, dgate=17024, qn=18048, qr=19072, kn=19584)
ZT_ROWS = 20608
ZN = dict(v=0, fv=1024, u=2048, wv=4096, dv=4224, mv=5248)
ZN_COLS = 6272


class Region:

    def __init__(self, w, kts, c0, blocks, width, form, evac, dst=None, d0=0, arg=None):
        self.w, self.kts, self.c0, self.blocks, self.width = w, kts, c0, blocks, width
        self.form, self.evac, self.dst, self.d0, self.arg = form, evac, dst, d0, arg
        self.pieces = kts // PK
        self.dmas = 1
        self.banks = -(-width // P) if form == "T" else MT

    def rows(self, m):
        return min(P, self.width - m * P) if self.form == "T" else P

    def cols(self):
        return L if self.form == "T" else self.width


class Attention:

    def __init__(self, *, buf, tiles, heads, comps, dv, scale, key_tiles, products, bias, bias_ready, pool_work, value,
                 gate, gate_of, kt0, loads, hi, lo, units0, jobs0, tiles0, in0, sink=None, lam=None, gain=None):
        self.buf, self.tiles, self.heads, self.comps, self.dv, self.scale = buf, tiles, heads, comps, dv, scale
        self.key_tiles, self.products, self.bias, self.bias_ready = key_tiles, products, bias, bias_ready
        self.pool_work, self.value, self.gate, self.gate_of, self.kt0 = pool_work, value, gate, gate_of, kt0
        self.loads, self.hi, self.lo, self.sink, self.lam, self.gain = loads, hi, lo, sink, lam, gain
        self.units0, self.jobs0, self.tiles0, self.in0 = units0, jobs0, tiles0, in0
        self.per = heads * NTOK
        self.jobs = tiles * self.per
        self.units = self.jobs * comps


def count_regions(regions):
    piece, bank, stage = 0, [0] * MT, [0] * MT
    for r in regions:
        r.piece0, r.bank0, r.stage0 = piece, list(bank), list(stage)
        piece += r.blocks * r.pieces
        for m in range(r.banks):
            bank[m] += r.blocks
            if r.dst is not None:
                stage[m] += r.blocks
    return piece

VECTORS = dict(
    ab_norm_g=("ab_norm_g", 0, D), c_norm_g=("c_norm_g", 0, D), final_norm_g=("final_norm_g", None, D),
    norm_a=("norm_gains_2", 0, D), norm_b=("norm_gains_2", 1, D), last_g=("final_norm_gain_2", None, D),
    alpha_b=("gla_alpha_b", 0, GH * GDK), head_g=("gla_head_g", 0, GH * GDV), glu_b=("glu_b", 0, D),
    kv_norm=("l1_kv_norm_2", None, MKVR),
    conv_b=("l0_conv_b_2", None, RB * P), lam=("l0_lru_lambda_2", None, RB * P),
    q_norm=("l1_q_norm_2", None, MQR), subln=("l1_subln_2", None, P),
    gx_b=("l0_gate_x_b_2", None, RB * P), ga_b=("l0_gate_a_b_2", None, RB * P),
    conv_w=("l0_conv_w_2", None, CW * RB * P), f_b=("fox_f_b", None, FH))
COL, NROWS = {}, 0
for _name, (_, _, _n) in VECTORS.items():
    COL[_name] = NROWS
    assert NROWS // P == (NROWS + -(-_n // P) - 1) // P
    NROWS += -(-_n // P)
COL["sinks"] = NROWS
NCOLS = NROWS + WH


def build(nc, inp, out):
    ctx = ExitStack()

    def sem(name):
        return ctx.enter_context(nc.semaphore(name))

    def dram(name, shape):
        return nc.dram_tensor(name, shape, F32, kind="Internal").ap()

    def sb(name, shape, dtype=F32):
        return ctx.enter_context(nc.sbuf_tensor(name, [P] + shape, dtype))

    def overlay(base, tensors):
        made = {}
        with ExitStack() as scope:
            if base:
                scope.enter_context(nc.sbuf_tensor(f"gap_{base}_{tensors[0][0]}", [P, base // 4], F32))
            for name, shape, dtype in tensors:
                made[name] = scope.enter_context(nc.sbuf_tensor(name, [P] + shape, dtype))
        return made

    zt = dram("zt", (ZT_ROWS, L))
    zn = dram("zn", (L, ZN_COLS))
    xds = [dram(f"xd{n}", (D, L)) for n in range(4)]
    negc_dram = dram("negc_dram", (FH, L))

    raw = sb("raw", [RING, PK * BLK])
    whi = sb("whi", [RING, PK * BLK], F32R)
    wlo = sb("wlo", [RING, PK * BLK], F32R)
    stage = sb("stage", [MT, L])
    ident = sb("ident", [P])
    ones = sb("ones", [P])
    cols = sb("cols", [NCOLS])
    acc = sb("acc", [L])
    rstd = sb("rstd", [L])
    wide = sb("wide", [L])
    band = sb("band", [2 * P])

    eps, onecol, halfpi = sb("eps", [1]), sb("onecol", [1]), sb("halfpi", [1])
    rows = sb("rows", [2, P])
    ident_in = sem("identity_in")
    NCONST = len(VECTORS) + 3
    VECTORS_AFTER = 8
    made, cols_turned, cols_ready = sem("constants_made"), sem("vectors_turned"), sem("vectors_ready")

    HALF = 2 * KT * L * 4
    EXTRA = 2 * HALF
    G = overlay(EXTRA, [("glu_z", [2, L], F32), ("glu_g", [2, L], F32)])
    A = overlay(0, [("a_hi", [KT, L], F32R), ("a_lo", [KT, L], F32R)])
    B = overlay(HALF, [("b_hi", [KT, L], F32R), ("b_lo", [KT, L], F32R)])
    XA = overlay(0, [("xa", [KT, L], F32), ("xa_in", [MT, L], F32), ("xa_sq", [2, L], F32), ("xa_n", [2, L], F32)])
    XB = overlay(HALF, [("xb", [KT, L], F32), ("xb_in", [MT, L], F32), ("xb_sq", [2, L], F32), ("xb_n", [2, L], F32),
                        ("xb_tok", [2, D], F32)])
    AB_HI_LO = {"A": (A["a_hi"], A["a_lo"]), "B": (B["b_hi"], B["b_lo"])}
    X_OF = {"A": (XA["xa"], XA["xa_in"], XA["xa_sq"], XA["xa_n"]),
            "B": (XB["xb"], XB["xb_in"], XB["xb_sq"], XB["xb_n"])}

    pg = [ctx.enter_context(nc.psum_tensor(f"pg{m}", [P, L], F32)) for m in range(MT)]
    pm = [ctx.enter_context(nc.psum_tensor(f"pm{m}", [P, L], F32)) for m in range(4)]

    bar = sem("phase_ended")
    consts_in = sem("consts_in")
    raw_in = [sem(f"raw_in{s}") for s in range(RING)]
    hi_ready, lo_ready, w_used = sem("w_hi_ready"), sem("w_lo_ready"), sem("w_used")
    bank_ready = [sem(f"bank_ready{m}") for m in range(MT)]
    evacd = [sem(f"bank_evacuated{m}") for m in range(MT)]
    stored = [sem(f"stored{m}") for m in range(MT)]
    xin_in = [sem(f"old_x_in{m}") for m in range(MT)]
    sq_ready, acc_done = sem("squares_ready"), sem("squares_added")
    x_stored = sem("x_stored")
    rs_ready, sd_ready, rstd_ready = sem("square_sum_ready"), sem("deviation_ready"), sem("rstd_ready")
    xn_ready, nh_ready, h_ready = sem("normed_ready"), sem("normed_hi_ready"), sem("normed_lo_ready")
    act_seq, dve_seq = sem("act_seq"), sem("dve_seq")
    glu_in = [sem(f"glu_operands_in{n}") for n in range(2)]
    glu_mid, glu_done, glu_hi, glu_lo = sem("glu_gates"), sem("glu_products"), sem("glu_hi"), sem("glu_lo")
    counts = {}

    def col(name, n=0):
        return cols[:, COL[name] + n:COL[name] + n + 1]

    def serial(eng, s):
        def run(ins):
            counts[s.name] = counts.get(s.name, 0) + 1
            ins.then_inc(s, 1)
            eng.wait_ge(s, counts[s.name])
        return run

    barriers = {}

    def barrier(eng, who):
        barriers[who] = barriers.get(who, 0) + 1
        eng.drain().then_inc(bar, 1)
        eng.wait_ge(bar, 4 * barriers[who])

    def window(w):
        return lambda i, q, c0: w[q * PK * P:(q + 1) * PK * P, bass.ds(c0 + i * BLK, BLK)].rearrange(
            "(k p) n -> p k n", p=P)

    def to_zt(name, row=0):
        return lambda i, m, r: zt[bass.ds(ZT[name] + row + i * BLK + m * P, r.rows(m)), :]

    def to_zn(name):
        return lambda i, m, r: zn[m * P:(m + 1) * P, bass.ds(ZN[name] + i * BLK, r.width)]

    def T(w, c0, n, evac, dst):
        made = []
        if n // BLK:
            made.append(Region(window(w), KT, c0, n // BLK, BLK, "T", evac, to_zt(dst)))
        if n % BLK:
            lo = n // BLK * BLK
            made.append(Region(window(w), KT, c0 + lo, 1, n % BLK, "T", evac, to_zt(dst, lo)))
        return made

    def N(w, c0, n, dst):
        return [Region(window(w), KT, c0, max(n // BLK, 1), min(n, BLK), "N", "copy", to_zn(dst))]

    def resid(w):
        return [Region(window(w), KT, 0, D // BLK, BLK, "T", "resid")]

    def as3(name):
        return inp[name][0]

    wab, wc = as3("ab_w_in"), as3("c_w_in")
    w0, w1 = inp["l0_w_in_2"], inp["l1_w_in_2"]
    uq = inp["l1_w_uq_2"].rearrange("(k p) (h c) -> p k h c", p=P, h=MH)
    ukv = inp["l1_w_ukv_2"].rearrange("(k p) (h c) -> p k h c", p=P, h=MH)

    def heads_of(w, n, c0, width):
        return lambda i, q, _: w[:, q * PK:(q + 1) * PK, i * n:(i + 1) * n, c0:c0 + width]

    PHASES = [
        ("A", T(wab, AB["lr"], GRANK, "copy", "lr") + T(wab, AB["ff"], FH, "copy", "ff")
         + T(wab, AB["q"], 1024, "copy", "q") + T(wab, AB["gate"], 1024, "silu", "gate")
         + T(wab, AB["fq"], 2048, "copy", "fq") + T(wab, AB["fgate"], 1024, "silu", "fgate")
         + N(wab, AB["v"], 1024, "v") + N(wab, AB["fv"], 1024, "fv")),
        ("A", resid(as3("ab_w_out"))),
        ("A", N(wc, 0, D, "u") + T(wc, D, D, "silu", "sgate")),
        ("A", [Region(window(as3("glu_w")), KT, 0, D // BLK, BLK, "T", "glu")]),
        ("B", resid(as3("c_w_out"))),
        ("B", T(w0, L0["x"], 1024, "copy", "rx") + T(w0, L0["gate"], 1024, "silu", "rgate")
         + T(w0, L0["q"], 1024, "copy", "wq") + T(w0, L0["k"], 128, "copy", "wkv")
         + N(w0, L0["v"], 128, "wv") + T(w0, L0["sgate"], 1024, "silu", "wgate")),
        ("B", resid(inp["l0_w_out_2"])),
        ("B", [Region(window(w1), KT, L1["cq"], 1, BLK, "T", "keep", None, 0, 0),
               Region(window(w1), KT, L1["cq"] + BLK, 1, MQR - BLK, "T", "keep", None, 0, 4),
               Region(window(w1), KT, L1["ckv"], 1, BLK, "T", "keep", None, 0, 6)]
         + T(w1, L1["kr"], MROPE, "copy", "kr") + T(w1, L1["gate"], 1024, "silu", "mgate")
         + T(w1, L1["dq"], 2048, "copy", "dq") + T(w1, L1["dgate"], 1024, "silu", "dgate")
         + N(w1, L1["dv"], 1024, "dv")),
        ("LQ", [Region(heads_of(uq, 4, 0, MNOPE), MQR // P, 0, 2, BLK, "T", "copy", to_zt("qn")),
                Region(heads_of(uq, 8, MNOPE, MROPE), MQR // P, 0, 1, BLK, "T", "copy", to_zt("qr"))]),
        ("LK", [Region(heads_of(ukv, 4, 0, MNOPE), MKVR // P, 0, 2, BLK, "T", "copy", to_zt("kn")),
                Region(heads_of(ukv, 4, MNOPE, P), MKVR // P, 0, 2, BLK, "N", "copy", to_zn("mv"))]),
        ("B", resid(inp["l1_w_out_2"])),
    ]
    pieces_in_all = count_regions([r for _, rs in PHASES for r in rs])
    for n, (_, regions) in enumerate(PHASES):
        for r in regions:
            r.peel = n in (0, 2, 3, 5, 7) and r is regions[0]

    landed, at_slot = [], [0] * RING
    for _, rs in PHASES:
        for r in rs:
            if r.kts != KT:
                r.dmas = PK
            for n in range(r.piece0, r.piece0 + r.blocks * r.pieces):
                at_slot[n % RING] += 16 * r.dmas
                landed.append(at_slot[n % RING])
    in_order = [r for _, rs in PHASES for r in rs]
    for r, after in zip(in_order, in_order[1:] + [None]):
        r.peel_last = after is None or after.dmas != r.dmas

    def each_block(eng, r, body, unroll=False):
        first = 1 if (0 in r.bank0[:r.banks] or r.piece0 < 2 * RING or r.dst is not None and 0 in r.stage0[:r.banks]
                      or r.evac == "resid" or r.peel) else 0
        last = 1 if r.peel_last else 0
        looped = r.blocks - first - last if r.pieces % RING == 0 and r.evac != "keep" and not unroll else 0
        if looped < 2:
            for i in range(r.blocks):
                body(i)
            return
        if first:
            body(0)
        with eng.Fori(first, first + looped) as i:
            body(i)
        if last:
            body(r.blocks - 1)

    def fixed(v):
        return isinstance(v, int)

    def sp_loads(sp, r):
        def body(i):
            for q in range(r.pieces):
                n = r.piece0 + q + i * r.pieces
                slot = (r.piece0 + q + (i * r.pieces if fixed(i) else 0)) % RING
                if r.evac == "glu" and fixed(i) and i == 0 and q == AHEAD + RING:
                    s5_sp(sp)
                if not fixed(i) or n >= RING:
                    sp.wait_ge(lo_ready, n - RING + 1)
                src = r.w(i, q, r.c0)
                if r.dmas == PK:
                    for k in range(PK):
                        sp.dma_start(raw[:, slot, k * BLK:(k + 1) * BLK].rearrange("p (h c) -> p h c", h=src.shape[2]),
                                     src[:, k]).then_inc(raw_in[slot], 16)
                else:
                    sp.dma_start(raw[:, slot, :].rearrange("p (k n) -> p k n", k=PK), src).then_inc(raw_in[slot], 16)
        each_block(sp, r, body)

    def split_hi(act, n, slot, target):
        if not fixed(n) or n < pieces_in_all:
            act.wait_ge(raw_in[slot], target)
            if not fixed(n) or n >= RING:
                act.wait_ge(w_used, n - RING + 1)
            nc.scalar.activation(whi[:, slot, :], raw[:, slot, :], ACT.Copy).then_inc(hi_ready, 1)

    def split_lo(dve, n, slot, target):
        if not fixed(n) or n < pieces_in_all:
            dve.wait_ge(hi_ready, n + 1)
            nc.vector.tensor_tensor(wlo[:, slot, :], raw[:, slot, :], whi[:, slot, :].bitcast(F32),
                                    ALU.subtract).then_inc(lo_ready, 1)

    def splits(eng, r, i, split):
        for q in range(r.pieces):
            n = r.piece0 + q + AHEAD + i * r.pieces
            if fixed(i):
                split(eng, n, n % RING, landed[n] if n < pieces_in_all else None)
            else:
                first = r.piece0 + q + AHEAD
                split(eng, n, first % RING, landed[first] + i * (16 * r.pieces // RING))

    def bank_full(eng, r, i, m):
        if m == r.banks - 1:
            eng.wait_ge(w_used, r.piece0 + r.pieces + i * r.pieces)
        else:
            eng.wait_ge(bank_ready[m], r.ready0[m] + 1 + i)

    ready = [0] * MT
    for _, rs in PHASES:
        for r in rs:
            r.ready0 = list(ready)
            for m in range(r.banks - 1):
                ready[m] += r.blocks

    def act_block(act, r, i, extra):
        splits(act, r, i, split_hi)
        if r.evac in ("copy", "silu"):
            for m in range(r.banks):
                bank_full(act, r, i, m)
                if not fixed(i) or r.stage0[m] + i > 0:
                    act.wait_ge(stored[m], 16 * r.stage0[m] + 16 * i)
                nc.scalar.activation(stage[:r.rows(m), m, :r.cols()], pg[m][:r.rows(m), :r.cols()],
                                     ACT.Copy if r.evac == "copy" else ACT.Silu).then_inc(evacd[m], 1)
        elif r.evac == "resid":
            x, _, sq, _ = X_OF["B" if extra["src"] == "A" else "A"]
            for m in range(r.banks):
                act.wait_ge(evacd[m], r.bank0[m] + 1 + i)
                if m >= 2 or not fixed(i) or i:
                    act.wait_ge(acc_done, extra["acc0"] + m - 1 + i * MT)
                nc.scalar.activation(sq[:, m % 2, :], x[:, bass.ds(i * MT + m, 1), :], ACT.Square).then_inc(sq_ready, 1)
        elif r.evac == "glu":
            for m in range(r.banks):
                bank_full(act, r, i, m)
                if i:
                    act.wait_ge(glu_mid, MT * (i - 1) + m + 1)
                nc.scalar.activation(stage[:, m, :], pg[m][:, :], ACT.Sigmoid,
                                     bias=col("glu_b", MT * i + m)).then_inc(evacd[m], 1)
            for m in range(r.banks):
                n = MT * i + m
                act.wait_ge(glu_done, n + 1)
                nc.scalar.activation(B["b_hi"][:, n, :], G["glu_z"][:, n % 2, :], ACT.Copy).then_inc(glu_hi, 1)

    def dve_block(dve, r, i, extra):
        splits(dve, r, i, split_lo)
        if r.evac == "resid":
            x, xin, _, _ = X_OF["B" if extra["src"] == "A" else "A"]
            for m in range(r.banks):
                bank_full(dve, r, i, m)
                dve.wait_ge(xin_in[m], 16 * (extra["xin0"] + 1) + 16 * i)
                nc.vector.tensor_tensor(x[:, bass.ds(i * MT + m, 1), :], xin[:, m:m + 1, :], pg[m][:, :],
                                        ALU.add).then_inc(evacd[m], 1)
        elif r.evac == "keep":
            for m in range(r.banks):
                bank_full(dve, r, i, m)
                dve.wait_ge(x_stored, 16 * 4)
                nc.vector.tensor_copy(M["latent"][:, r.arg + m, :], pg[m][:, :]).then_inc(evacd[m], 1)
        elif r.evac == "glu":
            for m in range(r.banks):
                n = MT * i + m
                z, g = G["glu_z"][:, n % 2, :], G["glu_g"][:, n % 2, :]
                dve.wait_ge(evacd[m], r.bank0[m] + i + 1)
                dve.wait_ge(glu_in[n % 2], 8 * KT + 32 * (n // 2 + 1))
                nc.vector.tensor_tensor(g, stage[:, m, :], g, ALU.mult).then_inc(glu_mid, 1)
                dve.wait_ge(glu_mid, n + 1)
                nc.vector.tensor_tensor(z, z, g, ALU.mult).then_inc(glu_done, 1)
                dve.wait_ge(glu_hi, n + 1)
                nc.vector.tensor_tensor(B["b_lo"][:, n, :], z, B["b_hi"][:, n, :].bitcast(F32),
                                        ALU.subtract).then_inc(glu_lo, 1)

    def pe_block(pe, r, i, extra):
        hi, lo = extra["hilo"]
        for q in range(r.pieces):
            n = r.piece0 + q + i * r.pieces
            slot = (r.piece0 + q + (i * r.pieces if fixed(i) else 0)) % RING
            pe.wait_ge(lo_ready, n + 1)
            for m in range(r.banks):
                if q == 0 and (not fixed(i) or r.bank0[m] + i > 0):
                    pe.wait_ge(evacd[m], r.bank0[m] + i)
                for k in range(PK):
                    kt = q * PK + k
                    if m == 0 and extra["h0"] is not None and fixed(i) and i == 0 and r is extra["first"]:
                        pe.wait_ge(h_ready, extra["h0"] + kt + 1)
                    for n_pass, (ws, hs) in enumerate(((whi, hi), (whi, lo), (wlo, hi))):
                        c = k * BLK
                        if r.form == "T":
                            lhsT = ws[:, slot, c + m * P:c + (m + 1) * P]
                            rhs = hs[:, kt, :]
                        else:
                            lhsT = hs[:, kt, m * P:(m + 1) * P]
                            rhs = ws[:, slot, c:c + r.width]
                        ins = nc.tensor.matmul(pg[m][:, :r.cols()], lhsT, rhs,
                                               start=(kt == 0 and n_pass == 0),
                                               stop=(kt == r.kts - 1 and n_pass == 2))
                if m == r.banks - 1:
                    ins.then_inc(w_used, 1)
                elif q == r.pieces - 1:
                    ins.then_inc(bank_ready[m], 1)

    def pool_block(pool, r, i, extra):
        if r.dst is not None:
            for m in range(r.banks):
                pool.wait_ge(evacd[m], r.bank0[m] + 1 + i)
                pool.dma_start(r.dst(i, m, r), stage[:r.rows(m), m, :r.cols()]).then_inc(stored[m], 16)
        elif r.evac == "resid":
            _, xin, sq, _ = X_OF["B" if extra["src"] == "A" else "A"]
            for m in range(r.banks):
                pool.wait_ge(evacd[m], r.bank0[m] + i)
                pool.dma_start(xin[:, m, :], extra["old"][bass.ds((i * MT + m) * P, P), :]).then_inc(xin_in[m], 16)
            for m in range(r.banks):
                pool.wait_ge(sq_ready, extra["acc0"] + m + 1 + i * MT)
                if m or not fixed(i) or i or extra["acc0"]:
                    pool.wait_ge(acc_done, extra["acc0"] + m + i * MT)
                if fixed(i) and i == 0 and m == 0:
                    nc.gpsimd.tensor_copy(acc[:, :], sq[:, 0, :]).then_inc(acc_done, 1)
                else:
                    nc.gpsimd.tensor_tensor(acc[:, :], acc[:, :], sq[:, m % 2, :], ALU.add).then_inc(acc_done, 1)
        elif r.evac == "glu":
            for m in range(r.banks):
                n = MT * i + m
                if n >= 2:
                    pool.wait_ge(glu_lo, n - 1)
                for name, src in (("glu_z", "z"), ("glu_g", "sgate")):
                    pool.dma_start(G[name][:, n % 2, :], zt[ZT[src] + n * P:ZT[src] + (n + 1) * P, :]).then_inc(glu_in[n % 2], 16)

    norms = {"n": 0}

    def squares_act(act, x, sq, base):
        for kt in range(KT):
            act.wait_ge(xn_ready, xn_after[3] - KT + kt + 1)
            if kt >= 2:
                act.wait_ge(acc_done, base + kt - 1)
            nc.scalar.activation(sq[:, kt % 2, :], x[:, kt, :], ACT.Square).then_inc(sq_ready, 1)

    def squares_pe(pe, sq, base, j):
        pe.wait_ge(sd_ready, j)
        for kt in range(KT):
            pe.wait_ge(sq_ready, base + kt + 1)
            nc.tensor.matmul(pm[0][:, :], ones[:, :], sq[:, kt % 2, :], start=(kt == 0), stop=(kt == KT - 1)).then_inc(acc_done, 1)

    def rstd_pe(pe, j):
        pe.wait_ge(acc_done, KT * (j + 1))
        pe.wait_ge(sd_ready, j)
        nc.tensor.matmul(pm[0][:, :], ones[:, :], acc[:, :], start=True, stop=True).then_inc(rs_ready, 1)

    def rstd_act(act, j):
        if j in (0, 3):
            act.wait_ge(acc_done, KT * (j + 1))
        else:
            act.wait_ge(rs_ready, 4 * NTOK + (j if j < 3 else j - 1))
        if j:
            act.wait_ge(xn_ready, xn_after[j])
        nc.scalar.activation(rstd[:, :], acc[:, :] if j == 0 else pm[0][:, :], ACT.Sqrt, scale=1.0 / D,
                             bias=eps[:, 0:1]).then_inc(sd_ready, 1)

    def rstd_dve(dve, j):
        dve.wait_ge(sd_ready, j + 1)
        nc.vector.reciprocal(rstd[:, :], rstd[:, :]).then_inc(rstd_ready, 1)
        dve.wait_ge(rstd_ready, j + 1)

    xn_after = [0, 16, 32, 48, 64, 80, 96]

    def split_norm_dve(dve, x, xn, gain, hi, lo, j, done):
        def sub(kt):
            dve.wait_ge(nh_ready, done + kt + 1)
            nc.vector.tensor_tensor(lo[:, kt, :], xn[:, kt % 2, :], hi[:, kt, :].bitcast(F32),
                                    ALU.subtract).then_inc(h_ready, 1)
        for kt in range(KT):
            if kt >= 2:
                dve.wait_ge(h_ready, done + kt - 1)
            nc.vector.scalar_tensor_tensor(out=xn[:, kt % 2, :], in0=x[:, kt, :], scalar=col(gain, kt),
                                           in1=rstd[:, :], op0=ALU.mult, op1=ALU.mult).then_inc(xn_ready, 1)
            if kt:
                sub(kt - 1)
        sub(KT - 1)

    def split_norm_act(act, xn, hi, j, done):
        for kt in range(KT):
            act.wait_ge(xn_ready, xn_after[j] + kt + 1)
            nc.scalar.activation(hi[:, kt, :], xn[:, kt % 2, :], ACT.Copy).then_inc(nh_ready, 1)

    def scale_x_dve(dve, x, gain, j):
        for kt in range(KT):
            nc.vector.scalar_tensor_tensor(out=x[:, kt, :], in0=x[:, kt, :], scalar=col(gain, kt),
                                           in1=rstd[:, :], op0=ALU.mult, op1=ALU.mult).then_inc(xn_ready, 1)

    xt_in = [sem(f"x_tokens_in{n}") for n in range(2)]
    xt_ready, xt_ev = sem("x_transposed"), sem("x_tile_copied")

    def turn_in_pool(pool):
        for t in range(NTOK):
            if t >= 2:
                pool.wait_ge(xt_ready, 4 * (t - 1))
            pool.dma_start(XB["xb_tok"][:, t % 2, :], inp["x"][0, t * P:(t + 1) * P, :]).then_inc(xt_in[t % 2], 16)


    def turn_in_pe(pe):
        pe.wait_ge(ident_in, 16)
        pe.wait_ge(made, 1)
        for n in range(4 * NTOK + 2):
            t, c = n // 4, n % 4
            if n < 4 * NTOK:
                pe.wait_ge(xt_in[t % 2], 16 * (t // 2 + 1))
                if n >= 4:
                    pe.wait_ge(xt_ev, n - 3)
                for k in range(4):
                    ins = nc.tensor.transpose(pm[n % 4][:, k * P:(k + 1) * P],
                                              XB["xb_tok"][:, t % 2, (4 * c + k) * P:(4 * c + k + 1) * P], ident[:, :])
                ins.then_inc(xt_ready, 1)
            if n == VECTORS_AFTER:
                pe.wait_ge(consts_in, 16 * NCONST)
                for r in range(2):
                    w = min(NROWS - r * P, P)
                    ins = nc.tensor.transpose(pg[3][:, r * P:r * P + w], rows[:w, r, :], ident[:w, :w])
                ins.then_inc(cols_turned, 1)
            if n >= 2:
                t, c = (n - 2) // 4, (n - 2) % 4
                if t == 3 and c == 0:
                    pe.wait_ge(cols_ready, 1)
                pe.wait_ge(sq_ready, n - 1)
                nc.tensor.matmul(pg[t][:, :], ones[:, :], XB["xb_sq"][:, n % 2, :], start=(c == 0),
                                 stop=(c == 3)).then_inc(rs_ready, 1)

    def turn_in_act(act):
        for n in range(4 * NTOK):
            t, c = n // 4, n % 4
            act.wait_ge(xt_ev, n + 1)
            if n >= 2:
                act.wait_ge(rs_ready, n - 1)
            nc.scalar.activation(XB["xb_sq"][:, n % 2, :].rearrange("p (k t) -> p k t", k=4),
                                 XB["xb"][:, 4 * c:4 * c + 4, t * P:(t + 1) * P], ACT.Square).then_inc(sq_ready, 1)
            if n == 4 * NTOK - 3:
                for piece in range(AHEAD):
                    split_hi(act, piece, piece % RING, 16)

    def turn_in_dve(dve):
        run = serial(dve, dve_seq)

        def add_up(t):
            dve.wait_ge(rs_ready, 4 * (t + 1))
            a = acc[:, t * P:(t + 1) * P]
            run(nc.vector.tensor_copy(a, pg[t][:, :P]))
            for k in range(1, 4):
                ins = nc.vector.tensor_tensor(a, a, pg[t][:, k * P:(k + 1) * P], ALU.add)
                run(ins) if k < 3 else ins.then_inc(acc_done, KT // NTOK)

        for n in range(4 * NTOK):
            t, c = n // 4, n % 4
            dve.wait_ge(xt_ready, n + 1)
            nc.vector.tensor_copy(XB["xb"][:, 4 * c:4 * c + 4, t * P:(t + 1) * P],
                                  pm[n % 4][:, :].rearrange("p (k t) -> p k t", k=4)).then_inc(xt_ev, 1)
            if n == VECTORS_AFTER:
                dve.wait_ge(cols_turned, 1)
                nc.vector.tensor_copy(cols[:, :NROWS], pg[3][:, :NROWS]).then_inc(cols_ready, 1)
            if n >= 7 and c == 3:
                add_up(t - 1)
        dve.wait_ge(cols_ready, 1)
        for piece in range(AHEAD):
            split_lo(dve, piece, piece % RING, 16)
        add_up(NTOK - 1)

    yt_out = [sem(f"y_tokens_out{n}") for n in range(2)]
    yt_ready, yt_ev = sem("y_transposed"), sem("y_tile_copied")

    def turn_out_pe(pe, x):
        pe.wait_ge(xn_ready, xn_after[6])
        for n in range(4 * NTOK):
            t, c = n // 4, n % 4
            if n >= 3:
                pe.wait_ge(yt_ev, n - 2)
            for k in range(4):
                ins = nc.tensor.transpose(pm[1 + n % 3][:, k * P:(k + 1) * P], x[:, 4 * c + k, t * P:(t + 1) * P],
                                          ident[:, :])
            ins.then_inc(yt_ready, 1)

    def turn_out_act(act, tok):
        for n in range(4 * NTOK):
            t, c = n // 4, n % 4
            act.wait_ge(yt_ready, n + 1)
            if t >= 2:
                act.wait_ge(yt_out[t % 2], 16 * (t // 2))
            nc.scalar.activation(tok[:, t % 2, 4 * c * P:4 * (c + 1) * P], pm[1 + n % 3][:, :], ACT.Copy).then_inc(yt_ev, 1)

    def turn_out_pool(pool, tok):
        for t in range(NTOK):
            pool.wait_ge(yt_ev, 4 * (t + 1))
            pool.dma_start(out[0, t * P:(t + 1) * P, :], tok[:, t % 2, :]).then_inc(yt_out[t % 2], 16)
        for n in range(2):
            pool.wait_ge(yt_out[n], 16 * (NTOK // 2))

    def store_x(pool, x, n):
        pool.wait_ge(acc_done, {0: 16, 1: 32, 2: 64, 3: 80}[n])
        pool.dma_start(xds[n].rearrange("(k p) t -> p k t", p=P), x[:, :, :]).then_inc(x_stored, 16)

    def pool_end(pool, n):
        for m in range(MT):
            pool.wait_ge(stored[m], 16 * sum(r.blocks for _, rs in PHASES[:n + 1] for r in rs if m < r.banks and r.dst is not None))
        pool.wait_ge(x_stored, 16 * {0: 1, 2: 2, 5: 3, 7: 4, 9: 4}[n])

    LEVELS = 8
    V0 = overlay(HALF, [
        ("g_q", [2, L], F32), ("g_k", [2, L], F32), ("g_v", [2, NTOK, GDV], F32), ("g_gate", [2, 2, L], F32),
        ("g_z", [L], F32), ("g_m", [L], F32), ("g_b", [L], F32), ("g_e", [2, L], F32),
        ("g_qe", [2, L], F32), ("g_ke", [2, L], F32), ("g_s", [NTOK, P], F32), ("g_qb", [L], F32),
        ("g_kd", [L], F32), ("g_kt", [NTOK, P], F32), ("g_state", [2, GDV], F32), ("g_sq", [2, L], F32),
        ("g_o", [2, L], F32), ("g_one", [P], F32), ("g_last4", [NTOK], F32)])
    EX0 = overlay(EXTRA, [("g_lr", [L], F32), ("g_up", [L], F32), ("g_masks", [LEVELS, P], F32)])
    gla_in = [sem(f"gla_head_in{n}") for n in range(2)]
    shared_in = sem("shared_operands_in")
    gz_ready, gz_read, gln_ready, gdl_ready = sem("gla_gate_ready"), sem("gla_gate_read"), sem("gla_ln_ready"), sem("gla_b_ready")
    ged_ready, gkd_ready, gkt_ready, gktok_ready = sem("gla_decays"), sem("gla_kd"), sem("gla_kd_turned"), sem("gla_kd_copied")
    gd_ready, gE_ready, gq_ready, gk_ready = sem("gla_level_diff"), sem("gla_level_exp"), sem("gla_level_q"), sem("gla_level_k")
    gs_ready, gsel_done = sem("gla_level_scores"), sem("gla_level_picked")
    gkv_ready, gst_ready, go_ready = sem("gla_kv"), sem("gla_state"), sem("gla_out")
    gsq_ready, gss_ready, gsd_ready, gf_ready, gf_hi, gf_lo = (sem("gla_out_sq"), sem("gla_out_sum"), sem("gla_out_dev"),
                                                               sem("gla_fin"), sem("gla_fin_hi"), sem("gla_fin_lo"))

    ff_in, ff_read, ff_ln, ff_neg, negc_stored, fb_ready = (sem("forget_in"), sem("forget_read"), sem("forget_ln"),
                                                            sem("forget_sums"), sem("forget_stored"), sem("forget_bias"))
    ff_z, ff_t, ff_c, ff_one = (stage[:FH, m, :] for m in range(4))

    def forget_read(dve):
        run = serial(dve, dve_seq)
        run(nc.vector.memset(ff_one, 1.0))
        dve.wait_ge(ff_in, 16)
        nc.vector.tensor_scalar(ff_z, ff_z, cols[:FH, COL["f_b"]:COL["f_b"] + 1], None, ALU.add).then_inc(ff_read, 1)

    def forget_sums(dve):
        run = serial(dve, dve_seq)
        dve.wait_ge(ff_ln, 1)
        run(nc.vector.tensor_scalar(ff_z, ff_z, 0.0, None, ALU.min))
        run(nc.vector.tensor_tensor(ff_z, ff_z, ff_t, ALU.subtract))
        run(nc.vector.tensor_tensor_scan(ff_c, ff_one, ff_z, 0.0, ALU.mult, ALU.add))
        nc.vector.tensor_scalar(ff_c, ff_c, -FD ** 0.5, None, ALU.mult).then_inc(ff_neg, 1)

    def gla_pool(pool):
        pool.dma_start(EX0["g_lr"][:GRANK, :], zt[ZT["lr"]:ZT["lr"] + GRANK, :]).then_inc(shared_in, 16)
        pool.dma_start(EX0["g_up"][:GRANK, :], inp["gla_alpha_up"][0]).then_inc(shared_in, 16)
        pool.dma_start(EX0["g_masks"][:, :, :], inp["masks"].rearrange("p (l j) -> p l j", l=LEVELS)).then_inc(shared_in, 16)
        def load_head(h):
            s = h % 2
            if h >= 2:
                pool.wait_ge(gf_lo, 2 * (h - 1))
            pool.dma_start(V0["g_q"][:, s, :], zt[ZT["q"] + h * P:ZT["q"] + (h + 1) * P, :]).then_inc(gla_in[s], 16)
            pool.dma_start(V0["g_k"][:, s, :], zt[ZT["k"] + h * P:ZT["k"] + (h + 1) * P, :]).then_inc(gla_in[s], 16)
            pool.dma_start(V0["g_v"][:, s, :, :], zn[:, ZN["v"] + h * GDV:ZN["v"] + (h + 1) * GDV].rearrange(
                "(t p) c -> p t c", p=P)).then_inc(gla_in[s], 16)
            pool.dma_start(V0["g_gate"][:, s, :, :], zt[ZT["gate"] + h * GDV:ZT["gate"] + (h + 1) * GDV, :].rearrange(
                "(e p) t -> p e t", p=P)).then_inc(gla_in[s], 16)

        load_head(0)
        for h in range(GH):
            s = h % 2
            pool.wait_ge(gla_in[s], 64 * (h // 2 + 1))
            for lv in range(1, LEVELS):
                n = 7 * h + lv - 1
                pool.wait_ge(gE_ready, n + 1)
                if n >= 2:
                    pool.wait_ge(gs_ready, LEVELS * h + lv - 1 if lv > 2 else LEVELS * h)
                nc.gpsimd.tensor_tensor(V0["g_ke"][:, n % 2, :], V0["g_k"][:, s, :], V0["g_e"][:, n % 2, :],
                                        ALU.mult).then_inc(gk_ready, 1)
                if lv == 2 and h + 1 < GH:
                    load_head(h + 1)
                if lv == 3 and h == 0:
                    pool.dma_start(ff_z, zt[ZT["ff"]:ZT["ff"] + FH, :]).then_inc(ff_in, 16)
        pool.wait_ge(ff_neg, 1)
        pool.dma_start(negc_dram[:, :], ff_c).then_inc(negc_stored, 16)

    def gla_pe(pe):
        pe.wait_ge(shared_in, 48)

        def gate_logits(h):
            if h:
                pe.wait_ge(gz_read, h)
            nc.tensor.matmul(pm[0][:, :], EX0["g_up"][:GRANK, h * P:(h + 1) * P], EX0["g_lr"][:GRANK, :],
                             start=True, stop=True).then_inc(gz_ready, 1)

        gate_logits(0)
        for h in range(GH):
            s = h % 2
            pe.wait_ge(gkd_ready, h + 1)
            if h:
                pe.wait_ge(gktok_ready, h)
            for c in range(NTOK):
                ins = nc.tensor.transpose(pm[1][:, c * P:(c + 1) * P], V0["g_kd"][:, c * P:(c + 1) * P], ident[:, :])
            ins.then_inc(gkt_ready, 1)
            if h + 1 < GH:
                gate_logits(h + 1)
            for lv in range(LEVELS):
                n = LEVELS * h + lv
                e = 7 * h + lv - 1
                if lv:
                    pe.wait_ge(gq_ready, 8 * h + lv + 1)
                    pe.wait_ge(gk_ready, e + 1)
                    q, k = V0["g_qe"][:, e % 2, :], V0["g_ke"][:, e % 2, :]
                else:
                    pe.wait_ge(gla_in[s], 64 * (h // 2 + 1))
                    pe.wait_ge(gq_ready, 8 * h + 1)
                    q, k = V0["g_q"][:, s, :], V0["g_k"][:, s, :]
                if n >= 2:
                    pe.wait_ge(gsel_done, n - 1)
                for c in range(NTOK):
                    ins = nc.tensor.matmul(pm[2 + n % 2][:, c * P:(c + 1) * P], k[:, c * P:(c + 1) * P],
                                           q[:, c * P:(c + 1) * P], start=True, stop=True)
                ins.then_inc(gs_ready, 1)
            pe.wait_ge(gsel_done, LEVELS * (h + 1))
            pe.wait_ge(gktok_ready, h + 1)
            if h:
                pe.wait_ge(gf_ready, 2 * h)
            for c in range(NTOK):
                if c or h:
                    pe.wait_ge(gst_ready, 3 * h + c)
                if c < NTOK - 1:
                    nc.tensor.matmul(pg[2][:, :GDV], V0["g_kt"][:, c, :], V0["g_v"][:, s, c, :],
                                     start=True, stop=True).then_inc(gkv_ready, 1)
                for e in range(2):
                    ins = nc.tensor.matmul(pg[e][:, c * P:(c + 1) * P], V0["g_v"][:, s, c, e * P:(e + 1) * P],
                                           V0["g_s"][:, c, :], start=True, stop=(c == 0))
                    if c:
                        ins = nc.tensor.matmul(pg[e][:, c * P:(c + 1) * P],
                                               V0["g_state"][:, (c - 1) % 2, e * P:(e + 1) * P],
                                               V0["g_qb"][:, c * P:(c + 1) * P], start=False, stop=True)
                if c == NTOK - 1:
                    ins.then_inc(go_ready, 1)
            pe.wait_ge(gsq_ready, 2 * (h + 1))
            if h:
                pe.wait_ge(gsd_ready, h)
            for e in range(2):
                ins = nc.tensor.matmul(pg[3][:, :], ones[:, :], V0["g_sq"][:, e, :], start=(e == 0), stop=(e == 1))
            ins.then_inc(gss_ready, 1)

    def gla_act(act):
        run = serial(act, act_seq)

        def gate_ln(h):
            act.wait_ge(gz_read, h + 1)
            run(nc.scalar.activation(V0["g_m"][:, :], V0["g_z"][:, :], ACT.Abs))
            forget = h == GH - 1
            if forget:
                act.wait_ge(ff_read, 1)
                run(nc.scalar.activation(ff_t, ff_z, ACT.Abs))
                run(nc.scalar.activation(ff_t, ff_t, ACT.Exp, scale=-1.0))
            run(nc.scalar.activation(V0["g_m"][:, :], V0["g_m"][:, :], ACT.Exp, scale=-1.0))
            nc.scalar.activation(V0["g_m"][:, :], V0["g_m"][:, :], ACT.Ln, bias=V0["g_one"][:, 0:1]).then_inc(gln_ready, 1)
            if forget:
                nc.scalar.activation(ff_t, ff_t, ACT.Ln, bias=onecol[:FH, 0:1]).then_inc(ff_ln, 1)

        def chunk_decays(h):
            act.wait_ge(gdl_ready, h + 1)
            if h:
                act.wait_ge(go_ready, h)
            run(nc.scalar.activation(V0["g_qb"][:, :], V0["g_b"][:, :], ACT.Exp))
            nc.scalar.activation(V0["g_kd"][:, :], V0["g_kd"][:, :], ACT.Exp, scale=-1.0).then_inc(ged_ready, 1)

        def copy_kt(h):
            act.wait_ge(gkt_ready, h + 1)
            nc.scalar.activation(V0["g_kt"][:, :, :], pm[1][:, :], ACT.Copy).then_inc(gktok_ready, 1)

        def level_decay(h, lv):
            n = 7 * h + lv - 1
            act.wait_ge(gd_ready, n + 1)
            run(nc.scalar.activation(V0["g_e"][:, n % 2, :], V0["g_e"][:, n % 2, :], ACT.Abs))
            nc.scalar.activation(V0["g_e"][:, n % 2, :], V0["g_e"][:, n % 2, :], ACT.Exp, scale=-1.0).then_inc(gE_ready, 1)

        gate_ln(0)
        chunk_decays(0)
        copy_kt(0)
        level_decay(0, 1)
        for h in range(GH):
            for lv in range(2, LEVELS):
                level_decay(h, lv)
            if h + 1 < GH:
                gate_ln(h + 1)
            act.wait_ge(go_ready, h + 1)
            if h:
                act.wait_ge(gss_ready, h)
            for e in range(2):
                nc.scalar.activation(V0["g_sq"][:, e, :], pg[e][:, :], ACT.Square).then_inc(gsq_ready, 1)
            if h + 1 < GH:
                chunk_decays(h + 1)
            act.wait_ge(gss_ready, h + 1)
            if h:
                act.wait_ge(gf_ready, 2 * h)
            nc.scalar.activation(rstd[:, :], pg[3][:, :], ACT.Sqrt, scale=1.0 / GDV, bias=eps[:, 0:1]).then_inc(gsd_ready, 1)
            if h + 1 < GH:
                copy_kt(h + 1)
                level_decay(h + 1, 1)
            for e in range(2):
                act.wait_ge(gf_ready, 2 * h + e + 1)
                nc.scalar.activation(A["a_hi"][:, 2 * h + e, :], V0["g_o"][:, e, :], ACT.Copy).then_inc(gf_hi, 1)

    def gla_dve(dve):
        run = serial(dve, dve_seq)
        vec = nc.vector
        tt = vec.tensor_tensor
        run(vec.memset(V0["g_one"][:, :], 1.0))
        dve.wait_ge(shared_in, 48)

        def start_head(h):
            s = h % 2
            dve.wait_ge(gz_ready, h + 1)
            vec.tensor_scalar(V0["g_z"][:, :], pm[0][:, :], col("alpha_b", h), None, ALU.add).then_inc(gz_read, 1)
            dve.wait_ge(gz_read, h + 1)
            dve.wait_ge(gla_in[s], 64 * (h // 2 + 1))
            if h:
                dve.wait_ge(gE_ready, 7 * h)
            vec.tensor_scalar(V0["g_q"][:, s, :], V0["g_q"][:, s, :], GDK ** -0.5, None, ALU.mult).then_inc(gq_ready, 1)

        def log_decays(h):
            dve.wait_ge(gln_ready, h + 1)
            run(vec.tensor_scalar(V0["g_z"][:, :], V0["g_z"][:, :], 0.0, 1.0 / GTAU, ALU.min, ALU.mult))
            run(vec.scalar_tensor_tensor(out=V0["g_z"][:, :], in0=V0["g_m"][:, :], scalar=-1.0 / GTAU,
                                         in1=V0["g_z"][:, :], op0=ALU.mult, op1=ALU.add))
            for c in range(NTOK):
                cs = slice(c * P, (c + 1) * P)
                run(vec.tensor_tensor_scan(V0["g_b"][:, cs], V0["g_one"][:, :], V0["g_z"][:, cs], 0.0, ALU.mult, ALU.add))
            b3 = V0["g_b"][:, :].rearrange("p (c t) -> p c t", t=P)
            tt(V0["g_kd"][:, :].rearrange("p (c t) -> p c t", t=P), b3, b3[:, :, P - 1:P].broadcast_to([P, NTOK, P]),
               ALU.subtract).then_inc(gdl_ready, 1)

        def decayed(h):
            s = h % 2
            dve.wait_ge(ged_ready, h + 1)
            dve.wait_ge(gq_ready, 8 * h + 1)
            run(vec.tensor_copy(V0["g_last4"][:, :], V0["g_qb"][:, :].rearrange("p (c t) -> p c t", t=P)[:, :, P - 1]))
            run(tt(V0["g_qb"][:, :], V0["g_qb"][:, :], V0["g_q"][:, s, :], ALU.mult))
            tt(V0["g_kd"][:, :], V0["g_kd"][:, :], V0["g_k"][:, s, :], ALU.mult).then_inc(gkd_ready, 1)

        def diff(h, lv):
            n = 7 * h + lv - 1
            step = 2 ** (lv - 1)
            if n >= 2:
                dve.wait_ge(gq_ready, 8 * h + lv - 1 if lv > 2 else 8 * h)
                dve.wait_ge(gk_ready, n - 1)
            v = V0["g_b"][:, :].rearrange("p (c t) -> p c t", t=2 * step)
            tt(V0["g_e"][:, n % 2, :].rearrange("p (c t) -> p c t", t=2 * step), v,
               v[:, :, step - 1:step].broadcast_to([P, L // (2 * step), 2 * step]), ALU.subtract).then_inc(gd_ready, 1)

        start_head(0)
        log_decays(0)
        decayed(0)
        diff(0, 1)
        for h in range(GH):
            s = h % 2

            def pick(lv):
                n = LEVELS * h + lv
                dve.wait_ge(gs_ready, n + 1)
                scores = pm[2 + n % 2][:, :].rearrange("p (c t) -> p c t", t=P)
                mask = EX0["g_masks"][:, lv:lv + 1, :].broadcast_to([P, NTOK, P])
                if lv == 0:
                    if h:
                        dve.wait_ge(go_ready, h)
                    tt(V0["g_s"][:, :, :], scores, mask, ALU.mult).then_inc(gsel_done, 1)
                else:
                    dve.wait_ge(gsel_done, n)
                    vec.copy_predicated(V0["g_s"][:, :, :], mask.bitcast(I32), scores).then_inc(gsel_done, 1)

            for lv in range(1, LEVELS + 1):
                if lv + 1 < LEVELS:
                    diff(h, lv + 1)
                if lv < LEVELS:
                    n = 7 * h + lv - 1
                    dve.wait_ge(gE_ready, n + 1)
                    if n >= 2:
                        dve.wait_ge(gs_ready, LEVELS * h + lv - 1 if lv > 2 else LEVELS * h)
                    tt(V0["g_qe"][:, n % 2, :], V0["g_q"][:, s, :], V0["g_e"][:, n % 2, :], ALU.mult).then_inc(gq_ready, 1)
                pick(lv - 1)
            if h + 1 == GH - 1:
                forget_read(dve)
            if h + 1 < GH:
                start_head(h + 1)
            for c in range(NTOK - 1):
                dve.wait_ge(gkv_ready, 3 * h + c + 1)
                if c == 0:
                    vec.tensor_copy(V0["g_state"][:, 0, :], pg[2][:, :GDV]).then_inc(gst_ready, 1)
                else:
                    dve.wait_ge(gst_ready, 3 * h + c)
                    vec.scalar_tensor_tensor(out=V0["g_state"][:, c % 2, :], in0=V0["g_state"][:, (c - 1) % 2, :],
                                             scalar=V0["g_last4"][:, c:c + 1], in1=pg[2][:, :GDV],
                                             op0=ALU.mult, op1=ALU.add).then_inc(gst_ready, 1)
            if h + 1 < GH:
                dve.wait_ge(gst_ready, 3 * (h + 1))
                log_decays(h + 1)
                decayed(h + 1)
                diff(h + 1, 1)
            if h + 1 == GH - 1:
                forget_sums(dve)
            dve.wait_ge(gsd_ready, h + 1)
            run(vec.reciprocal(rstd[:, :], rstd[:, :]))
            for e in range(2):
                if h:
                    dve.wait_ge(gf_lo, 2 * (h - 1) + e + 1)
                run(vec.scalar_tensor_tensor(out=V0["g_o"][:, e, :], in0=pg[e][:, :], scalar=col("head_g", 2 * h + e),
                                             in1=rstd[:, :], op0=ALU.mult, op1=ALU.mult))
                tt(V0["g_o"][:, e, :], V0["g_o"][:, e, :], V0["g_gate"][:, s, e, :], ALU.mult).then_inc(gf_ready, 1)
            for e in range(2):
                dve.wait_ge(gf_hi, 2 * h + e + 1)
                tt(A["a_lo"][:, 2 * h + e, :], V0["g_o"][:, e, :], A["a_hi"][:, 2 * h + e, :].bitcast(F32),
                   ALU.subtract).then_inc(gf_lo, 1)

    att = dict(
        scores=sem("scores_ready"), nmax=sem("negated_max_ready"), probs=sem("exp_ready"), normed=sem("probs_normed"),
        turned=sem("probs_turned"), copied=sem("turned_copied"), pv=sem("pv_ready"), tile=sem("tile_gated"),
        hi=sem("tile_hi"), lo=sem("tile_lo"), sq=sem("tile_squares"), ss=sem("tile_square_sum"), sd=sem("tile_deviation"))
    att_in = [sem(f"attention_tile_in{n}") for n in range(2)]
    gate_in = [sem(f"attention_gate_in{n}") for n in range(2)]

    def head_rows(name):
        return lambda t: zt[ZT[name] + t * P:ZT[name] + (t + 1) * P, :]

    def place(a, j):
        return j // a.per, j // NTOK % a.heads, j % NTOK

    def att_pe(pe, a):
        def scores(u):
            t, h, qb = place(a, u // a.comps)
            n = a.units0 + u
            pe.wait_ge(att_in[t % 2], a.in0 + a.loads[1] * (t // 2 + 1))
            if n >= 2:
                pe.wait_ge(att["nmax"], n - 1)
            first, count = a.key_tiles(qb)
            ops = a.products(t, h, u % a.comps, qb, first, count)
            for i, (lhsT, rhs) in enumerate(ops):
                ins = nc.tensor.matmul(pm[n % 2][:, :count * P], lhsT, rhs, start=(i == 0), stop=(i == len(ops) - 1))
            ins.then_inc(att["scores"], 1)

        def turn(j):
            _, count = a.key_tiles(place(a, j)[2])
            n = a.jobs0 + j
            u = a.units0 + (j + 1) * a.comps
            pe.wait_ge(att["normed"], u)
            if n >= 2:
                pe.wait_ge(att["copied"], n - 1)
            for b in range(count):
                ins = nc.tensor.transpose(pm[2 + n % 2][:, b * P:(b + 1) * P],
                                          a.buf["p"][:, (u - 1) % 4, b * P:(b + 1) * P], ident[:, :])
            ins.then_inc(att["turned"], 1)

        def pv(j):
            t, h, qb = place(a, j)
            first, count = a.key_tiles(qb)
            n = a.jobs0 + j
            pe.wait_ge(att["copied"], n + 1)
            if a.tiles0 + t >= 2:
                pe.wait_ge(att["tile"], a.tiles0 + t - 1)
            rows = slice(h * a.dv, (h + 1) * a.dv)
            for b in range(count):
                ins = nc.tensor.matmul(pg[(a.tiles0 + t) % 2][rows, qb * P:(qb + 1) * P], a.value(t, h, first + b),
                                       a.buf["pt"][:, n % 2, b * P:(b + 1) * P], start=(b == 0), stop=(b == count - 1))
            ins.then_inc(att["pv"], 1)

        def square_sum(t):
            pe.wait_ge(att["sq"], t + 1)
            if t:
                pe.wait_ge(att["sd"], t)
            nc.tensor.matmul(pg[2][:, :], ones[:, :], a.buf["sq"][:, :], start=True, stop=True).then_inc(att["ss"], 1)

        for j in range(a.jobs + 4):
            for c in range(a.comps):
                if j < a.jobs:
                    scores(j * a.comps + c)
            if 2 <= j <= a.jobs + 1:
                turn(j - 2)
            if 3 <= j < a.jobs + 3:
                pv(j - 3)
            if a.gain is not None and j >= a.per + 3 and (j - 3) % a.per == 0:
                square_sum((j - 3) // a.per - 1)

    def att_act(act, a):
        run = serial(act, act_seq)

        def exp(u):
            n = a.units0 + u
            t, h, _ = place(a, u // a.comps)
            first, count = a.key_tiles(place(a, u // a.comps)[2])
            act.wait_ge(att["nmax"], n + 1)
            s = n % 4
            if a.sink is not None:
                run(nc.scalar.activation(a.buf["small"][:, 12 + s:13 + s], a.sink(t, h), ACT.Exp,
                                         bias=a.buf["small"][:, s:s + 1]))
            p = a.buf["p"][:, s, :count * P]
            nc.scalar.activation(p, p, ACT.Exp, bias=a.buf["small"][:, s:s + 1],
                                 accum_out=a.buf["small"][:, 4 + s:5 + s]).then_inc(att["probs"], 1)

        def copy(j):
            n = a.jobs0 + j
            _, count = a.key_tiles(place(a, j)[2])
            act.wait_ge(att["turned"], n + 1)
            if n >= 2:
                act.wait_ge(att["pv"], n - 1)
            nc.scalar.activation(a.buf["pt"][:, n % 2, :count * P], pm[2 + n % 2][:, :count * P],
                                 ACT.Copy).then_inc(att["copied"], 1)

        def squares(t):
            n = a.tiles0 + t
            if a.gain is not None:
                act.wait_ge(att["pv"], a.jobs0 + (t + 1) * a.per)
                if t:
                    act.wait_ge(att["ss"], t)
                nc.scalar.activation(a.buf["sq"][:, :], pg[n % 2][:, :], ACT.Square).then_inc(att["sq"], 1)

        def round_tile(t):
            n = a.tiles0 + t
            if a.gain is not None:
                act.wait_ge(att["ss"], t + 1)
                if t:
                    act.wait_ge(att["tile"], n)
                nc.scalar.activation(rstd[:, :], pg[2][:, :], ACT.Sqrt, scale=1.0 / P, bias=eps[:, 0:1]).then_inc(att["sd"], 1)
            act.wait_ge(att["tile"], n + 1)
            nc.scalar.activation(a.hi[:, a.kt0 + t, :], a.buf["o"][:, t % 2, :], ACT.Copy).then_inc(att["hi"], 1)

        for j in range(a.jobs + 6):
            if j < a.jobs:
                for c in range(a.comps):
                    exp(j * a.comps + c)
            if 2 <= j <= a.jobs + 1:
                copy(j - 2)
            if j >= a.per + 3 and (j - 3) % a.per == 0:
                squares((j - 3) // a.per - 1)
            if j >= a.per + 5 and (j - 5) % a.per == 0:
                round_tile((j - 5) // a.per - 1)

    def att_dve(dve, a):
        run = serial(dve, dve_seq)
        vec = nc.vector
        small = a.buf["small"]

        def maxes(u):
            n = a.units0 + u
            t, h, qb = place(a, u // a.comps)
            s = n % 4
            _, count = a.key_tiles(qb)
            dve.wait_ge(att["scores"], n + 1)
            if n >= 4:
                dve.wait_ge(att["turned"], a.jobs0 + (u - 4) // a.comps + 1 if u >= 4 else a.jobs0)
            if a.bias_ready is not None and u % (a.per * a.comps) == 0:
                a.bias_ready(dve, t)
            run(vec.tensor_tensor_reduce(out=a.buf["p"][:, s, :count * P], in0=pm[n % 2][:, :count * P],
                                         in1=a.bias(t, qb, count), scale=a.scale, scalar=LOWEST, op0=ALU.add,
                                         op1=ALU.max, accum_out=small[:, 8 + s:9 + s]))
            vec.tensor_scalar(small[:, s:s + 1], small[:, 8 + s:9 + s], a.sink(t, h) if a.sink is not None else LOWEST, -1.0,
                              ALU.max, ALU.mult).then_inc(att["nmax"], 1)

        def norm(u):
            n = a.units0 + u
            _, count = a.key_tiles(place(a, u // a.comps)[2])
            s = n % 4
            p = a.buf["p"][:, s, :count * P]
            dve.wait_ge(att["probs"], n + 1)
            if a.sink is not None:
                run(vec.tensor_tensor(small[:, 4 + s:5 + s], small[:, 4 + s:5 + s], small[:, 12 + s:13 + s], ALU.add))
            run(vec.reciprocal(small[:, 8 + s:9 + s], small[:, 4 + s:5 + s]))
            if u % a.comps == 0:
                vec.tensor_scalar(p, p, small[:, 8 + s:9 + s], None, ALU.mult).then_inc(att["normed"], 1)
            else:
                run(vec.tensor_tensor(small[:, 8 + s:9 + s], small[:, 8 + s:9 + s], a.lam, ALU.mult))
                dve.wait_ge(att["normed"], n)
                vec.scalar_tensor_tensor(out=p, in0=p, scalar=small[:, 8 + s:9 + s],
                                         in1=a.buf["p"][:, (n - 1) % 4, :count * P], op0=ALU.mult,
                                         op1=ALU.add).then_inc(att["normed"], 1)

        def gate(t):
            n = a.tiles0 + t
            if n >= 2:
                dve.wait_ge(att["lo"], n - 1)
            o = a.buf["o"][:, t % 2, :]
            dve.wait_ge(gate_in[t % 2], 16 * (n // 2 + 1))
            if a.gain is not None:
                dve.wait_ge(att["sd"], t + 1)
                run(vec.reciprocal(rstd[:, :], rstd[:, :]))
                run(vec.scalar_tensor_tensor(out=o, in0=pg[n % 2][:, :], scalar=a.gain, in1=rstd[:, :],
                                             op0=ALU.mult, op1=ALU.mult))
                vec.tensor_tensor(o, o, a.gate(t), ALU.mult).then_inc(att["tile"], 1)
            else:
                dve.wait_ge(att["pv"], a.jobs0 + (t + 1) * a.per)
                vec.tensor_tensor(o, pg[n % 2][:, :], a.gate(t), ALU.mult).then_inc(att["tile"], 1)

        def low(t):
            n = a.tiles0 + t
            dve.wait_ge(att["hi"], n + 1)
            vec.tensor_tensor(a.lo[:, a.kt0 + t, :], a.buf["o"][:, t % 2, :], a.hi[:, a.kt0 + t, :].bitcast(F32),
                              ALU.subtract).then_inc(att["lo"], 1)

        for j in range(a.jobs + 7):
            if j < a.jobs:
                for c in range(a.comps):
                    maxes(j * a.comps + c)
            if 1 <= j <= a.jobs:
                for c in range(a.comps):
                    norm((j - 1) * a.comps + c)
            if j >= a.per + 5 and (j - 5) % a.per == 0:
                gate((j - 5) // a.per - 1)
            if j >= a.per + 6 and (j - 6) % a.per == 0:
                low((j - 6) // a.per - 1)

    def att_pool(pool, a):
        def load_gate(t):
            n = a.tiles0 + t
            if n >= 2:
                pool.wait_ge(att["tile"], n - 1)
            pool.dma_start(a.gate(t), a.gate_of(t)).then_inc(gate_in[t % 2], 16)

        for t in range(a.tiles):
            for_scores, values = a.loads[0](t)
            before = max(t - 1, 0) * a.per
            if a.tiles0 + t >= 2:
                pool.wait_ge(att["nmax"], a.units0 + before * a.comps)
            for dst, src in for_scores:
                pool.dma_start(dst, src).then_inc(att_in[t % 2], 16)
            if a.pool_work is not None:
                a.pool_work(pool, t)
            if values and a.tiles0 + t >= 2:
                pool.wait_ge(att["pv"], a.jobs0 + before)
            for dst, src in values:
                pool.dma_start(dst, src).then_inc(att_in[t % 2], 16)
            if t:
                load_gate(t - 1)
        load_gate(a.tiles - 1)

    V1 = overlay(HALF, [
        ("f_p", [4, L], F32), ("f_pt", [2, L], F32), ("f_o", [2, L], F32), ("f_q", [2, L], F32),
        ("f_k", [2, L], F32), ("f_v", [2, NTOK, FD], F32), ("f_gate", [2, L], F32), ("f_nc", [2, L], F32),
        ("f_small", [16], F32), ("f_bias", [2, 10 * P], F32)])
    def fox_loads(t):
        s = t % 2
        rows = lambda name: zt[ZT[name] + t * P:ZT[name] + (t + 1) * P, :]
        return ([(V1["f_nc"][:, s, :], negc_dram[t:t + 1, :].broadcast_to([P, L])),
                 (V1["f_q"][:, s, :], rows("fq")), (V1["f_k"][:, s, :], rows("fk"))],
                [(V1["f_v"][:, s, :, :], zn[:, ZN["fv"] + t * FD:ZN["fv"] + (t + 1) * FD].rearrange("(b p) c -> p b c", p=P))])

    def fox_bias_pool(pool, t):
        pool.wait_ge(att_in[t % 2], 64 * (t // 2) + 48)
        for qb in range(NTOK):
            at = qb * (qb + 1) // 2 * P
            ins = nc.gpsimd.tensor_tensor(V1["f_bias"][:, t % 2, at:at + (qb + 1) * P], V1["f_nc"][:, t % 2, :(qb + 1) * P],
                                          wide[:, (NTOK - 1 - qb) * P:], ALU.add)
            ins.then_inc(fb_ready, 1)

    FOX = Attention(
        buf=dict(p=V1["f_p"], pt=V1["f_pt"], o=V1["f_o"], small=V1["f_small"]), tiles=FH, heads=1, comps=1, dv=FD,
        scale=FD ** -0.5, key_tiles=lambda qb: (0, qb + 1),
        products=lambda t, h, c, qb, first, count: [(V1["f_q"][:, t % 2, qb * P:(qb + 1) * P],
                                                     V1["f_k"][:, t % 2, :count * P])],
        bias=lambda t, qb, count: V1["f_bias"][:, t % 2, qb * (qb + 1) // 2 * P:(qb * (qb + 1) // 2 + count) * P],
        bias_ready=lambda dve, t: dve.wait_ge(fb_ready, NTOK * (t + 1)), pool_work=fox_bias_pool,
        value=lambda t, h, b: V1["f_v"][:, t % 2, b, :], gate=lambda t: V1["f_gate"][:, t % 2, :], kt0=KT // 2,
        loads=(fox_loads, 64), gate_of=head_rows("fgate"), hi=A["a_hi"], lo=A["a_lo"], units0=0, jobs0=0, tiles0=0, in0=0,
        sink=None, lam=None, gain=None)

    V2 = overlay(0, [
        ("r_x", [2, L + CW - 1], F32), ("r_gate", [4, L], F32), ("r_y", [4, L], F32), ("r_i", [4, L], F32),
        ("r_r", [4, L], F32), ("r_a", [4, L], F32), ("r_m", [2, L], F32), ("r_h", [L], F32),
        ("r_o", [2, L], F32), ("r_gx", [RB, P], F32), ("r_ga", [RB, P], F32), ("r_sp", [6, RB], F32)])
    ru_in = [sem(f"lru_tile_in{n}") for n in range(2)]
    ru_e, ru_sp, ru_y, ru_g, ru_s, ru_a, ru_m, ru_q, ru_o, ru_hi, ru_lo = (sem(f"lru_{n}") for n in (
        "exp_lambda", "softplus", "conv", "gate_sums", "gates", "decay", "gain", "gain_root", "out", "out_hi", "out_lo"))

    def lru_pool(pool):
        pool.dma_start(V2["r_gx"][:, :, :], inp["l0_gate_x_w_2"].rearrange("n d e -> d n e")).then_inc(shared_in, 16)
        pool.dma_start(V2["r_ga"][:, :, :], inp["l0_gate_a_w_2"].rearrange("n d e -> d n e")).then_inc(shared_in, 16)
        pool.wait_ge(ru_e, 2)
        for n in range(RB):
            s = n % 2
            if n >= 2:
                pool.wait_ge(ru_y, n - 1)
            if n >= 4:
                pool.wait_ge(ru_o, n - 3)
            pool.dma_start(V2["r_x"][:, s, CW - 1:], zt[ZT["rx"] + n * P:ZT["rx"] + (n + 1) * P, :]).then_inc(ru_in[s], 16)
            pool.dma_start(V2["r_gate"][:, n % 4, :], zt[ZT["rgate"] + n * P:ZT["rgate"] + (n + 1) * P, :]).then_inc(ru_in[s], 16)

    def lru_pe(pe):
        pe.wait_ge(shared_in, 80)
        for n in range(RB):
            pe.wait_ge(ru_y, n + 1)
            if n >= 2:
                pe.wait_ge(ru_s, 2 * (n - 1))
            nc.tensor.matmul(pm[2 * (n % 2)][:, :], V2["r_gx"][:, n, :], V2["r_y"][:, n % 4, :], start=True, stop=True)
            nc.tensor.matmul(pm[2 * (n % 2) + 1][:, :], V2["r_ga"][:, n, :], V2["r_y"][:, n % 4, :],
                             start=True, stop=True).then_inc(ru_g, 1)

    def lru_act(act):
        sp = V2["r_sp"]
        run = serial(act, act_seq)
        act.wait_ge(ru_e, 3)
        run(nc.scalar.activation(sp[:, 0, :], cols[:, COL["lam"]:COL["lam"] + RB], ACT.Abs))
        nc.scalar.activation(sp[:, 0, :], sp[:, 0, :], ACT.Exp, scale=-1.0).then_inc(ru_e, 1)
        for pair in range(RB // 2 + 1):
            now = range(2 * pair, 2 * pair + 2)
            if pair < RB // 2:
                for n in now:
                    act.wait_ge(ru_g, n + 1)
                    if n >= 4:
                        act.wait_ge(ru_o, n - 3)
                    nc.scalar.activation(V2["r_i"][:, n % 4, :], pm[2 * (n % 2)][:, :], ACT.Sigmoid, bias=col("gx_b", n)).then_inc(ru_s, 1)
                    nc.scalar.activation(V2["r_r"][:, n % 4, :], pm[2 * (n % 2) + 1][:, :], ACT.Sigmoid,
                                         bias=col("ga_b", n)).then_inc(ru_s, 1)
                act.wait_ge(ru_s, 4 * (pair + 1))
                act.wait_ge(ru_sp, 1)
                for n in now:
                    nc.scalar.activation(V2["r_a"][:, n % 4, :], V2["r_r"][:, n % 4, :], ACT.Exp,
                                         scale=sp[:, 4, n:n + 1]).then_inc(ru_a, 1)
                act.wait_ge(ru_a, 4 * pair + 2)
                for n in now:
                    nc.scalar.activation(V2["r_r"][:, n % 4, :], V2["r_r"][:, n % 4, :], ACT.Tanh,
                                         scale=sp[:, 5, n:n + 1]).then_inc(ru_a, 1)
            if pair:
                for n in range(2 * pair - 2, 2 * pair):
                    act.wait_ge(ru_o, n + 1)
                    nc.scalar.activation(B["b_hi"][:, n, :], V2["r_o"][:, n % 2, :], ACT.Copy).then_inc(ru_hi, 1)
            if pair < RB // 2:
                for n in now:
                    act.wait_ge(ru_m, n + 1)
                    nc.scalar.activation(V2["r_r"][:, n % 4, :], V2["r_r"][:, n % 4, :], ACT.Sqrt).then_inc(ru_q, 1)

    def lru_dve(dve):
        run = serial(dve, dve_seq)
        vec, sp = nc.vector, V2["r_sp"]

        def softplus():
            dve.wait_ge(ru_e, 4)
            run(vec.tensor_scalar(sp[:, 2, :], sp[:, 0, :], 2.0, None, ALU.add))
            run(vec.reciprocal(sp[:, 2, :], sp[:, 2, :]))
            run(vec.tensor_tensor(sp[:, 0, :], sp[:, 0, :], sp[:, 2, :], ALU.mult))
            run(vec.tensor_tensor(sp[:, 2, :], sp[:, 0, :], sp[:, 0, :], ALU.mult))
            run(vec.tensor_scalar(sp[:, 3, :], sp[:, 2, :], 1.0 / 17, 1.0 / 15, ALU.mult, ALU.add))
            for k in (13, 11, 9, 7, 5, 3, 1):
                run(vec.tensor_tensor(sp[:, 3, :], sp[:, 3, :], sp[:, 2, :], ALU.mult))
                run(vec.tensor_scalar(sp[:, 3, :], sp[:, 3, :], 1.0 / k, None, ALU.add))
            run(vec.tensor_tensor(sp[:, 3, :], sp[:, 3, :], sp[:, 0, :], ALU.mult))
            run(vec.scalar_tensor_tensor(out=sp[:, 3, :], in0=sp[:, 3, :], scalar=2.0, in1=sp[:, 1, :], op0=ALU.mult, op1=ALU.add))
            run(vec.tensor_scalar(sp[:, 5, :], sp[:, 3, :], LRU_C, None, ALU.mult))
            vec.tensor_scalar(sp[:, 4, :], sp[:, 3, :], -LRU_C, None, ALU.mult).then_inc(ru_sp, 1)

        for n in range(2):
            vec.memset(V2["r_x"][:, n, :CW - 1], 0.0).then_inc(ru_e, 1)
        vec.tensor_scalar(sp[:, 1, :], cols[:, COL["lam"]:COL["lam"] + RB], -1.0, 0.0, ALU.mult, ALU.max).then_inc(ru_e, 1)
        for pair in range(RB // 2 + 1):
            for n in range(2 * pair, min(2 * pair + 2, RB)):
                s = n % 2
                dve.wait_ge(ru_in[s], 32 * (n // 2 + 1))
                if n >= 4:
                    dve.wait_ge(ru_g, n - 3)
                    dve.wait_ge(ru_o, n - 3)
                x, y = V2["r_x"][:, s, :], V2["r_y"][:, n % 4, :]
                tap = lambda i: col("conv_w", i * RB + n)
                run(vec.tensor_scalar(y, x[:, 0:L], tap(0), col("conv_b", n), ALU.mult, ALU.add))
                for i in range(1, CW):
                    ins = vec.scalar_tensor_tensor(out=y, in0=x[:, i:i + L], scalar=tap(i), in1=y, op0=ALU.mult, op1=ALU.add)
                    run(ins) if i < CW - 1 else ins.then_inc(ru_y, 1)
                dve.wait_ge(ru_y, n + 1)
            if pair == 0:
                softplus()
                continue
            last = range(2 * pair - 2, 2 * pair)
            at = lambda name, n: V2[name][:, n % 4, :]
            dve.wait_ge(ru_a, 4 * pair)
            for n in last:
                run(vec.tensor_tensor(V2["r_m"][:, n % 2, :], at("r_a", n), at("r_a", n), ALU.mult))
                vec.scalar_tensor_tensor(out=at("r_r", n), in0=V2["r_m"][:, n % 2, :], scalar=1.0, in1=at("r_r", n), op0=ALU.add,
                                         op1=ALU.mult).then_inc(ru_m, 1)
            for n in last:
                run(vec.tensor_tensor(at("r_i", n), at("r_i", n), at("r_y", n), ALU.mult))
            for n in last:
                dve.wait_ge(ru_q, n + 1)
                run(vec.tensor_tensor(at("r_i", n), at("r_i", n), at("r_r", n), ALU.mult))
                if n:
                    dve.wait_ge(ru_o, n)
                run(vec.tensor_tensor_scan(V2["r_h"][:, :], at("r_a", n), at("r_i", n), 0.0, ALU.mult, ALU.add))
                if n >= 2:
                    dve.wait_ge(ru_lo, n - 1)
                vec.tensor_tensor(V2["r_o"][:, n % 2, :], V2["r_h"][:, :], at("r_gate", n), ALU.mult).then_inc(ru_o, 1)
            for n in last:
                dve.wait_ge(ru_o, n + 1)
                dve.wait_ge(ru_hi, n + 1)
                vec.tensor_tensor(B["b_lo"][:, n, :], V2["r_o"][:, n % 2, :], B["b_hi"][:, n, :].bitcast(F32),
                                  ALU.subtract).then_inc(ru_lo, 1)

    V3 = overlay(0, [
        ("w_p", [4, 2 * P], F32), ("w_pt", [2, 2 * P], F32), ("w_o", [2, L], F32), ("w_q", [2, 2, L], F32),
        ("w_gate", [2, L], F32), ("w_k", [WKV, L], F32), ("w_v", [NTOK, WKV * WD], F32), ("w_small", [16], F32)])

    def swa_pre_pool(pool):
        pool.dma_start(V3["w_k"][:WD, :, :], zt[ZT["wkv"]:ZT["wkv"] + WKV * WD, :].rearrange("(n d) t -> d n t", d=WD)).then_inc(shared_in, 16)
        pool.dma_start(V3["w_v"][:, :, :], zn[:, ZN["wv"]:ZN["wv"] + WKV * WD].rearrange("(b p) c -> p b c", p=P)).then_inc(shared_in, 16)

    def swa_loads(t):
        s = t % 2
        return ([(V3["w_q"][:WD, s, :, :], zt[ZT["wq"] + t * P:ZT["wq"] + (t + 1) * P, :].rearrange("(h d) t -> d h t", d=WD))], [])

    def swa_kv(t, h):
        return (2 * t + h) // (WH // WKV)

    SWA = Attention(
        buf=dict(p=V3["w_p"], pt=V3["w_pt"], o=V3["w_o"], small=V3["w_small"]), tiles=WH // 2, heads=2, comps=1, dv=WD,
        scale=WD ** -0.5, key_tiles=lambda qb: (max(qb - 1, 0), min(qb, 1) + 1),
        products=lambda t, h, c, qb, first, count: [(V3["w_q"][:WD, t % 2, h, qb * P:(qb + 1) * P],
                                                     V3["w_k"][:WD, swa_kv(t, h), first * P:(first + count) * P])],
        bias=lambda t, qb, count: band[:, (2 - count) * P:], bias_ready=None, pool_work=None,
        value=lambda t, h, b: V3["w_v"][:, b, swa_kv(t, h) * WD:(swa_kv(t, h) + 1) * WD],
        gate=lambda t: V3["w_gate"][:, t % 2, :], kt0=KT // 2, loads=(swa_loads, 16), gate_of=head_rows("wgate"), hi=B["b_hi"], lo=B["b_lo"],
        units0=32, jobs0=32, tiles0=8, in0=256,
        sink=lambda t, h: col("sinks", 2 * t + h), lam=None, gain=None)

    M = overlay(0, [("latent", [10, L], F32), ("l_sq", [2, L], F32), ("l_n", [2, L], F32), ("l_rs", [2, L], F32),
                    ("lq_hi", [6, L], F32R), ("lq_lo", [6, L], F32R)])
    MK = overlay(HALF, [("lk_hi", [4, L], F32R), ("lk_lo", [4, L], F32R)])
    lt_sq, lt_ss, lt_sd, lt_n, lt_hi, lt_lo = (sem(f"latent_{n}") for n in ("squares", "sum", "deviation", "normed", "hi", "lo"))
    LATENTS = [(0, 6, MQR, "q_norm"), (6, 4, MKVR, "kv_norm")]

    def latent_part(part, g):
        return M["lq_" + part][:, g, :] if g < 6 else MK["lk_" + part][:, g - 6, :]

    def latent_pe(pe):
        for j, (first, n, _, _) in enumerate(LATENTS):
            for g in range(first, first + n):
                pe.wait_ge(lt_sq, g + 1)
                nc.tensor.matmul(pm[j][:, :], ones[:, :], M["l_sq"][:, g % 2, :], start=(g == first),
                                 stop=(g == first + n - 1)).then_inc(lt_ss, 1)

    def latent_act(act):
        for j, (first, n, width, _) in enumerate(LATENTS):
            for g in range(first, first + n):
                if g >= 2:
                    act.wait_ge(lt_ss, g - 1)
                nc.scalar.activation(M["l_sq"][:, g % 2, :], M["latent"][:, g, :], ACT.Square).then_inc(lt_sq, 1)
            act.wait_ge(lt_ss, first + n)
            nc.scalar.activation(M["l_rs"][:, j, :], pm[j][:, :], ACT.Sqrt, scale=1.0 / width,
                                 bias=eps[:, 0:1]).then_inc(lt_sd, 1)
        for g in range(10):
            act.wait_ge(lt_n, g + 1)
            nc.scalar.activation(latent_part("hi", g), M["l_n"][:, g % 2, :], ACT.Copy).then_inc(lt_hi, 1)

    def latent_dve(dve):
        run = serial(dve, dve_seq)
        for j, (first, n, _, gain) in enumerate(LATENTS):
            dve.wait_ge(lt_sd, j + 1)
            run(nc.vector.reciprocal(M["l_rs"][:, j, :], M["l_rs"][:, j, :]))
            for g in range(first, first + n):
                if g >= 2:
                    dve.wait_ge(lt_lo, g - 1)
                nc.vector.scalar_tensor_tensor(out=M["l_n"][:, g % 2, :], in0=M["latent"][:, g, :],
                                               scalar=col(gain, g - first), in1=M["l_rs"][:, j, :], op0=ALU.mult,
                                               op1=ALU.mult).then_inc(lt_n, 1)
                dve.wait_ge(lt_hi, g + 1)
                nc.vector.tensor_tensor(latent_part("lo", g), M["l_n"][:, g % 2, :], latent_part("hi", g).bitcast(F32),
                                        ALU.subtract).then_inc(lt_lo, 1)

    V4 = overlay(0, [
        ("m_p", [4, L], F32), ("m_pt", [2, L], F32), ("m_o", [2, L], F32), ("m_q", [2, L], F32), ("m_k", [2, L], F32),
        ("m_v", [2, NTOK, P], F32), ("m_gate", [2, L], F32), ("m_sq", [L], F32), ("m_small", [16], F32),
        ("m_qr", [4, L], F32), ("m_qs", [4, L], F32), ("m_kr", [L], F32), ("m_ks", [L], F32), ("m_cs", [2, L], F32),
        ("m_lam", [4, DQK], F32), ("m_l", [8], F32)])
    rope_done, lam_sums, lam_exp = sem("rope_done"), sem("lambda_sums"), sem("lambda_exp")

    def rope_loads(act):
        qr = zt[ZT["qr"]:ZT["qr"] + MH * MROPE, :].rearrange("(j r) t -> r j t", r=P)
        kr = zt[ZT["kr"]:ZT["kr"] + MROPE, :]
        H2 = MROPE // 2
        act.dma_start(V4["m_cs"][:, :, :], inp["rope"].rearrange("p (a t) -> p a t", a=2)).then_inc(consts_in, 16)
        act.dma_start(V4["m_qr"][:, :, :], qr).then_inc(consts_in, 16)
        for h in range(2):
            act.dma_start(V4["m_kr"][h * MROPE:(h + 1) * MROPE, :], kr).then_inc(consts_in, 16)
            for half in range(2):
                to, of = h * MROPE + half * H2, h * MROPE + (1 - half) * H2
                act.dma_start(V4["m_qs"][to:to + H2, :, :], qr[of:of + H2]).then_inc(consts_in, 16)
                act.dma_start(V4["m_ks"][to:to + H2, :], kr[(1 - half) * H2:(2 - half) * H2, :]).then_inc(consts_in, 16)
        for n, name in enumerate(("l1_lambda_q1_2", "l1_lambda_k1_2", "l1_lambda_q2_2", "l1_lambda_k2_2")):
            act.dma_start(V4["m_lam"][:, n, :], inp[name].rearrange("(a d) -> a d", a=1).broadcast_to([P, DQK])).then_inc(consts_in, 16)

    def rope_dve(dve):
        run = serial(dve, dve_seq)
        vec = nc.vector
        dve.wait_ge(consts_in, 16 * (NCONST + 16))
        cos, sin = V4["m_cs"][:, 0:1, :], V4["m_cs"][:, 1:2, :]
        lam, l = V4["m_lam"], V4["m_l"]
        for n in range(2):
            run(vec.tensor_tensor_reduce(out=lam[:, 2 * n, :], in0=lam[:, 2 * n, :], in1=lam[:, 2 * n + 1, :], scale=1.0,
                                         scalar=0.0, op0=ALU.mult, op1=ALU.add, accum_out=l[:, n:n + 1]))
        vec.tensor_scalar(l[:, 4:5], col("subln"), 1.0 - LAMBDA_INIT, None, ALU.mult).then_inc(lam_sums, 1)
        for x, y, n in ((V4["m_qr"][:, :, :], V4["m_qs"][:, :, :], 4), (V4["m_kr"][:, :], V4["m_ks"][:, :], 0)):
            c, s = (cos.broadcast_to([P, n, L]), sin.broadcast_to([P, n, L])) if n else (cos[:, 0, :], sin[:, 0, :])
            run(vec.tensor_tensor(x, x, c, ALU.mult))
            run(vec.tensor_tensor(y, y, s, ALU.mult))
            run(vec.tensor_tensor(x, x, y, ALU.add))
        dve.wait_ge(lam_exp, 1)
        run(vec.tensor_tensor(l[:, 5:6], l[:, 3:4], l[:, 2:3], ALU.subtract))
        vec.tensor_scalar(l[:, 6:7], l[:, 5:6], -LAMBDA_INIT, None, ALU.add).then_inc(rope_done, 1)
        dve.wait_ge(rope_done, 1)

    def rope_act(act):
        act.wait_ge(lam_sums, 1)
        nc.scalar.activation(V4["m_l"][:, 2:4], V4["m_l"][:, 0:2], ACT.Exp).then_inc(lam_exp, 1)

    def mla_loads(t):
        s = t % 2
        rows = lambda name: zt[ZT[name] + t * P:ZT[name] + (t + 1) * P, :]
        return ([(V4["m_q"][:, s, :], rows("qn")), (V4["m_k"][:, s, :], rows("kn"))],
                [(V4["m_v"][:, s, :, :], zn[:, ZN["mv"] + t * P:ZN["mv"] + (t + 1) * P].rearrange("(b p) c -> p b c", p=P))])

    def diff_loads(t):
        s = t % 2
        rows = lambda name: zt[ZT[name] + t * P:ZT[name] + (t + 1) * P, :]
        return ([(V4["m_q"][:, s, :], rows("dq")), (V4["m_k"][:, s, :], rows("dk"))],
                [(V4["m_v"][:, s, :, :], zn[:, ZN["dv"] + t * P:ZN["dv"] + (t + 1) * P].rearrange("(b p) c -> p b c", p=P))])

    def half(t):
        return slice(64 * (t % 2), 64 * (t % 2) + 64)

    buf4 = dict(p=V4["m_p"], pt=V4["m_pt"], o=V4["m_o"], small=V4["m_small"], sq=V4["m_sq"])
    causal_bias = lambda t, qb, count: wide[:, (NTOK - count) * P:]
    MLA = Attention(
        buf=buf4, tiles=MH, heads=1, comps=1, dv=P, scale=(MNOPE + MROPE) ** -0.5, key_tiles=lambda qb: (0, qb + 1),
        products=lambda t, h, c, qb, first, count: [
            (V4["m_q"][:, t % 2, qb * P:(qb + 1) * P], V4["m_k"][:, t % 2, :count * P]),
            (V4["m_qr"][half(t), t // 2, qb * P:(qb + 1) * P], V4["m_kr"][half(t), :count * P])],
        bias=causal_bias, bias_ready=None, pool_work=None, value=lambda t, h, b: V4["m_v"][:, t % 2, b, :],
        gate=lambda t: V4["m_gate"][:, t % 2, :], kt0=0, loads=(mla_loads, 48), gate_of=head_rows("mgate"), hi=B["b_hi"], lo=B["b_lo"],
        units0=96, jobs0=96, tiles0=16, in0=320, sink=None, lam=None, gain=None)
    DIFF = Attention(
        buf=buf4, tiles=DH, heads=1, comps=2, dv=P, scale=DQK ** -0.5, key_tiles=lambda qb: (0, qb + 1),
        products=lambda t, h, c, qb, first, count: [(V4["m_q"][half(c), t % 2, qb * P:(qb + 1) * P],
                                                     V4["m_k"][half(c), t % 2, :count * P])],
        bias=causal_bias, bias_ready=None, pool_work=None, value=lambda t, h, b: V4["m_v"][:, t % 2, b, :],
        gate=lambda t: V4["m_gate"][:, t % 2, :], kt0=KT // 2, loads=(diff_loads, 48), gate_of=head_rows("dgate"), hi=B["b_hi"], lo=B["b_lo"],
        units0=128, jobs0=128, tiles0=24, in0=512, sink=None, lam=V4["m_l"][:, 6:7], gain=V4["m_l"][:, 4:5])

    s5_ug = sem("s5_u_by_group")
    s5_tmp2, s5_cc, s5_mg_pool = sem("s5_scans"), sem("s5_c_copied"), sem("s5_kernels_spread_by_pool")
    BARRIERS_BEFORE_S5 = 4
    NPAIR = SG // 2
    NG = 2 * SPAIR
    CH = NG * SC
    E9 = ST + 1
    V5 = overlay(HALF, [
        ("s_b", [2, SPAIR, SC], F32), ("s_B", [2, SPAIR, SC], F32), ("s_BP", [2, SPAIR, 2, SC], F32), ("s_cn", [4, P], F32), ("s_c", [2, SPAIR, SC], F32),
        ("s_C", [2, SPAIR, E9, SC], F32), ("s_t", [2, SPAIR, E9, SC], F32), ("s_L", [2, SPAIR, ST, SC], F32),
        ("s_u", [ST, CH], F32)])
    V6 = overlay(0, [
        ("s_pw", [2, E9, NPAIR], F32), ("s_small", [12, NPAIR], F32), ("s_ang", [2, E9, NPAIR], F32), ("s_nat", [3, P], F32),
        ("s_ls", [2], F32), ("s_kv", [SK], F32), ("s_BT", [2, SPAIR, P], F32), ("s_UT", [NG, SK], F32), ("s_K", [SPAIR, P], F32),
        ("s_MG", [NG, P], F32)])
    V7 = overlay(0 + 40 * 1024, [
        ("s_cs", [2, SPAIR, SK], F32), ("s_w", [2, SPAIR, SK], F32), ("s_x", [2, SPAIR, 2, SK], F32), ("s_z", [2, L], F32)])
    V8 = overlay(HALF + 41 * 1024, [("s_y", [ST, SPAIR * SC], F32), ("s_w2", [2, SPAIR, SK], F32), ("s_r", [SPAIR, SK], F32), ("s_ug", [NG, ST * SC], F32)])
    s5_nat, s5_ex, s5_tp, s5_th, s5_sc = (sem(f"s5_{n}") for n in (
        "parameters_in", "step_spread", "parameters_turned", "angles", "sines"))
    (s5_in, s5_ct, s5_ut, s5_bt, s5_kk, s5_v, s5_y, s5_yt, s5_bl, s5_c, s5_k, s5_xp, s5_ute, s5_bte, s5_ke, s5_ye, s5_ang,
     s5_cs, s5_mg, s5_ze, s5_zs) = (sem(f"s5_{n}") for n in (
        "slice_in", "c_turned", "u_turned", "b_turned", "kernels", "inputs_to_states", "y", "y_turned", "b_powers", "c_powers",
        "kernels_with_d", "states", "u_turned_copied", "b_turned_copied", "kernels_copied", "y_copied", "phase", "phase_sines",
        "kernels_spread", "z", "z_stored"))
    S_LR, S_LI, S_ST, S_TH, S_RR, S_DEN, S_NR, S_CR, S_CI, S_T1, S_T2, S_R8 = range(12)
    TWO_PI = 6.283185307179586
    C1 = 6.28125
    C2 = 0.0019350051879882812
    C3 = TWO_PI - C1 - C2
    MAGIC = 12582912.0
    PI_F = 3.1415925

    def reduce_angle(run, ang, n):
        vec = nc.vector
        run(vec.tensor_scalar(n, ang, 1.0 / TWO_PI, MAGIC, ALU.mult, ALU.add))
        run(vec.tensor_scalar(n, n, -MAGIC, None, ALU.add))
        for c in (C1, C2, C3):
            run(vec.scalar_tensor_tensor(out=ang, in0=n, scalar=-c, in1=ang, op0=ALU.mult, op1=ALU.add))
        run(vec.tensor_scalar(ang, ang, PI_F, -PI_F, ALU.min, ALU.max))

    spare = stage[:2 * SC, :, :].rearrange("p m c -> p (m c)")
    d_diag = spare[:, :NPAIR * SC].rearrange("p (j c) -> p j c", c=SC)
    same_c = spare[:, NPAIR * SC:NPAIR * SC + SC]

    def s5_pre_pool(pool):
        for n, name in enumerate(("s5_lambda_re", "s5_lambda_im")):
            pool.dma_start(V6["s_nat"][:NPAIR, n, :], inp[name][0].rearrange("(j g) p -> j (g p)", g=2)).then_inc(s5_nat, 16)
        pool.dma_start(V6["s_ls"][:NPAIR, :], inp["s5_log_step"][0].rearrange("(j g) -> j g", g=2)).then_inc(s5_nat, 16)
        pool.dma_start(V6["s_kv"][:, :], inp["steps"][:, :]).then_inc(s5_nat, 16)
        for g in range(2):
            d = inp["s5_d"].rearrange("a (j g c) -> a g j c", g=2, c=SC)[:, g]
            pool.dma_start(d_diag[g * SC:(g + 1) * SC], d.broadcast_to([SC, NPAIR, SC])).then_inc(s5_nat, 16)

    def s5_pre_pe(pe):
        pe.wait_ge(s5_ex, 1)
        for n in range(3):
            ins = nc.tensor.transpose(pm[0][:, n * NPAIR:(n + 1) * NPAIR], V6["s_nat"][:NPAIR, n, :], ident[:NPAIR, :NPAIR])
        ins.then_inc(s5_tp, 1)

    def s5_pre_dve(dve):
        run = serial(dve, dve_seq)
        vec = nc.vector
        s = lambda n: V6["s_small"][:, n, :]
        dve.wait_ge(s5_nat, 96)
        vec.tensor_copy(V6["s_nat"][:NPAIR, 2, :].rearrange("j (g p) -> j g p", g=2),
                        V6["s_ls"][:NPAIR, :].unsqueeze(2).broadcast_to([NPAIR, 2, P // 2])).then_inc(s5_ex, 1)
        run(vec.tensor_tensor(same_c, ident[:2 * SC, :SC], ident[:2 * SC, SC:2 * SC], ALU.add))
        run(vec.tensor_tensor(d_diag, d_diag, same_c.unsqueeze(1).broadcast_to([2 * SC, NPAIR, SC]), ALU.mult))
        dve.wait_ge(s5_tp, 1)
        run(vec.tensor_copy(V6["s_small"][:, S_LR:S_ST + 1, :], pm[0][:, :3 * NPAIR].rearrange("p (n j) -> p n j", n=3)))
        vec.tensor_scalar(s(S_LR), s(S_LR), -1e-4, None, ALU.min).then_inc(s5_th, 1)
        dve.wait_ge(s5_sc, 1)
        vec.tensor_tensor(s(S_RR), s(S_LR), s(S_ST), ALU.mult).then_inc(s5_th, 1)
        run(vec.tensor_tensor(s(S_TH), s(S_LI), s(S_ST), ALU.mult))
        reduce_angle(run, s(S_TH), s(S_T1))
        for e in range(E9):
            run(vec.tensor_scalar(V6["s_ang"][:, 0, e, :], s(S_TH), float(e), None, ALU.mult))
        scratch = V5["s_t"][:, 0, :, :, :].rearrange("p j e c -> p (j e c)")[:, :E9 * NPAIR].rearrange("p (e j) -> p e j", j=NPAIR)
        reduce_angle(run, V6["s_ang"][:, 0, :, :], scratch)
        run(vec.tensor_copy(s(S_TH), V6["s_ang"][:, 0, ST, :]))
        vec.tensor_tensor(s(S_DEN), s(S_LR), s(S_LR), ALU.mult).then_inc(s5_th, 1)
        run(vec.memset(V6["s_MG"][:, :, :], 0.0))
        run(vec.memset(V7["s_x"][:, :, :, :, :], 0.0))
        run(vec.memset(V5["s_BP"][:, :, :, :, :], 0.0))
        run(vec.memset(V8["s_r"][:, :, 0:1], 0.0))
        dve.wait_ge(s5_sc, 2)
        for c in range(2):
            run(vec.tensor_tensor(V6["s_pw"][:, c, :, :], V6["s_pw"][:, c, :, :], V6["s_ang"][:, 1, :, :], ALU.mult))
        run(vec.tensor_copy(s(S_R8), V6["s_ang"][:, 1, ST, :]))
        for i in range(ST):
            run(vec.tensor_copy(V6["s_ang"][:, :, i, :], V6["s_pw"][:, :, ST - 1 - i, :]))
        run(vec.tensor_tensor(s(S_T1), s(S_LI), s(S_LI), ALU.mult))
        run(vec.tensor_tensor(s(S_DEN), s(S_DEN), s(S_T1), ALU.add))
        run(vec.reciprocal(s(S_DEN), s(S_DEN)))
        run(vec.tensor_scalar(s(S_NR), V6["s_pw"][:, 0, 1, :], -1.0, None, ALU.add))
        ni = V6["s_pw"][:, 1, 1, :]
        for out_, a, b, op in ((S_CR, (S_NR, S_LR), (None, S_LI), ALU.add), (S_CI, (None, S_LR), (S_NR, S_LI), ALU.subtract)):
            run(vec.tensor_tensor(s(S_T1), s(a[0]) if a[0] is not None else ni, s(a[1]), ALU.mult))
            run(vec.tensor_tensor(s(S_T2), s(b[0]) if b[0] is not None else ni, s(b[1]), ALU.mult))
            run(vec.tensor_tensor(s(S_T1), s(S_T1), s(S_T2), op))
            run(vec.tensor_tensor(s(out_), s(S_T1), s(S_DEN), ALU.mult))

    def s5_pre_act(act):
        run = serial(act, act_seq)
        s = lambda n: V6["s_small"][:, n, :]
        act.wait_ge(s5_th, 1)
        nc.scalar.activation(s(S_ST), s(S_ST), ACT.Exp).then_inc(s5_sc, 1)
        act.wait_ge(s5_th, 2)
        for e in range(E9):
            run(nc.scalar.activation(V6["s_ang"][:, 1, e, :], s(S_RR), ACT.Exp, scale=float(e)))
        act.wait_ge(s5_th, 3)
        run(nc.scalar.activation(V6["s_pw"][:, 1, :, :], V6["s_ang"][:, 0, :, :], ACT.Sin))
        run(nc.scalar.activation(V6["s_ang"][:, 0, :, :], V6["s_ang"][:, 0, :, :], ACT.Abs))
        nc.scalar.activation(V6["s_pw"][:, 0, :, :], V6["s_ang"][:, 0, :, :], ACT.Sin, scale=-1.0,
                             bias=halfpi[:, 0:1]).then_inc(s5_sc, 1)

    BY_SP = 10

    def kernels_spread(eng, slices):
        eng.wait_ge(s5_mg, 16 * BY_SP * slices)
        eng.wait_ge(s5_mg_pool, 16 * (2 * ST - BY_SP) * slices)

    def spread(eng, blocks, done):
        by_g = V6["s_MG"][:, :, :].rearrange("p (j g) x -> p g j x", g=2)
        for b in blocks:
            i, g = b // 2, b % 2
            eng.dma_start(by_g[i * SC:(i + 1) * SC, g, :, i * SC:], V6["s_K"][g * SC:(g + 1) * SC, :, :P - i * SC]).then_inc(done, 16)

    def s5_sp(sp):
        sp.wait_ge(bar, 4 * BARRIERS_BEFORE_S5)
        for sl in range(SSL + 1):
            if sl < SSL:
                g0 = sl * NG
                if sl:
                    sp.wait_ge(s5_ug, sl)
                    sp.wait_ge(s5_bl, sl)
                    sp.wait_ge(s5_ct, sl)
                for n, name in enumerate(("s5_b_re", "s5_b_im")):
                    src = inp[name][0, g0:g0 + NG].rearrange("(j g) p c -> g p j c", g=2)
                    for g in range(2):
                        sp.dma_start(V5["s_b"][g * SP_:(g + 1) * SP_, n, :, :], src[g]).then_inc(s5_in, 16)
                sp.dma_start(V5["s_u"][:SK, :, :], zn[:, ZN["u"] + sl * CH:ZN["u"] + (sl + 1) * CH].rearrange(
                    "(k t) c -> k t c", t=ST)).then_inc(s5_in, 16)
                for n, name in enumerate(("s5_c_re", "s5_c_im")):
                    for r in range(2):
                        src = inp[name][0, g0 + 8 * r:g0 + 8 * r + 8].rearrange("g c p -> (g c) p")
                        for twice in range(2):
                            sp.dma_start(V5["s_cn"][:, 2 * n + r, twice * SP_:(twice + 1) * SP_], src).then_inc(s5_in, 16)
            if sl:
                sp.wait_ge(s5_k, sl)
                if sl > 1:
                    sp.wait_ge(s5_y, sl - 1)
                spread(sp, range(BY_SP), s5_mg)
        sp.wait_ge(s5_mg, 16 * BY_SP * SSL)

    def s5_pool(pool):
        def store_z(sl):
            pool.wait_ge(s5_ze, 2 * sl + 2)
            rows_of = zt[ZT["z"] + sl * CH:ZT["z"] + (sl + 1) * CH, :].rearrange("(j g c) t -> g j c t", g=2, c=SC)
            for g in range(2):
                pool.dma_start(rows_of[g], V7["s_z"][:, g, :]).then_inc(s5_zs, 16)

        for sl in range(SSL):
            pool.wait_ge(s5_ke, sl + 1)
            nc.gpsimd.tensor_tensor(V6["s_K"][:2 * SC, :, :SC], V6["s_K"][:2 * SC, :, :SC],
                                    d_diag[:, sl * SPAIR:(sl + 1) * SPAIR, :], ALU.add).then_inc(s5_k, 1)
            if sl:
                pool.wait_ge(s5_y, sl)
            pool.wait_ge(s5_k, sl + 1)
            spread(pool, range(BY_SP, 2 * ST), s5_mg_pool)
            if sl:
                store_z(sl - 1)
        store_z(SSL - 1)
        pool.wait_ge(s5_zs, 16 * 2 * SSL)
        pool.wait_ge(s5_mg_pool, 16 * (2 * ST - BY_SP) * SSL)

    LOADS = 13


    def s5_pe(pe):
        def turn_c(sl):
            pe.wait_ge(s5_in, 16 * LOADS * (sl + 1))
            if sl > 1:
                pe.wait_ge(s5_ze, 2 * (sl - 1))
            for n in range(2):
                for r in range(2):
                    ins = nc.tensor.transpose(pg[2][:, (2 * n + r) * P:(2 * n + r + 1) * P], V5["s_cn"][:, 2 * n + r, :], ident[:, :])
            ins.then_inc(s5_ct, 1)

        def turn_u(sl):
            pe.wait_ge(s5_ug, sl + 1)
            if sl:
                pe.wait_ge(s5_xp, sl)
            for g in range(NG):
                ins = nc.tensor.transpose(pg[g // 8][:, g % 8 * SK:(g % 8 + 1) * SK], V8["s_ug"][:SK, g, :],
                                          ident[:SK, :SK])
            ins.then_inc(s5_ut, 1)

        def turn_y(sl):
            pe.wait_ge(s5_ye, sl + 1)
            for i in range(ST):
                ins = nc.tensor.transpose(pg[2 + i // 4][:, i % 4 * P:(i % 4 + 1) * P], V8["s_y"][:, i, :], ident[:, :])
                if i % 4 == 3:
                    ins.then_inc(s5_yt, 1)

        turn_c(0)
        pe.wait_ge(s5_th, 1)
        for sl in range(SSL):
            pe.wait_ge(s5_bl, sl + 1)
            for n in range(2):
                if n and sl:
                    pe.wait_ge(s5_ye, sl)
                for j in range(SPAIR):
                    ins = nc.tensor.transpose(pm[2 * n + j // 4][:, j % 4 * P:(j % 4 + 1) * P],
                                              V5["s_L"][:, n, j, :, :], ident[:, :])
            ins.then_inc(s5_bt, 1)
            turn_u(sl)
            pe.wait_ge(s5_bte, sl + 1)
            pe.wait_ge(s5_ute, sl + 1)
            for n in range(2):
                for g in range(NG):
                    rows = slice(g % 2 * SP_, (g % 2 + 1) * SP_)
                    ins = nc.tensor.matmul(pg[n][rows, g // 2 * SK:(g // 2 + 1) * SK], V6["s_BT"][:, n, g // 2, rows],
                                           V6["s_UT"][:, g, :], start=True, stop=True)
            ins.then_inc(s5_v, 1)
            pe.wait_ge(s5_c, sl + 1)
            for j in range(SPAIR):
                for n in range(2):
                    ins = nc.tensor.matmul(pm[j // 4][:2 * SC, j % 4 * P:(j % 4 + 1) * P],
                                           V5["s_BP"][:, n, j, :, :].rearrange("p g c -> p (g c)"),
                                           V5["s_C"][:, n, j, :ST, :], start=(n == 0), stop=(n == 1))
            ins.then_inc(s5_kk, 1)
            if sl:
                pe.wait_ge(s5_cc, sl + 1)
                turn_y(sl - 1)
            if sl + 1 < SSL:
                turn_c(sl + 1)
            y_of = lambda j: pm[2 + j // 4][:, j % 4 * P:(j % 4 + 1) * P]
            kernels_spread(pe, sl + 1)
            pe.wait_ge(s5_xp, sl + 1)
            for j in range(SPAIR):
                for n in range(2):
                    nc.tensor.matmul(y_of(j), V7["s_x"][:, n, j, :, :].rearrange("p g k -> p (g k)"),
                                     V5["s_C"][:, n, j, 1:, :], start=(n == 0), stop=False)
                for g in range(2):
                    ins = nc.tensor.matmul(y_of(j)[g * SK:(g + 1) * SK, :], V6["s_UT"][:, 2 * j + g, :], V6["s_MG"][:, 2 * j + g, :],
                                           start=False, stop=True)
            ins.then_inc(s5_y, 1)
        turn_y(SSL - 1)

    def s5_act(act):
        run = serial(act, act_seq)

        def u_by_group(sl):
            act.wait_ge(s5_in, 16 * LOADS * (sl + 1))
            if sl:
                act.wait_ge(s5_ut, sl)
            nc.scalar.activation(V8["s_ug"][:SK, :, :].rearrange("k g (t c) -> k g t c", c=SC),
                                 V5["s_u"][:SK, :, :].rearrange("k t (g c) -> k g t c", c=SC), ACT.Copy).then_inc(s5_ug, 1)

        def gelu(sl):
            if sl:
                act.wait_ge(s5_zs, 32 * sl)
            for h in range(2):
                act.wait_ge(s5_yt, 2 * sl + h + 1)
                nc.scalar.activation(V7["s_z"][:, :, :].rearrange("p g (k t) -> p t g k", t=ST)[:, 4 * h:4 * h + 4],
                                     pg[2 + h][:, :].rearrange("p (t g k) -> p t g k", t=4, g=2),
                                     ACT.Gelu_apprx_tanh).then_inc(s5_ze, 1)

        u_by_group(0)
        for sl in range(SSL):
            act.wait_ge(s5_bt, sl + 1)
            for n in range(4):
                ins = nc.scalar.activation(V6["s_BT"][:, n // 2, n % 2 * 4:n % 2 * 4 + 4, :], pm[n][:, :], ACT.Copy)
                run(ins)
            for g in range(2):
                rows = slice(g * SP_, (g + 1) * SP_)
                ins = nc.scalar.activation(V5["s_BP"][rows, :, :, g, :], V5["s_B"][rows, :, :, :], ACT.Copy)
                run(ins) if g == 0 else ins.then_inc(s5_bte, 1)
            act.wait_ge(s5_ut, sl + 1)
            for h in range(2):
                ins = nc.scalar.activation(V6["s_UT"][:, 8 * h:8 * h + 8, :], pg[h][:, :], ACT.Copy)
                run(ins) if h == 0 else ins.then_inc(s5_ute, 1)
            act.wait_ge(s5_ang, sl + 1)
            run(nc.scalar.activation(V7["s_cs"][:, 1, :, :], V8["s_w2"][:, 0, :, :], ACT.Sin))
            run(nc.scalar.activation(V8["s_w2"][:, 0, :, :], V8["s_w2"][:, 0, :, :], ACT.Abs))
            nc.scalar.activation(V7["s_cs"][:, 0, :, :], V8["s_w2"][:, 0, :, :], ACT.Sin, scale=-1.0,
                                 bias=halfpi[:, 0:1]).then_inc(s5_cs, 1)
            act.wait_ge(s5_kk, sl + 1)
            if sl:
                kernels_spread(act, sl)
            for h in range(2):
                ins = nc.scalar.activation(V6["s_K"][:2 * SC, 4 * h:4 * h + 4, :], pm[h][:2 * SC, :], ACT.Copy)
                run(ins) if h == 0 else ins.then_inc(s5_ke, 1)
            if sl:
                gelu(sl - 1)
            if sl + 1 < SSL:
                u_by_group(sl + 1)
            act.wait_ge(s5_y, sl + 1)
            if sl:
                act.wait_ge(s5_yt, 2 * sl)
            for h in range(2):
                ins = nc.scalar.activation(
                    V8["s_y"][:, :, :].rearrange("p t (j c) -> p j t c", c=SC)[:, 4 * h:4 * h + 4],
                    pm[2 + h][:, :].rearrange("p (j t c) -> p j t c", j=4, t=ST), ACT.Copy)
                run(ins) if h == 0 else ins.then_inc(s5_ye, 1)
        gelu(SSL - 1)

    def s5_dve(dve):
        run = serial(dve, dve_seq)
        vec = nc.vector
        tt = vec.tensor_tensor
        for sl in range(SSL):
            js = slice(sl * SPAIR, (sl + 1) * SPAIR)
            over_c = lambda n: V6["s_small"][:, n, js].unsqueeze(2).broadcast_to([P, SPAIR, SC])
            t = V5["s_t"]
            dve.wait_ge(s5_ct, sl + 1)
            for n in range(2):
                for g in range(2):
                    rows = slice(g * SP_, (g + 1) * SP_)
                    ins = vec.tensor_copy(V5["s_c"][rows, n, :, :],
                                        pg[2][rows, 2 * n * P:2 * (n + 1) * P].rearrange("p (j g c) -> p j g c", g=2, c=SC)[:, :, g, :])
                    run(ins) if n + g < 2 else ins.then_inc(s5_cc, 1)
            dve.wait_ge(s5_in, 16 * LOADS * (sl + 1))
            if sl:
                dve.wait_ge(s5_kk, sl)
            for n in range(2):
                run(tt(t[:, 0, :, 0, :], V5["s_b"][:, n, :, :], over_c(S_CR), ALU.mult))
                run(tt(t[:, 1, :, 0, :], V5["s_b"][:, 1 - n, :, :], over_c(S_CI), ALU.mult))
                run(tt(V5["s_B"][:, n, :, :], t[:, 0, :, 0, :], t[:, 1, :, 0, :], ALU.subtract if n == 0 else ALU.add))
            power = lambda table, c, n: V6[table][:, c, :n, js].rearrange("p e j -> p j e").unsqueeze(3).broadcast_to([P, SPAIR, n, SC])
            for n in range(2):
                b3 = lambda x: V5["s_B"][:, x, :, :].unsqueeze(2).broadcast_to([P, SPAIR, ST, SC])
                run(tt(t[:, 0, :, :ST, :], b3(n), power("s_ang", 0, ST), ALU.mult))
                run(tt(t[:, 1, :, :ST, :], b3(1 - n), power("s_ang", 1, ST), ALU.mult))
                ins = tt(V5["s_L"][:, n, :, :, :], t[:, 0, :, :ST, :], t[:, 1, :, :ST, :], ALU.subtract if n == 0 else ALU.add)
                run(ins) if n == 0 else ins.then_inc(s5_bl, 1)
            ang, n_ = V8["s_w2"][:, 0, :, :], V8["s_w2"][:, 1, :, :]
            run(tt(ang, V6["s_small"][:, S_TH, js].unsqueeze(2).broadcast_to([P, SPAIR, SK]),
                   V6["s_kv"][:, :].unsqueeze(1).broadcast_to([P, SPAIR, SK]), ALU.mult))
            reduce_angle(run, ang, n_)
            vec.tensor_copy(V8["s_r"][:, :, 1:], V6["s_small"][:, S_R8, js].unsqueeze(2).broadcast_to([P, SPAIR, SK - 1])).then_inc(s5_ang, 1)
            dve.wait_ge(s5_bl, sl + 1)
            dve.wait_ge(s5_cc, sl + 1)
            if sl:
                dve.wait_ge(s5_y, sl)
            for n in range(2):
                c3 = lambda x: V5["s_c"][:, x, :, :].unsqueeze(2).broadcast_to([P, SPAIR, E9, SC])
                run(tt(t[:, 0, :, :, :], c3(n), power("s_pw", 0, E9), ALU.mult))
                run(tt(t[:, 1, :, :, :], c3(1 - n), power("s_pw", 1, E9), ALU.mult))
                if n == 0:
                    run(tt(V5["s_C"][:, 0, :, :, :], t[:, 0, :, :, :], t[:, 1, :, :, :], ALU.subtract))
                else:
                    vec.scalar_tensor_tensor(out=V5["s_C"][:, 1, :, :, :], in0=t[:, 0, :, :, :], scalar=-1.0,
                                             in1=t[:, 1, :, :, :], op0=ALU.mult, op1=ALU.subtract).then_inc(s5_c, 1)
            dve.wait_ge(s5_v, sl + 1)
            dve.wait_ge(s5_cs, sl + 1)
            cs, w, w2, x = V7["s_cs"], V7["s_w"], V8["s_w2"], V7["s_x"]
            v = lambda n: pg[n][:, :].rearrange("p (j k) -> p j k", j=SPAIR)
            for n in range(2):
                run(tt(w[:, n, :, :], v(n), cs[:, 0, :, :], ALU.mult))
                run(tt(w2[:, n, :, :], v(1 - n), cs[:, 1, :, :], ALU.mult))
                run(tt(w[:, n, :, :], w[:, n, :, :], w2[:, n, :, :], ALU.add if n == 0 else ALU.subtract))
            row = lambda x: x.rearrange("p j k -> p (j k)")
            for n in range(2):
                vec.tensor_tensor_scan(row(w2[:, n, :, :]), row(V8["s_r"][:, :, :]), row(w[:, n, :, :]), 0.0, ALU.mult,
                                       ALU.add).then_inc(s5_tmp2, 1)
            dve.wait_ge(s5_tmp2, (sl + 1) * 2)
            m = SK - 1
            for n in range(2):
                run(tt(w[:, 0, :, :m], w2[:, n, :, :m], cs[:, 0, :, :m], ALU.mult))
                run(tt(w[:, 1, :, :m], w2[:, 1 - n, :, :m], cs[:, 1, :, :m], ALU.mult))
                for g in range(2):
                    rows = slice(g * SP_, (g + 1) * SP_)
                    ins = tt(x[rows, n, :, g, 1:], w[rows, 0, :, :m], w[rows, 1, :, :m], ALU.subtract if n == 0 else ALU.add)
                    run(ins) if n + g < 2 else ins.then_inc(s5_xp, 1)
            dve.wait_ge(s5_xp, sl + 1)


    def z_pool(pool):
        for kt in range(KT):
            if kt >= 2:
                pool.wait_ge(h_ready, H0_Z + kt - 1)
            pool.dma_start(G["glu_z"][:, kt % 2, :], zt[ZT["z"] + kt * P:ZT["z"] + (kt + 1) * P, :]).then_inc(glu_in[kt % 2], 16)

    def z_act(act):
        for kt in range(KT):
            act.wait_ge(glu_in[kt % 2], 16 * (kt // 2 + 1))
            nc.scalar.activation(A["a_hi"][:, kt, :], G["glu_z"][:, kt % 2, :], ACT.Copy).then_inc(nh_ready, 1)

    def z_dve(dve):
        for kt in range(KT):
            dve.wait_ge(nh_ready, H0_Z + kt + 1)
            nc.vector.tensor_tensor(A["a_lo"][:, kt, :], G["glu_z"][:, kt % 2, :], A["a_hi"][:, kt, :].bitcast(F32),
                                    ALU.subtract).then_inc(h_ready, 1)

    H0 = {0: 0, 1: 16, "z": 32, 3: 48, 4: 64}
    H0_Z = H0["z"]
    DETAILS = [
        dict(h0=H0[0]), dict(old=xds[0], acc0=16, xin0=0), dict(h0=H0[1]), dict(h0=H0["z"]),
        dict(old=xds[1], acc0=32, xin0=4), dict(h0=H0[3]), dict(old=xds[2], acc0=64, xin0=8), dict(h0=H0[4]),
        dict(), dict(), dict(old=xds[3], acc0=80, xin0=12)]

    def details(n):
        d = dict(h0=None, old=None, acc0=0, xin0=0)
        d.update(DETAILS[n])
        side, regions = PHASES[n]
        d["src"], d["first"] = side, regions[0]
        d["hilo"] = {"A": AB_HI_LO["A"], "B": AB_HI_LO["B"], "LQ": (M["lq_hi"], M["lq_lo"]),
                     "LK": (MK["lk_hi"], MK["lk_lo"])}[side]
        return d

    def products(eng, n, block):
        if n >= len(PHASES):
            return
        d = details(n)
        for r in PHASES[n][1]:
            each_block(eng, r, lambda i: block(eng, r, i, d), unroll=r.evac == "glu" and block is not pe_block)


    block = ctx.enter_context(nc.Block())

    @block.sync
    def _(sp):
        sp.dma_start(ident[:, :], inp["ident"]).then_inc(ident_in, 16)
        sp.wait_ge(made, 5)
        for name, (src, index, n) in VECTORS.items():
            v = inp[src] if index is None else inp[src][index]
            if len(v.shape) == 2:
                v = v.rearrange("a b -> (a b)")
            row, width = COL[name], min(n, P)
            sp.dma_start(rows[row % P:row % P + n // width, row // P, :width],
                         v.rearrange("(k p) -> k p", p=width)).then_inc(consts_in, 16)
        sp.dma_start(cols[:, COL["sinks"]:COL["sinks"] + WH],
                     inp["l0_sinks_2"].rearrange("(a h) -> a h", a=1).broadcast_to([P, WH])).then_inc(consts_in, 16)
        sp.dma_start(wide[:, :], inp["wide"]).then_inc(consts_in, 16)
        sp.dma_start(band[:, :], inp["band"]).then_inc(consts_in, 16)
        for _, regions in PHASES:
            for r in regions:
                sp_loads(sp, r)

    @block.gpsimd
    def _(pool):
        turn_in_pool(pool)
        store_x(pool, XB["xb"], 0)
        products(pool, 0, pool_block)
        pool_end(pool, 0)
        barrier(pool, "pool")
        gla_pool(pool)
        barrier(pool, "pool")
        pool.wait_ge(negc_stored, 16)
        att_pool(pool, FOX)
        barrier(pool, "pool")
        products(pool, 1, pool_block)
        store_x(pool, XB["xb"], 1)
        products(pool, 2, pool_block)
        pool_end(pool, 2)
        barrier(pool, "pool")
        s5_pre_pool(pool)
        s5_pool(pool)
        barrier(pool, "pool")
        z_pool(pool)
        pool.wait_ge(h_ready, H0_Z + KT)
        products(pool, 3, pool_block)
        barrier(pool, "pool")
        products(pool, 4, pool_block)
        pool.wait_ge(xn_ready, 48)
        store_x(pool, XA["xa"], 2)
        products(pool, 5, pool_block)
        pool_end(pool, 5)
        barrier(pool, "pool")
        lru_pool(pool)
        barrier(pool, "pool")
        swa_pre_pool(pool)
        att_pool(pool, SWA)
        barrier(pool, "pool")
        products(pool, 6, pool_block)
        store_x(pool, XA["xa"], 3)
        products(pool, 7, pool_block)
        pool_end(pool, 7)
        barrier(pool, "pool")
        barrier(pool, "pool")
        products(pool, 8, pool_block)
        products(pool, 9, pool_block)
        pool_end(pool, 9)
        barrier(pool, "pool")
        att_pool(pool, MLA)
        att_pool(pool, DIFF)
        barrier(pool, "pool")
        products(pool, 10, pool_block)
        turn_out_pool(pool, XB["xb_tok"])

    @block.tensor
    def _(pe):
        turn_in_pe(pe)
        products(pe, 0, pe_block)
        barrier(pe, "pe")
        gla_pe(pe)
        barrier(pe, "pe")
        att_pe(pe, FOX)
        barrier(pe, "pe")
        products(pe, 1, pe_block)
        rstd_pe(pe, 1)
        products(pe, 2, pe_block)
        barrier(pe, "pe")
        s5_pre_pe(pe)
        s5_pe(pe)
        barrier(pe, "pe")
        products(pe, 3, pe_block)
        barrier(pe, "pe")
        products(pe, 4, pe_block)
        rstd_pe(pe, 2)
        squares_pe(pe, XA["xa_sq"], 48, 3)
        products(pe, 5, pe_block)
        barrier(pe, "pe")
        lru_pe(pe)
        barrier(pe, "pe")
        pe.wait_ge(shared_in, 112)
        att_pe(pe, SWA)
        barrier(pe, "pe")
        products(pe, 6, pe_block)
        rstd_pe(pe, 4)
        products(pe, 7, pe_block)
        barrier(pe, "pe")
        latent_pe(pe)
        barrier(pe, "pe")
        products(pe, 8, pe_block)
        products(pe, 9, pe_block)
        barrier(pe, "pe")
        pe.wait_ge(rope_done, 1)
        att_pe(pe, MLA)
        att_pe(pe, DIFF)
        barrier(pe, "pe")
        products(pe, 10, pe_block)
        rstd_pe(pe, 5)
        turn_out_pe(pe, XA["xa"])

    @block.scalar
    def _(act):
        turn_in_act(act)
        act.wait_ge(consts_in, 16 * NCONST)
        act.wait_ge(cols_ready, 1)
        rstd_act(act, 0)
        split_norm_act(act, XB["xb_n"], A["a_hi"], 0, 0)
        products(act, 0, act_block)
        barrier(act, "act")
        gla_act(act)
        barrier(act, "act")
        att_act(act, FOX)
        barrier(act, "act")
        products(act, 1, act_block)
        rstd_act(act, 1)
        split_norm_act(act, XB["xb_n"], A["a_hi"], 1, 16)
        products(act, 2, act_block)
        barrier(act, "act")
        s5_pre_act(act)
        s5_act(act)
        barrier(act, "act")
        z_act(act)
        products(act, 3, act_block)
        barrier(act, "act")
        products(act, 4, act_block)
        rstd_act(act, 2)
        squares_act(act, XA["xa"], XA["xa_sq"], 48)
        rstd_act(act, 3)
        split_norm_act(act, XA["xa_n"], B["b_hi"], 3, 48)
        products(act, 5, act_block)
        barrier(act, "act")
        lru_act(act)
        barrier(act, "act")
        att_act(act, SWA)
        barrier(act, "act")
        products(act, 6, act_block)
        rstd_act(act, 4)
        split_norm_act(act, XA["xa_n"], B["b_hi"], 4, 64)
        products(act, 7, act_block)
        barrier(act, "act")
        latent_act(act)
        barrier(act, "act")
        products(act, 8, act_block)
        products(act, 9, act_block)
        barrier(act, "act")
        rope_loads(act)
        rope_act(act)
        att_act(act, MLA)
        att_act(act, DIFF)
        barrier(act, "act")
        products(act, 10, act_block)
        rstd_act(act, 5)
        turn_out_act(act, XB["xb_tok"])

    @block.vector
    def _(dve):
        nc.vector.memset(ones[:, :], 1.0).then_inc(made, 1)
        nc.vector.memset(eps[:, :], EPS).then_inc(made, 1)
        nc.vector.memset(onecol[:, :], 1.0).then_inc(made, 1)
        nc.vector.memset(halfpi[:, :], 1.5707963267948966).then_inc(made, 1)
        nc.vector.memset(rows[:, :, :], 0.0).then_inc(made, 1)
        turn_in_dve(dve)
        rstd_dve(dve, 0)
        split_norm_dve(dve, XB["xb"], XB["xb_n"], "ab_norm_g", A["a_hi"], A["a_lo"], 0, 0)
        products(dve, 0, dve_block)
        barrier(dve, "dve")
        gla_dve(dve)
        barrier(dve, "dve")
        att_dve(dve, FOX)
        barrier(dve, "dve")
        products(dve, 1, dve_block)
        rstd_dve(dve, 1)
        split_norm_dve(dve, XB["xb"], XB["xb_n"], "c_norm_g", A["a_hi"], A["a_lo"], 1, 16)
        products(dve, 2, dve_block)
        barrier(dve, "dve")
        s5_pre_dve(dve)
        s5_dve(dve)
        barrier(dve, "dve")
        z_dve(dve)
        products(dve, 3, dve_block)
        barrier(dve, "dve")
        products(dve, 4, dve_block)
        rstd_dve(dve, 2)
        scale_x_dve(dve, XA["xa"], "final_norm_g", 2)
        rstd_dve(dve, 3)
        split_norm_dve(dve, XA["xa"], XA["xa_n"], "norm_a", B["b_hi"], B["b_lo"], 3, 48)
        products(dve, 5, dve_block)
        barrier(dve, "dve")
        lru_dve(dve)
        barrier(dve, "dve")
        att_dve(dve, SWA)
        barrier(dve, "dve")
        products(dve, 6, dve_block)
        rstd_dve(dve, 4)
        split_norm_dve(dve, XA["xa"], XA["xa_n"], "norm_b", B["b_hi"], B["b_lo"], 4, 64)
        products(dve, 7, dve_block)
        barrier(dve, "dve")
        latent_dve(dve)
        barrier(dve, "dve")
        products(dve, 8, dve_block)
        products(dve, 9, dve_block)
        barrier(dve, "dve")
        rope_dve(dve)
        att_dve(dve, MLA)
        att_dve(dve, DIFF)
        barrier(dve, "dve")
        products(dve, 10, dve_block)
        rstd_dve(dve, 5)
        scale_x_dve(dve, XA["xa"], "last_g", 5)

    ctx.close()


INPUTS = [
    "x", "ab_norm_g", "ab_w_in", "gla_alpha_up", "gla_alpha_b", "gla_head_g", "fox_f_b", "ab_w_out", "c_norm_g", "c_w_in",
    "s5_lambda_re", "s5_lambda_im", "s5_log_step", "s5_b_re", "s5_b_im", "s5_c_re", "s5_c_im", "s5_d", "glu_w", "glu_b",
    "c_w_out", "final_norm_g", "norm_gains_2", "final_norm_gain_2", "l0_w_in_2", "l0_conv_w_2", "l0_conv_b_2",
    "l0_gate_x_w_2", "l0_gate_x_b_2", "l0_gate_a_w_2", "l0_gate_a_b_2", "l0_lru_lambda_2", "l0_sinks_2", "l0_w_out_2",
    "l1_w_in_2", "l1_q_norm_2", "l1_w_uq_2", "l1_kv_norm_2", "l1_w_ukv_2", "l1_lambda_q1_2", "l1_lambda_k1_2",
    "l1_lambda_q2_2", "l1_lambda_k2_2", "l1_subln_2", "l1_w_out_2"]


def shape_constants():
    import numpy as np

    q, k = np.arange(P)[:, None], np.arange(P)[None, :]
    causal = np.where(k <= q, 0.0, NEG).astype(np.float32)
    before = np.where(k > q, 0.0, NEG).astype(np.float32)
    wide = np.concatenate([np.zeros((P, L - P), np.float32), causal], 1)
    masks = np.zeros((P, 8, P), np.float32)
    masks[:, 0, :] = q == k
    for level in range(1, 8):
        s = 2 ** (level - 1)
        masks[:, level, :] = (q // (2 * s) == k // (2 * s)) & (q // s % 2 == 0) & (k // s % 2 == 1)
    half = MROPE // 2
    freq = np.float32(10000.0) ** (-np.arange(half, dtype=np.float32) / np.float32(half))
    angle = np.arange(L, dtype=np.float32)[None, :] * freq.astype(np.float32)[:, None]
    cos, sin = np.cos(angle), np.sin(angle)
    rope = np.stack([np.concatenate([cos] * 4), np.concatenate([-sin, sin] * 2)], 1).astype(np.float32)
    steps = np.broadcast_to(np.arange(SK, dtype=np.float32), (P, SK)).copy()
    return {"ident": np.eye(P, dtype=np.float32), "wide": wide, "band": np.concatenate([before, causal], 1),
            "masks": masks.reshape(P, -1), "rope": rope.reshape(P, -1), "steps": steps}


def kernel(**inputs):
    import numpy as np
    import concourse.bacc as bacc
    from concourse.bass_utils import run_bass_kernel_spmd

    nc = bacc.Bacc("TRN2", target_bir_lowering=False, num_devices=1)
    arrays, inp = {}, {}
    given = {name: np.ascontiguousarray(inputs[name]) for name in INPUTS}
    given.update(shape_constants())
    for name, a in given.items():
        arrays["in_" + name] = a
        inp[name] = nc.dram_tensor("in_" + name, a.shape, mybir.dt.from_np(a.dtype), kind="ExternalInput").ap()
    out = nc.dram_tensor("out_x", (1, L, D), F32, kind="ExternalOutput").ap()
    build(nc, inp, out)
    r = run_bass_kernel_spmd(nc, [arrays], core_ids=[0])
    return r.results[0]["out_x"]
```
